# Optimizing a Trainium2 kernel written in Bass

```python
import jax
import jax.numpy as jnp
from jax import lax
import numpy as np

D_MODEL = 1024
BATCH = 1
SEQ = 256
DEPTH = 1

MEM_LEN = 256
HEAD_DIM = 64
NORM_EPS = 1e-5

RWKV_HEADS = 8
RWKV_DIM = RWKV_HEADS * HEAD_DIM
DECAY_LORA = 64
AAA_LORA = 64
GATE_LORA = 128
GN_EPS = HEAD_DIM * 1e-5
RWKV_SPLITS = (RWKV_DIM, RWKV_DIM, RWKV_DIM, DECAY_LORA, AAA_LORA, GATE_LORA)
RWKV_IN = 3 * RWKV_DIM + DECAY_LORA + AAA_LORA + GATE_LORA

DIL_PATTERNS = ((128, 1), (512, 4), (2048, 16))
DIL_HEADS_PER_GROUP = 4
DIL_HEADS = DIL_HEADS_PER_GROUP * 3
DIL_DIM = DIL_HEADS * HEAD_DIM
DIL_OUT_DIM = DIL_HEADS_PER_GROUP * HEAD_DIM
ATTN_BLOCK = 128

MEM_HEADS = 4
MEM_HEAD_DIM = 128
MEM_DIM = MEM_HEADS * MEM_HEAD_DIM

N_BRANCHES = 3
IN_COLS = RWKV_IN + 3 * DIL_DIM + MEM_DIM + N_BRANCHES * D_MODEL

N_EXPERTS = 32
TOP_K = 4
D_FF = D_MODEL
SWIGLU_ALPHA = 1.702
SWIGLU_LIMIT = 7.0
MOE_BLOCK = 128

kernel_name = 'rwkv7_dilated_memory_moe_hybrid'

def rms_norm(x, gain):
    xf = x.astype(jnp.float32)
    y = xf * lax.rsqrt(jnp.mean(xf * xf, axis=-1, keepdims=True) + NORM_EPS)
    return (y * gain.astype(jnp.float32)).astype(x.dtype)

def token_shift(z):
    return jnp.pad(z, ((0, 0), (1, 0), (0, 0)))[:, :-1]

def rwkv7_scan(r, w, k, v, a, b):
    bsz, _, h, n = r.shape

    def step(state, inp):
        r_t, w_t, k_t, v_t, a_t, b_t = inp
        sa = jnp.einsum('bhvk,bhk->bhv', state, a_t)
        state = (state * w_t[:, :, None, :] + sa[..., None] * b_t[:, :, None, :]
                 + v_t[..., None] * k_t[:, :, None, :])
        return state, jnp.einsum('bhvk,bhk->bhv', state, r_t)

    xs = tuple(jnp.swapaxes(t, 0, 1) for t in (r, w, k, v, a, b))
    _, ys = lax.scan(step, jnp.zeros((bsz, h, n, n), jnp.float32), xs)
    return jnp.swapaxes(ys, 0, 1)

def rwkv7_time_mix(zr, w0, w2, a0, a2, g2, k_k, k_a, r_k, ln_w, ln_b):
    bsz, s, _ = zr.shape
    r, k, v, zw, za, zg = jnp.split(zr, list(np.cumsum(RWKV_SPLITS)[:-1]), axis=-1)
    w = -jax.nn.softplus(-(w0 + jnp.tanh(zw) @ w2)) - 0.5
    decay = jnp.exp(-jnp.exp(w.astype(jnp.float32)))
    a = jax.nn.sigmoid(a0 + za @ a2)
    g = jax.nn.sigmoid(zg) @ g2

    def hd(t):
        return t.reshape(bsz, s, RWKV_HEADS, HEAD_DIM).astype(jnp.float32)

    kk = hd(k * k_k)
    kk = kk / jnp.maximum(jnp.sqrt(jnp.sum(kk * kk, axis=-1, keepdims=True)), 1e-12)
    k = k * (1.0 + (a - 1.0) * k_a)
    r_h, k_h, v_h, a_h = hd(r), hd(k), hd(v), hd(a)
    y = rwkv7_scan(r_h, hd(decay), k_h, v_h, -kk, kk * a_h)
    mu = jnp.mean(y, axis=-1, keepdims=True)
    var = jnp.mean(jnp.square(y - mu), axis=-1, keepdims=True)
    yn = ((y - mu) * lax.rsqrt(var + GN_EPS)).reshape(bsz, s, RWKV_DIM)
    yn = yn * ln_w.astype(jnp.float32) + ln_b.astype(jnp.float32)
    bonus = (jnp.sum(r_h * k_h * r_k.astype(jnp.float32), axis=-1, keepdims=True) * v_h).reshape(bsz, s, RWKV_DIM)
    return ((yn + bonus) * g.astype(jnp.float32)).astype(zr.dtype)

def dilated_group_attn(q, k, v, window, dilation):
    bsz, h, s, dh = q.shape
    span = window // dilation
    n = s // dilation
    nb = -(-n // ATTN_BLOCK)
    n_pad = nb * ATTN_BLOCK

    def strided(t, front):
        t = t.reshape(bsz, h, n, dilation, dh).transpose(0, 1, 3, 2, 4)
        return jnp.pad(t, ((0, 0), (0, 0), (0, 0), (front, n_pad - n), (0, 0)))

    qb = strided(q, 0).reshape(bsz, h, dilation, nb, ATTN_BLOCK, dh)

    def key_blocks(t):
        tb = strided(t, ATTN_BLOCK).reshape(bsz, h, dilation, nb + 1, ATTN_BLOCK, dh)
        return jnp.concatenate([tb[:, :, :, :-1], tb[:, :, :, 1:]], axis=4)

    kb = key_blocks(k)
    vb = key_blocks(v)
    sc = jnp.einsum('bhrnqd,bhrnkd->bhrnqk', qb, kb).astype(jnp.float32) * dh ** -0.5
    qi = jnp.arange(ATTN_BLOCK)[:, None]
    ki = jnp.arange(2 * ATTN_BLOCK)[None, :]
    offset = qi + ATTN_BLOCK - ki
    key_idx = jnp.arange(nb)[:, None, None] * ATTN_BLOCK - ATTN_BLOCK + ki
    mask = (offset >= 0) & (offset <= span) & (key_idx >= 0)
    sc = jnp.where(mask, sc, -jnp.inf)
    m = jnp.max(sc, axis=-1, keepdims=True)
    p = jnp.exp(sc - m)
    den = jnp.sum(p, axis=-1, keepdims=True)
    o = jnp.einsum('bhrnqk,bhrnkd->bhrnqd', p, vb.astype(jnp.float32)) / den
    lse = (m + jnp.log(den))[..., 0]
    o = o.reshape(bsz, h, dilation, n_pad, dh)[:, :, :, :n].transpose(0, 1, 3, 2, 4).reshape(bsz, h, s, dh)
    lse = lse.reshape(bsz, h, dilation, n_pad)[..., :n].transpose(0, 1, 3, 2).reshape(bsz, h, s)
    return o, lse

def dilated_attention(q, k, v, q_norm, k_norm):
    bsz, s, _ = q.shape

    def heads(t):
        return t.reshape(bsz, s, DIL_HEADS, HEAD_DIM)

    qh = rms_norm(heads(q), q_norm).transpose(0, 2, 1, 3)
    kh = rms_norm(heads(k), k_norm).transpose(0, 2, 1, 3)
    vh = heads(v).transpose(0, 2, 1, 3)
    outs, lses = [], []
    for gi, (window, dilation) in enumerate(DIL_PATTERNS):
        sl = slice(gi * DIL_HEADS_PER_GROUP, (gi + 1) * DIL_HEADS_PER_GROUP)
        o, l = dilated_group_attn(qh[:, sl], kh[:, sl], vh[:, sl], window, dilation)
        outs.append(o)
        lses.append(l)
    outs = jnp.stack(outs)
    wts = jax.nn.softmax(jnp.stack(lses), axis=0)
    o = jnp.sum(wts[..., None] * outs, axis=0)
    return o.transpose(0, 2, 1, 3).reshape(bsz, s, DIL_OUT_DIM).astype(q.dtype)

def memory_cross_attn(q, mem, ln_mem, w_mem_kv, q_norm, k_norm):
    bsz, s, _ = q.shape
    m_len = mem.shape[1]
    kv = rms_norm(mem, ln_mem) @ w_mem_kv
    k, v = jnp.split(kv, 2, axis=-1)
    qh = rms_norm(q.reshape(bsz, s, MEM_HEADS, MEM_HEAD_DIM), q_norm)
    kh = rms_norm(k.reshape(bsz, m_len, MEM_HEADS, MEM_HEAD_DIM), k_norm)
    vh = v.reshape(bsz, m_len, MEM_HEADS, MEM_HEAD_DIM)
    sc = jnp.einsum('bshd,bmhd->bhsm', qh, kh).astype(jnp.float32) * MEM_HEAD_DIM ** -0.5
    p = jax.nn.softmax(sc, axis=-1)
    o = jnp.einsum('bhsm,bmhd->bshd', p, vh.astype(jnp.float32))
    return o.reshape(bsz, s, MEM_DIM).astype(q.dtype)

def mixer_sublayer(x, mem, ln1, w_in, token_mu, rwkv_w0, rwkv_w2, rwkv_a0, rwkv_a2, rwkv_g2,
                   rwkv_k_k, rwkv_k_a, rwkv_r_k, rwkv_ln_w, rwkv_ln_b, dil_q_norm, dil_k_norm,
                   ln_mem, w_mem_kv, mem_q_norm, mem_k_norm, p_rwkv, p_dil, p_mem, w_out):
    bsz, s, _ = x.shape
    h = rms_norm(x, ln1)
    z = h @ w_in
    cut = [RWKV_IN, RWKV_IN + 3 * DIL_DIM, RWKV_IN + 3 * DIL_DIM + MEM_DIM]
    zr, z_dil, z_memq, z_gate = jnp.split(z, cut, axis=-1)
    zr = zr + (token_shift(zr) - zr) * token_mu
    y_rwkv = rwkv7_time_mix(zr, rwkv_w0, rwkv_w2, rwkv_a0, rwkv_a2, rwkv_g2,
                            rwkv_k_k, rwkv_k_a, rwkv_r_k, rwkv_ln_w, rwkv_ln_b)
    dq, dk, dv = jnp.split(z_dil, 3, axis=-1)
    y_dil = dilated_attention(dq, dk, dv, dil_q_norm, dil_k_norm)
    y_mem = memory_cross_attn(z_memq, mem, ln_mem, w_mem_kv, mem_q_norm, mem_k_norm)
    g = jax.nn.sigmoid(z_gate).reshape(bsz, s, N_BRANCHES, D_MODEL)
    mixed = (g[:, :, 0] * (y_rwkv @ p_rwkv) + g[:, :, 1] * (y_dil @ p_dil)
             + g[:, :, 2] * (y_mem @ p_mem))
    return x + mixed @ w_out

def moe_ffn(h, w_router, b_router, w1, b1, w2, b2):
    bsz, s, d = h.shape
    n_tok = bsz * s
    n_asg = n_tok * TOP_K
    xt = h.reshape(n_tok, d)
    logits = (xt @ w_router).astype(jnp.float32) + b_router.astype(jnp.float32)
    top_vals, top_idx = lax.top_k(logits, TOP_K)
    gates = jax.nn.softmax(top_vals, axis=-1)
    flat_e = top_idx.reshape(-1).astype(jnp.int32)
    flat_w = gates.reshape(-1)
    flat_tok = jnp.arange(n_asg, dtype=jnp.int32) // TOP_K
    order = jnp.argsort(flat_e)
    se, stok, sw = flat_e[order], flat_tok[order], flat_w[order]
    counts = jnp.bincount(flat_e, length=N_EXPERTS).astype(jnp.int32)
    padded = ((counts + MOE_BLOCK - 1) // MOE_BLOCK) * MOE_BLOCK
    pend = jnp.cumsum(padded)
    pstart = pend - padded
    sstart = jnp.cumsum(counts) - counts
    dest = pstart[se] + (jnp.arange(n_asg, dtype=jnp.int32) - sstart[se])
    n_blocks = -(-n_asg // MOE_BLOCK) + N_EXPERTS
    n_slots = n_blocks * MOE_BLOCK
    slot_tok = jnp.zeros((n_slots,), jnp.int32).at[dest].set(stok)
    slot_w = jnp.zeros((n_slots,), jnp.float32).at[dest].set(sw)
    block_start = jnp.arange(n_blocks, dtype=jnp.int32) * MOE_BLOCK
    block_e = jnp.minimum(jnp.searchsorted(pend, block_start, side='right'), N_EXPERTS - 1)
    xs = xt[slot_tok].reshape(n_blocks, MOE_BLOCK, d)

    def expert_block(args):
        xb, e = args
        hb = xb @ w1[e] + b1[e]
        x_glu = jnp.minimum(hb[:, ::2], SWIGLU_LIMIT)
        x_lin = jnp.clip(hb[:, 1::2], -SWIGLU_LIMIT, SWIGLU_LIMIT)
        act = x_glu * jax.nn.sigmoid(SWIGLU_ALPHA * x_glu) * (x_lin + 1.0)
        return act @ w2[e] + b2[e]

    ys = lax.map(expert_block, (xs, block_e)).reshape(n_slots, d)
    out = jnp.zeros((n_tok, d), jnp.float32).at[slot_tok].add(ys.astype(jnp.float32) * slot_w[:, None])
    return out.reshape(bsz, s, d).astype(h.dtype)

def setup_inputs(seed: int = 0) -> dict:
    key = jax.random.key(seed)
    ks = iter(jax.random.split(key, 40))
    f32 = jnp.float32
    L = (DEPTH,)

    def nrm(shape, scale):
        return jax.random.normal(next(ks), shape, f32) * scale

    def unif(shape, lo, hi):
        return jax.random.uniform(next(ks), shape, f32, lo, hi)

    return {
        'x': nrm((BATCH, SEQ, D_MODEL), 1.0),
        'mem': nrm((BATCH, MEM_LEN, D_MODEL), 1.0),
        'ln1': 1.0 + nrm(L + (D_MODEL,), 0.05),
        'w_in': nrm(L + (D_MODEL, IN_COLS), D_MODEL ** -0.5),
        'token_mu': unif(L + (RWKV_IN,), 0.0, 1.0),
        'rwkv_w0': unif(L + (RWKV_DIM,), -3.0, 1.0),
        'rwkv_w2': nrm(L + (DECAY_LORA, RWKV_DIM), 0.5 * DECAY_LORA ** -0.5),
        'rwkv_a0': nrm(L + (RWKV_DIM,), 0.1),
        'rwkv_a2': nrm(L + (AAA_LORA, RWKV_DIM), 0.5 * AAA_LORA ** -0.5),
        'rwkv_g2': nrm(L + (GATE_LORA, RWKV_DIM), GATE_LORA ** -0.5),
        'rwkv_k_k': 0.85 + nrm(L + (RWKV_DIM,), 0.05),
        'rwkv_k_a': 1.0 + nrm(L + (RWKV_DIM,), 0.05),
        'rwkv_r_k': nrm(L + (RWKV_HEADS, HEAD_DIM), 0.1),
        'rwkv_ln_w': 1.0 + nrm(L + (RWKV_DIM,), 0.05),
        'rwkv_ln_b': nrm(L + (RWKV_DIM,), 0.01),
        'dil_q_norm': 1.0 + nrm(L + (HEAD_DIM,), 0.05),
        'dil_k_norm': 1.0 + nrm(L + (HEAD_DIM,), 0.05),
        'ln_mem': 1.0 + nrm(L + (D_MODEL,), 0.05),
        'w_mem_kv': nrm(L + (D_MODEL, 2 * MEM_DIM), D_MODEL ** -0.5),
        'mem_q_norm': 1.0 + nrm(L + (MEM_HEAD_DIM,), 0.05),
        'mem_k_norm': 1.0 + nrm(L + (MEM_HEAD_DIM,), 0.05),
        'p_rwkv': nrm(L + (RWKV_DIM, D_MODEL), RWKV_DIM ** -0.5),
        'p_dil': nrm(L + (DIL_OUT_DIM, D_MODEL), DIL_OUT_DIM ** -0.5),
        'p_mem': nrm(L + (MEM_DIM, D_MODEL), MEM_DIM ** -0.5),
        'w_out': nrm(L + (D_MODEL, D_MODEL), D_MODEL ** -0.5),
        'ln2': 1.0 + nrm(L + (D_MODEL,), 0.05),
        'w_router': nrm(L + (D_MODEL, N_EXPERTS), D_MODEL ** -0.5),
        'b_router': nrm(L + (N_EXPERTS,), 0.01),
        'w1': nrm(L + (N_EXPERTS, D_MODEL, 2 * D_FF), D_MODEL ** -0.5),
        'b1': nrm(L + (N_EXPERTS, 2 * D_FF), 0.01),
        'w2': nrm(L + (N_EXPERTS, D_FF, D_MODEL), D_FF ** -0.5),
        'b2': nrm(L + (N_EXPERTS, D_MODEL), 0.01),
    }

def reference(x, mem, ln1, w_in, token_mu, rwkv_w0, rwkv_w2, rwkv_a0, rwkv_a2, rwkv_g2,
              rwkv_k_k, rwkv_k_a, rwkv_r_k, rwkv_ln_w, rwkv_ln_b, dil_q_norm, dil_k_norm,
              ln_mem, w_mem_kv, mem_q_norm, mem_k_norm, p_rwkv, p_dil, p_mem, w_out,
              ln2, w_router, b_router, w1, b1, w2, b2):
    for l in range(DEPTH):
        x = mixer_sublayer(x, mem, ln1[l], w_in[l], token_mu[l], rwkv_w0[l], rwkv_w2[l],
                           rwkv_a0[l], rwkv_a2[l], rwkv_g2[l], rwkv_k_k[l], rwkv_k_a[l],
                           rwkv_r_k[l], rwkv_ln_w[l], rwkv_ln_b[l], dil_q_norm[l], dil_k_norm[l],
                           ln_mem[l], w_mem_kv[l], mem_q_norm[l], mem_k_norm[l],
                           p_rwkv[l], p_dil[l], p_mem[l], w_out[l])
        x = x + moe_ffn(rms_norm(x, ln2[l]), w_router[l], b_router[l], w1[l], b1[l], w2[l], b2[l])
    return x


_drawn_inputs = setup_inputs


def setup_inputs(seed=0):
    import zlib

    import numpy as np

    out = dict(_drawn_inputs(seed))
    spreads = {}
    factors = {'rwkv_ln_b': 15.976,
     'ln_mem': 2.67,
     'mem_q_norm': 4.143,
     'mem_k_norm': 2.672,
     'b1': 8.0,
     'b2': 8.0,
     'rwkv_w2': 2.703,
     'rwkv_a0': 3.88,
     'rwkv_k_k': 4.855,
     'rwkv_k_a': 2.706,
     'rwkv_ln_w': 2.941,
     'dil_q_norm': 7.006,
     'dil_k_norm': 5.249,
     'b_router': 2.973}
    for name, (base, spread) in spreads.items():
        noise = np.random.default_rng([zlib.crc32(name.encode()), seed]).standard_normal(out[name].shape)
        drawn = base * np.exp(spread * noise) if base else spread * noise
        out[name] = jnp.asarray(drawn.astype(out[name].dtype))
    for name, factor in factors.items():
        out[name] = (out[name] * factor).astype(out[name].dtype)
    return out
```

```python
from contextlib import ExitStack

import numpy as np

import concourse.bass as bass
from concourse import mybir

F32 = mybir.dt.float32
ALU = mybir.AluOpType
ACT = mybir.ActivationFunctionType
AX = mybir.AxisListType.X

P = 128
D = 1024
SEQ = 256
NT = SEQ // P
KD = D // P
HD = 64
RH = 8
RT4 = RH * HD // P
L = 64
NCH = SEQ // L
LEVELS = 6
DH = 4
DG = 3
DIL = (1, 4, 16)
SPAN = 128
MH = 4
E = 32
TOPK = 4
FF = 1024
CAP = 64
NJ = SEQ // CAP
MAX_OVER = 15
NORM_EPS = 1e-5
GN_EPS = HD * 1e-5
NEG = -1e30
CW = 256
LO = 6
SLOTS = 12
W1C = 2 * FF // CW
W2C = D // CW

ROWS = {}
_at = 0
for _name, _n in (("ln1", 8), ("ln_mem", 8), ("ln2", 8), ("token_mu", 14), ("rwkv_w0", 4), ("rwkv_a0", 4),
                  ("rwkv_k_k", 4), ("rwkv_k_a", 4), ("rwkv_r_k", 4), ("rwkv_ln_w", 4), ("rwkv_ln_b", 4),
                  ("dil_q_norm", 1), ("dil_k_norm", 1), ("mem_q_norm", 1), ("mem_k_norm", 1)):
    ROWS[_name] = (_at, _n)
    _at += _n
NROWS = _at

C_RWKV, C_QK, C_V, C_MQ, C_MK, C_MV, C_GATE = 0, 7, 13, 16, 18, 20, 22
C_PMEM, C_PDIL, C_PRWKV, C_OUT, NMIX = 34, 36, 37, 39, 43
MIX = ((2, 0), (2, 4), (1, 0), (1, 4), (0, 0), (0, 4))
MIX_CHUNKS = ((C_PMEM, 4), (C_PMEM + 1, 4), (C_PDIL, 2), (C_PDIL, 2), (C_PRWKV, 4), (C_PRWKV + 1, 4))
FIRST = (-NMIX) % LO


UNITS = [(kind, h, i) for kind in ("mem", "dil") for h in range(4) for i in range(NT)]


def unit_keys(unit):
    return SEQ if unit[0] == "mem" else DG * P * (unit[2] + 1)


NORM_GROUPS = (("qk", 0, ("dil_q_norm", "dil_q_norm")), ("qk", 4, ("dil_q_norm", "dil_k_norm")),
               ("qk", 8, ("dil_k_norm", "dil_k_norm")), ("mq", 0, ("mem_q_norm", "mem_q_norm")),
               ("mk", 0, ("mem_k_norm", "mem_k_norm")))


class Own:

    def __init__(self, engine, sem, base=0):
        self.engine, self.sem, self.base, self.n = engine, sem, base, 0

    def __call__(self, instruction):
        instruction.then_inc(self.sem, 1)
        self.n += 1

    def wait(self):
        self.engine.wait_ge(self.sem, self.base + self.n)

    def link(self, instruction):
        self(instruction)
        self.wait()


class Layout:
    pass


def build(nc, a, out, part=None):
    g = Layout()
    with ExitStack() as ctx:
        g.sems = {}

        def sem(name):
            if name not in g.sems:
                g.sems[name] = ctx.enter_context(nc.semaphore(name))
            return g.sems[name]

        def psb(name):
            return ctx.enter_context(nc.psum_tensor(name, [P, 8 * 512], F32))

        g.ps = psb("banks")

        def bank(b, n=1):
            return g.ps[:, b * 512:(b + n) * 512]

        g.arena = ctx.enter_context(nc.sbuf_tensor("arena", [P, 52800], F32))
        g.top = [0]

        def place(n, at=None):
            if at is None:
                at = g.top[0]
            g.top[0] = at + n
            assert g.top[0] <= 52800, g.top[0]
            return g.arena[:, at:at + n]

        def cut(ap, **dims):
            names = list(dims)
            return ap.rearrange(f"p ({' '.join(names)} n) -> p {' '.join(names)} n", **dims)

        g.ring_lo = cut(place(LO * 2048), s=LO)
        g.x = cut(place(NT * D), i=NT)
        g.hT = cut(place(KD * SEQ), k=KD)
        g.ident, g.mask_s, g.mask_l, g.mask_i, g.head_ones, g.ones = (place(P) for _ in range(6))
        g.amask = cut(place(3 * SEQ), g=3)
        g.cols = place(NROWS + 8)
        g.eps_norm = g.cols[:, NROWS:NROWS + 1]
        g.eps_gn = g.cols[:, NROWS + 1:NROWS + 2]
        g.stat = place(64)

        def param(name):
            at, n = ROWS[name]
            return g.cols[:, at:at + n]

        region = g.top[0]
        g.Zraw = cut(place(14 * 257), k=14)
        g.qk = cut(place(12 * SEQ), k=12)
        g.vtok = cut(place(NT * 768), i=NT)
        g.mq = cut(place(4 * SEQ), k=4)
        g.mk = cut(place(4 * SEQ), k=4)
        g.mv = cut(place(NT * 512), i=NT)
        g.sc2 = cut(place(2 * 768), u=2)
        g.pt2 = cut(place(2 * 768), u=2)
        end_attention = g.top[0]
        g.top[0] = region
        g.tokm = cut(place(4 * NT * 512), q=4)
        g.tok_a, g.tok_b, g.tok_k, g.tok_v = (cut(g.tokm[:, q], i=NT) for q in range(4))
        g.WT = cut(place(4 * SEQ), k=4)
        g.Zt = cut(place(NT * 512), i=NT)
        g.mrb = cut(place(16 * P), q=16)
        g.Y0 = cut(place(4 * SEQ), k=4)
        g.S_hist = cut(place((NCH + 1) * 256), c=NCH + 1)
        g.qxn4 = place(4 * 256).rearrange("p (u q j n) -> p u q j n", u=2, q=2, j=2)
        g.xx4 = place(4 * P).rearrange("p (u q n) -> p u q n", u=2, q=2)
        g.ak4 = place(4 * P).rearrange("p (u q n) -> p u q n", u=2, q=2)
        g.rk4 = place(4 * P).rearrange("p (u q n) -> p u q n", u=2, q=2)
        g.mv2 = place(4 * HD).rearrange("p (u q n) -> p u q n", u=2, q=2)
        g.U = cut(place(NT * 512), i=NT)
        g.top[0] = max(g.top[0], end_attention)
        g.gates = cut(place(24 * SEQ), k=24)
        g.rT, g.kT, g.aT, g.kkT, g.vT, g.gT, g.dec = (cut(place(4 * SEQ), k=4) for _ in range(7))
        g.lora = cut(place(2 * SEQ), k=2)
        g.tmp = cut(place(4 * SEQ), k=4)
        g.zs = g.Zraw.rearrange("p k n -> p (k n)")
        g.t1, g.t2, g.t3 = (cut(g.zs[:, q * 1024:(q + 1) * 1024], k=4) for q in range(3))
        g.p_last = place(4 * NCH).rearrange("p (k c) -> p k c", k=4)
        g.lw2 = place(512)
        g.lg2 = place(512)
        g.yT = cut(place(10 * SEQ), k=10)
        g.y_rwkv, g.y_dil, g.y_mem = g.yT[:, 0:4], g.yT[:, 4:6], g.yT[:, 6:10]
        gflat = g.gates.rearrange("p k n -> p (k n)")
        g.memx = cut(gflat[:, 0:NT * D], i=NT)
        g.memT = cut(gflat[:, NT * D:2 * NT * D], k=KD)
        g.sq = gflat[:, 4096:5120]
        g.prow = gflat[0:NROWS, 5120:5248]
        mixer_end = g.top[0]

        g.top[0] = region
        g.ring_hi = cut(place((SLOTS - LO) * 2048), s=SLOTS - LO)
        g.xn = cut(place(NT * D), i=NT)
        g.xnT = cut(place(KD * SEQ), k=KD)
        g.b1raw = place(2 * FF)
        g.b2raw = place(D)
        g.wr = place(KD * E)
        g.brow = place(E)
        g.b1T = place(16 * E).rearrange("p (two j e) -> p two j e", j=8, two=2)
        g.logit = cut(place(NT * E), i=NT)
        g.top8 = cut(place(NT * 8), i=NT)
        g.ti8 = place(NT * 8).rearrange("p (i n) -> p i n", i=NT)
        g.tif = cut(place(NT * 8), i=NT)
        g.eio = place(E)
        g.chosen = cut(place(NT * (NJ - 1) * E), i=NT)
        g.gate = cut(place(NT * E), i=NT)
        g.gateT = place(SEQ)
        g.posj = cut(place(NT * NJ * E), i=NT)
        g.oh = place(2 * E)
        g.rsc = place(64)
        g.before = place(P)
        over = place(64)
        g.over_i = place(64).bitcast(mybir.dt.int32)
        g.slot_no = place(CAP)
        g.sel = cut(place(NT * CAP), i=NT)
        g.selg = cut(place(NT * CAP), i=NT)
        g.selT = place(SEQ)
        g.xg = cut(place(KD * CAP), k=KD)
        g.hg, g.hl, g.hs, g.actT = (cut(place(KD * CAP), k=KD) for _ in range(4))
        g.yeT = cut(place(KD * CAP), k=KD)
        g.ye = place(D)
        assert g.top[0] <= 52800
        g.top[0] = max(g.top[0], mixer_end)

        def ring(n):
            return g.ring_lo[:, (FIRST + n) % LO]

        g.arrived = [sem(f"slot{s}_arrived") for s in range(SLOTS)]

        def nth(n):
            return (FIRST + n) // LO + (1 if (FIRST + n) % LO >= FIRST else 0)

        g.lo_loads = [nth(NMIX - LO + s) for s in range(LO)]

        w_in, w_kv = a["w_in"][0], a["w_mem_kv"][0]

        def columns(w, at, n=CW):
            return w[:, at:at + n].rearrange("(k p) n -> p k n", p=P)

        def chunk_source(n):
            if n < C_MK:
                return columns(w_in, n * CW)
            if n < C_GATE:
                return columns(w_kv, (n - C_MK) * CW)
            if n < C_PMEM:
                return columns(w_in, (n - C_GATE) * CW + C_MK * CW)
            if n < C_PDIL:
                return columns(a["p_mem"][0], (n - C_PMEM) * 512, 512)
            if n < C_PRWKV:
                return columns(a["p_dil"][0], 0, 1024)
            if n < C_OUT:
                return columns(a["p_rwkv"][0], (n - C_PRWKV) * 512, 512)
            return columns(a["w_out"][0], (n - C_OUT) * CW)

        g.sem, g.bank, g.cut, g.param, g.ring, g.nth, g.chunk_source = sem, bank, cut, param, ring, nth, chunk_source
        g.part = part
        if part != "moe":
            mixer(nc, a, g)
        if part == "mixer":
            with nc.Block() as block:
                @block.sync
                def _(sp):
                    sp.dma_start(out[0].rearrange("(i p) n -> p i n", p=P), g.x).then_inc(sem("stored"), 16)
                    sp.wait_ge(sem("stored"), 16)
        else:
            moe(nc, a, out, g)


def mixer(nc, a, g):
    sem, bank, cut, param = g.sem, g.bank, g.cut, g.param
    x, hT, ident, cols = g.x, g.hT, g.ident, g.cols

    with nc.Block() as block:
        @block.sync
        def _(sp):
            def wait_used(n):
                if n < C_PMEM:
                    sp.wait_ge(sem("proj_done"), n + 1)
                elif n < C_OUT:
                    last = max(q for q in range(len(MIX)) if MIX_CHUNKS[q][0] == n)
                    sp.wait_ge(sem("mix_done"), last + 1)
                else:
                    sp.wait_ge(sem("out_done"), n - C_OUT + 1)

            sp.dma_start(x, a["x"][0].rearrange("(i p) n -> p i n", p=P)).then_inc(sem("x_in"), 16)
            sp.dma_start(g.memx, a["mem"][0].rearrange("(i p) n -> p i n", p=P)).then_inc(sem("mem_in"), 16)
            for n in range(NMIX):
                if n >= LO:
                    wait_used(n - LO)
                src = g.chunk_source(n)
                dst = cut(g.ring(n), k=src.shape[1])
                sp.dma_start(dst, src).then_inc(g.arrived[(FIRST + n) % LO], 16)
            for s in range(LO):
                wait_used(NMIX - LO + s)
                sp.dma_start(cut(g.ring_lo[:, s], k=KD), a["w1"][0, 0][:, s * CW:(s + 1) * CW]
                             .rearrange("(k p) n -> p k n", p=P)).then_inc(g.arrived[s], 16)

        @block.gpsimd
        def _(pool):
            own = Own(pool, sem("pool_steps"))
            own.link(nc.gpsimd.memset(ident, 0.0))
            nc.gpsimd.affine_select(out=ident, in_=ident, compare_op=ALU.not_equal, fill=1.0, base=0,
                                    pattern=[[-1, P]], channel_multiplier=1).then_inc(sem("ident_set"), 1)
            for name, (at, n) in ROWS.items():
                src = a[name][0]
                if name == "rwkv_r_k":
                    src = src.rearrange("h d -> (h d)")
                if name.startswith("dil"):
                    for half in range(2):
                        pool.dma_start(g.prow[at:at + 1, half * HD:(half + 1) * HD],
                                       src.rearrange("(a n) -> a n", a=1)).then_inc(sem("rows_in"), 16)
                else:
                    pool.dma_start(g.prow[at:at + n, :], src.rearrange("(a n) -> a n", a=n)) \
                        .then_inc(sem("rows_in"), 16)
            pool.dma_start(g.lw2[0:64, :], a["rwkv_w2"][0]).then_inc(sem("lora_in"), 16)
            pool.dma_start(g.lw2[64:128, :], a["rwkv_a2"][0]).then_inc(sem("lora_in"), 16)
            pool.dma_start(g.lg2[:, :], a["rwkv_g2"][0]).then_inc(sem("lora_in"), 16)
            own.link(nc.gpsimd.memset(g.ones, 1.0))
            own.link(nc.gpsimd.memset(g.eps_norm, NORM_EPS))
            own.link(nc.gpsimd.memset(g.eps_gn, GN_EPS))
            own.link(nc.gpsimd.memset(g.head_ones, 0.0))
            own.link(nc.gpsimd.memset(g.head_ones[0:64, 0:64], 1.0))
            own.link(nc.gpsimd.memset(g.head_ones[64:128, 64:128], 1.0))
            own.link(nc.gpsimd.memset(g.mask_s, 0.0))
            own.link(nc.gpsimd.memset(g.mask_l, 0.0))
            own.link(nc.gpsimd.memset(g.mask_i, 0.0))
            for q in range(2):
                r = slice(q * L, (q + 1) * L)
                for msk in (g.mask_s, g.mask_l, g.mask_i):
                    own.link(nc.gpsimd.memset(msk[r, r], 1.0))
            own.link(nc.gpsimd.memset(g.amask, 0.0))
            for msk, op, sign in ((g.mask_s, ALU.is_gt, 1), (g.mask_l, ALU.is_gt, -1), (g.mask_i, ALU.is_ge, 1)):
                own.link(nc.gpsimd.affine_select(out=msk, in_=msk, compare_op=op, fill=0.0, base=0,
                                        pattern=[[sign, P]], channel_multiplier=-sign))
            own.link(nc.gpsimd.affine_select(out=g.amask, in_=g.amask, compare_op=ALU.is_ge, fill=NEG, base=P,
                                             pattern=[[0, 3], [-1, SEQ]], channel_multiplier=1))
            own.link(nc.gpsimd.affine_select(out=g.amask[:, 0], in_=g.amask[:, 0], compare_op=ALU.is_ge, fill=NEG,
                                    base=SPAN - P, pattern=[[1, SEQ]], channel_multiplier=-1))
            ti = g.pt2.rearrange("p u n -> p (u n)")[:, 0:SEQ].bitcast(mybir.dt.int32)
            own.link(nc.gpsimd.iota(ti, pattern=[[-1, SEQ]], base=P, channel_multiplier=1))
            nc.gpsimd.memset(g.stat, 0.0).then_inc(sem("consts_set"), 1)

        @block.vector
        def _(dve):
            own = Own(dve, sem("dve_steps"))
            tt, ts, stt = nc.vector.tensor_tensor, nc.vector.tensor_scalar, nc.vector.scalar_tensor_tensor

            def bc(v, n):
                return v.unsqueeze(2).broadcast_to([P, v.shape[1], n])

            dve.wait_ge(sem("consts_set"), 1)
            ti = g.pt2.rearrange("p u n -> p (u n)")[:, 0:SEQ].bitcast(mybir.dt.int32)
            tr = g.pt2.rearrange("p u n -> p (u n)")[:, 256:512].bitcast(mybir.dt.int32)
            neg = g.pt2.rearrange("p u n -> p (u n)")[:, 512:768]
            own.link(ts(neg, ti, 0, NEG, ALU.is_lt, ALU.mult))
            for q in (1, 2):
                own.link(ts(tr, ti, DIL[q] - 1, None, ALU.bitwise_and))
                own.link(ts(g.amask[:, q], tr, 0, NEG, ALU.is_gt, ALU.mult))
                own.link(tt(g.amask[:, q], g.amask[:, q], neg, ALU.min))

            for k, (name, src) in enumerate((("mem", g.memx), ("x", x))):
                dve.wait_ge(sem("root_set"), k + 1)
                own.link(nc.vector.reciprocal(g.stat[:, 8 + 2 * k:10 + 2 * k], g.stat[:, 4 + 2 * k:6 + 2 * k]))
                for i in range(NT):
                    dst = src[:, i] if k == 0 else g.zs[:, i * D:(i + 1) * D]
                    nc.vector.tensor_scalar(dst, src[:, i], g.stat[:, 8 + 2 * k + i:9 + 2 * k + i], None, ALU.mult) \
                        .then_inc(sem("normed"), 1)
            dve.wait_ge(sem("cols_set"), 1)
            for k, (dst, gain) in enumerate(((g.memT, "ln_mem"), (hT, "ln1"))):
                for q in range(4):
                    n = 4 * k + q
                    dve.wait_ge(sem("turned"), n + 1)
                    tt(dst[:, 2 * q:2 * q + 2], cut(bank(n % 2), k=2), bc(param(gain)[:, 2 * q:2 * q + 2], SEQ),
                       ALU.mult).then_inc(sem("turned_out"), 1)

            mu = param("token_mu")
            for q, (dst, first, n) in enumerate(((g.rT, 0, 4), (g.kT, 4, 4), (g.vT, 8, 4), (g.lora, 12, 2))):
                dve.wait_ge(sem("z_out"), first // 2 + (n + 1) // 2)
                z, zp = g.Zraw[:, first:first + n, 1:257], g.Zraw[:, first:first + n, 0:256]
                d = g.tmp[:, 0:n]
                own.link(tt(d, zp, z, ALU.subtract))
                own.link(tt(d, d, bc(mu[:, first:first + n], SEQ), ALU.mult))
                tt(dst, d, z, ALU.add).then_inc(sem("shifted"), 1)
                dve.wait_ge(sem("shifted"), q + 1)
            dve.wait_ge(sem("shifted"), 4)
            own.link(tt(g.kkT, g.kT, bc(param("rwkv_k_k"), SEQ), ALU.mult))
            tt(g.t1, g.kkT, g.kkT, ALU.mult).then_inc(sem("kk_squared"), 1)
            for q in range(2):
                dve.wait_ge(sem("kk_summed"), q + 1)
                ts(g.t1[:, 2 * q:2 * q + 2], cut(bank(6 + q), k=2), 1e-24, None, ALU.max) \
                    .then_inc(sem("kk_sum_out"), 1)
            dve.wait_ge(sem("kk_root"), 1)
            own.link(nc.vector.reciprocal(g.t1, g.t1))
            own.link(tt(g.kkT, g.kkT, g.t1, ALU.mult))
            dve.wait_ge(sem("a_set"), 1)
            own.link(ts(g.t2, g.aT, -1.0, None, ALU.add))
            own.link(tt(g.t2, g.t2, bc(param("rwkv_k_a"), SEQ), ALU.mult))
            own.link(stt(g.kT, g.t2, 1.0, g.kT, ALU.add, ALU.mult))
            own.link(tt(g.t2, g.rT, g.kT, ALU.mult))
            tt(g.t2, g.t2, bc(param("rwkv_r_k"), SEQ), ALU.mult).then_inc(sem("rk_set"), 1)
            own.link(tt(g.aT, g.aT, g.kkT, ALU.mult))
            dve.wait_ge(sem("decay_set"), 1)
            nc.vector.memset(g.t3, 0.0)
            fl = lambda v: v.rearrange("p k n -> p (k n)")
            ch = lambda v: v.rearrange("p k (c t) -> p (k c) t", t=L)
            own.link(nc.vector.memset(g.t1, 0.0))
            own.link(nc.vector.tensor_copy(ch(g.t3)[:, :, 0:1], ch(g.tmp)[:, :, 0:1]))
            own.link(nc.vector.memset(ch(g.tmp)[:, :, 0:1], 0.0))
            own.link(nc.vector.tensor_tensor_scan(fl(g.dec), fl(g.tmp), fl(g.t3), 0.0, ALU.mult, ALU.add))
            own.link(nc.vector.tensor_copy(g.p_last.rearrange("p k c -> p (k c)").unsqueeze(2),
                                           ch(g.dec)[:, :, L - 1:L]))
            nc.vector.tensor_scalar(ch(g.t1)[:, :, 0:1], ch(g.kkT)[:, :, 0:1], -1.0, None, ALU.mult)
            own.link(stt(ch(g.t1)[:, :, 1:L], ch(g.kkT)[:, :, 1:L], -1.0, ch(g.dec)[:, :, 0:L - 1],
                         ALU.mult, ALU.mult))
            nc.vector.tensor_copy(g.kkT, g.t1)
            own.link(tt(g.rT, g.rT, g.dec, ALU.mult))
            own.link(nc.vector.reciprocal(g.dec, g.dec))
            tt(g.kT, g.kT, g.dec, ALU.mult)
            tt(g.aT, g.aT, g.dec, ALU.mult).then_inc(sem("tildes_set"), 1)
            dve.wait_ge(sem("tildes_set"), 1)
            for q in range(2):
                dve.wait_ge(sem("rk_summed"), q + 1)
                own.link(tt(g.dec[:, 2 * q:2 * q + 2], cut(bank(6 + q), k=2), g.vT[:, 2 * q:2 * q + 2], ALU.mult))
            for q, (buf, k0, gain) in enumerate(NORM_GROUPS):
                t = {"qk": g.qk, "mq": g.mq, "mk": g.mk}[buf][:, k0:k0 + 4]
                dve.wait_ge(sem("dil_out"), C_GATE - C_QK)
                if q:
                    dve.wait_ge(sem("qk_summed"), q)
                tt(g.t1, t, t, ALU.mult).then_inc(sem("squared"), 1)
                dve.wait_ge(sem("qk_root"), q + 1)
                own.link(nc.vector.reciprocal(g.t2, g.t2))
                for h in range(2):
                    c = slice(2 * h, 2 * h + 2)
                    ins = stt(t[:, c], t[:, c], param(gain[h]), g.t2[:, c], ALU.mult, ALU.mult)
                ins.then_inc(sem("qk_normed"), 1)
            def attention_out(u):
                kind, h, i = UNITS[u]
                dve.wait_ge(sem("pv_done"), u + 1)
                if kind == "mem":
                    dst, src = g.y_mem[:, h, i * P:(i + 1) * P], bank(u % 2)[:, 0:P]
                else:
                    r = slice(64 * (h % 2), 64 * (h % 2) + 64)
                    dst, src = g.y_dil[r, h // 2, i * P:(i + 1) * P], bank(u % 2)[r, 0:P]
                nc.vector.tensor_copy(dst, src).then_inc(sem("attended"), 1)

            for u, unit in enumerate(UNITS):
                n = unit_keys(unit)
                sc = g.sc2[:, u % 2, 0:n]
                pb = 2 + 2 * (u % 2)
                dve.wait_ge(sem("scored"), u + 1)
                if u >= 2:
                    dve.wait_ge(sem("probs_turned"), u - 1)
                if unit[0] == "mem":
                    own.link(nc.vector.tensor_copy(sc, bank(pb, 2)[:, 0:n]))
                    scale = float(P) ** -0.5
                else:
                    w = n // 3
                    own.link(tt(cut(sc, g=3), bank(pb, 2)[:, 0:3 * SEQ].rearrange("p (g n) -> p g n", g=3)[:, :, 0:w],
                                g.amask[:, :, SEQ - w:SEQ], ALU.add))
                    scale = float(HD) ** -0.5
                s = g.stat[:, 16 + 4 * (u % 2):20 + 4 * (u % 2)]
                own.link(nc.vector.tensor_reduce(out=s[:, 0:1], in_=sc, axis=AX, op=ALU.max))
                ts(s[:, 1:2], s[:, 0:1], -scale, None, ALU.mult).then_inc(sem("max_set"), 1)
                dve.wait_ge(sem("exp_set"), u + 1)
                own.link(nc.vector.reciprocal(s[:, 3:4], s[:, 2:3]))
                ts(sc, sc, s[:, 3:4], None, ALU.mult).then_inc(sem("probs_set"), 1)
                if u:
                    attention_out(u - 1)
            attention_out(len(UNITS) - 1)

            nc.vector.memset(g.S_hist[:, 0], 0.0)
            for r in range(4):
                for u in (2 * r, 2 * r + 1):
                    e, i, hp = u % 2, u // 4, u % 4
                    b = 2 + 3 * e
                    dve.wait_ge(sem("grams_done"), u + 1)
                    if r == 0 and e == 0:
                        dve.wait_ge(sem("tok_out"), 8)
                    w = bank(b).rearrange("p (q j n) -> p q j n", q=2, j=2)
                    v = bank(b + 2).rearrange("p (q n) -> p q n", q=2)
                    qxn = g.qxn4[:, e]
                    m2 = lambda k: k.unsqueeze(1).broadcast_to([P, 2, P])
                    pr = 8 * i + 2 * hp
                    own.link(tt(qxn[:, :, 0], w[:, :, 0], m2(g.mask_s), ALU.mult))
                    tt(qxn[:, :, 1], w[:, :, 1], m2(g.mask_l), ALU.mult)
                    tt(g.mrb[:, pr:pr + 2], bank(b + 1)[:, 0:2 * P].rearrange("p (q n) -> p q n", q=2),
                       m2(g.mask_i), ALU.mult)
                    tt(g.xx4[:, e], qxn[:, :, 0], m2(ident), ALU.add)
                    tt(g.ak4[:, e], v[:, :, 0:P], m2(g.mask_s), ALU.mult)
                    tt(g.rk4[:, e], v[:, :, P:2 * P], m2(g.mask_i), ALU.mult).then_inc(sem("grams_out"), 1)
                for lv in range(1, LEVELS):
                    for u in (2 * r, 2 * r + 1):
                        e = u % 2
                        dve.wait_ge(sem("level_done"), 2 * LEVELS * r + 2 * lv + e + 1)
                        tt(g.xx4[:, e], g.xx4[:, e], bank(3 + 3 * e)[:, 0:2 * P].rearrange("p (q n) -> p q n", q=2),
                           ALU.add) \
                            .then_inc(sem("x_updated"), 1)
                for u in (2 * r, 2 * r + 1):
                    e, i, hp = u % 2, u // 4, u % 4
                    o = bank(4 + 3 * e)
                    dve.wait_ge(sem("mv_done"), u + 1)
                    nc.vector.tensor_copy(g.mv2[:, e], o[:, 0:P].rearrange("p (q n) -> p q n", q=2)) \
                        .then_inc(sem("mv_out"), 1)
                    dve.wait_ge(sem("wz_done"), u + 1)
                    nc.vector.tensor_copy(g.Zt[:, i, hp * P:(hp + 1) * P], o[:, P:2 * P])
                    nc.vector.tensor_copy(g.WT[:, hp, i * P:(i + 1) * P], o[:, 2 * P:3 * P])
                    nc.vector.tensor_copy(g.Y0[:, hp, i * P:(i + 1) * P], o[:, 3 * P:4 * P]) \
                        .then_inc(sem("wz_out"), 1)
            for c in range(NCH):
                i, cb = c // 2, L * (c % 2)
                if c == 0:
                    dve.wait_ge(sem("wz_out"), 8)
                    nc.vector.tensor_copy(g.U[0:L, 0], g.Zt[0:L, 0]).then_inc(sem("u_set"), 1)
                else:
                    dve.wait_ge(sem("u_done"), c)
                    tt(g.U[cb:cb + L, i], bank(2)[cb:cb + L, :], g.Zt[cb:cb + L, i], ALU.add) \
                        .then_inc(sem("u_set"), 1)
                if c == NCH - 1:
                    break
                dve.wait_ge(sem("s_done"), c + 1)
                s1 = g.S_hist[:, c + 1].rearrange("p (k n) -> p k n", k=4)
                own.link(tt(g.S_hist[:, c + 1], bank(3)[:, 0:256], g.S_hist[:, c], ALU.add))
                tt(s1, s1, g.p_last[:, :, c:c + 1].broadcast_to([P, 4, HD]), ALU.mult) \
                    .then_inc(sem("s_set"), 1)
                dve.wait_ge(sem("s_set"), c + 1)
            Y = g.Y0
            for i in range(NT):
                dve.wait_ge(sem("y_done"), i + 1)
                own.link(tt(Y[:, :, i * P:(i + 1) * P], Y[:, :, i * P:(i + 1) * P],
                            bank(4 + i).rearrange("p (k n) -> p k n", k=4), ALU.add))
            dve.wait_ge(sem("dve_steps"), own.n)
            nc.vector.tensor_copy(g.y_rwkv, Y).then_inc(sem("y_summand"), 1)
            for q in range(2):
                dve.wait_ge(sem("y_summed"), q + 1)
                own.link(stt(g.y_rwkv[:, 2 * q:2 * q + 2], cut(bank(6 + q), k=2), -1.0 / HD,
                             Y[:, 2 * q:2 * q + 2], ALU.mult, ALU.add))
            tt(g.rT, g.y_rwkv, g.y_rwkv, ALU.mult).then_inc(sem("y_squared"), 1)
            dve.wait_ge(sem("y_root"), 1)
            own.link(nc.vector.reciprocal(g.kT, g.kT))
            own.link(tt(g.y_rwkv, g.y_rwkv, g.kT, ALU.mult))
            own.link(tt(g.y_rwkv, g.y_rwkv, bc(param("rwkv_ln_w"), SEQ), ALU.mult))
            own.link(tt(g.y_rwkv, g.y_rwkv, bc(param("rwkv_ln_b"), SEQ), ALU.add))
            own.link(tt(g.y_rwkv, g.y_rwkv, g.dec, ALU.add))
            tt(g.y_rwkv, g.y_rwkv, g.gT, ALU.mult).then_inc(sem("y_rwkv_set"), 1)

            for q, (gb, first) in enumerate(MIX):
                b = 2 + 2 * (q % 2)
                t = (g.rT, g.kT)[q % 2]
                dve.wait_ge(sem("mix_done"), q + 1)
                dve.wait_ge(sem("gates_out"), 12)
                dst = hT[:, first:first + 4]
                w = cut(bank(b, 2), k=4)
                if gb == 2:
                    tt(dst, w, g.gates[:, 8 * gb + first:8 * gb + first + 4], ALU.mult) \
                        .then_inc(sem("mix_out"), 1)
                else:
                    tt(t, w, g.gates[:, 8 * gb + first:8 * gb + first + 4], ALU.mult).then_inc(sem("mix_out"), 1)
                    dve.wait_ge(sem("mix_out"), q + 1)
                    tt(dst, dst, t, ALU.add).then_inc(sem("mixed"), 1)
            for q in range(4):
                dve.wait_ge(sem("out_done"), q + 1)
                tt(x[:, :, q * CW:(q + 1) * CW], x[:, :, q * CW:(q + 1) * CW],
                   bank(q % 2).rearrange("p (i n) -> p i n", i=2), ALU.add).then_inc(sem("x2_set"), 1)

        @block.scalar
        def _(act):
            own = Own(act, sem("act_steps"))
            act.wait_ge(sem("consts_set"), 1)
            for k, (name, src) in enumerate((("mem", g.memx), ("x", x))):
                act.wait_ge(sem(name + "_in"), 16)
                for i in range(NT):
                    own.link(nc.scalar.activation(g.sq, src[:, i], ACT.Square,
                                                  accum_out=g.stat[:, 2 * k + i:2 * k + i + 1]))
                nc.scalar.activation(g.stat[:, 4 + 2 * k:6 + 2 * k], g.stat[:, 2 * k:2 * k + 2], ACT.Sqrt,
                                     bias=g.eps_norm, scale=1.0 / D).then_inc(sem("root_set"), 1)
            act.wait_ge(sem("cols_turned"), 1)
            nc.scalar.activation(cols[:, 0:NROWS], bank(7)[:, 0:NROWS], ACT.Copy).then_inc(sem("cols_set"), 1)
            act.wait_ge(sem("normed"), 4)
            act.wait_ge(sem("turned"), 8)
            zero = g.stat[:, 63:64].unsqueeze(2).broadcast_to([P, 14, 1])
            own.link(nc.scalar.activation(g.Zraw[:, :, 0:1], zero, ACT.Copy))

            def evacuate(n, dst, func=ACT.Copy):
                act.wait_ge(sem("proj_done"), n + 1)
                w = bank(n % 2).rearrange("p (q n) -> p q n", q=2)
                return nc.scalar.activation(dst, w, func)

            for n in range(C_QK):
                evacuate(n, g.Zraw[:, 2 * n:2 * n + 2, 1:257]).then_inc(sem("z_out"), 1)
            act.wait_ge(sem("shifted"), 4)
            nc.scalar.activation(g.lora[0:64, 0], g.lora[0:64, 0], ACT.Tanh)
            nc.scalar.activation(g.lora[:, 1], g.lora[:, 1], ACT.Sigmoid).then_inc(sem("lora_set"), 1)
            for n in range(C_QK, C_QK + 2):
                evacuate(n, g.qk[:, 2 * (n - C_QK):2 * (n - C_QK) + 2]).then_inc(sem("dil_out"), 1)
            act.wait_ge(sem("lora_done"), 1)
            for k in range(4):
                own.link(nc.scalar.activation(g.tmp[:, k], bank(2, 2)[:, k * SEQ:(k + 1) * SEQ], ACT.Sigmoid,
                                              bias=param("rwkv_w0")[:, k:k + 1]))
            for k in range(4):
                ins = nc.scalar.activation(g.aT[:, k], bank(4, 2)[:, k * SEQ:(k + 1) * SEQ], ACT.Sigmoid,
                                           bias=param("rwkv_a0")[:, k:k + 1])
            ins.then_inc(sem("a_set"), 1)
            nc.scalar.activation(g.gT, cut(bank(6, 2), k=4), ACT.Copy).then_inc(sem("g_out"), 1)
            nc.scalar.activation(g.tmp, g.tmp, ACT.Exp, scale=-float(np.exp(-0.5))).then_inc(sem("decay_set"), 1)
            act.wait_ge(sem("kk_sum_out"), 2)
            nc.scalar.activation(g.t1, g.t1, ACT.Sqrt).then_inc(sem("kk_root"), 1)
            for n in range(C_QK + 2, C_GATE):
                if n < C_V:
                    ins = evacuate(n, g.qk[:, 2 * (n - C_QK):2 * (n - C_QK) + 2])
                elif n < C_MQ:
                    ins = evacuate(n, g.vtok[:, :, (n - C_V) * CW:(n - C_V + 1) * CW])
                elif n < C_MK:
                    ins = evacuate(n, g.mq[:, 2 * (n - C_MQ):2 * (n - C_MQ) + 2])
                elif n < C_MV:
                    ins = evacuate(n, g.mk[:, 2 * (n - C_MK):2 * (n - C_MK) + 2])
                else:
                    ins = evacuate(n, g.mv[:, :, (n - C_MV) * CW:(n - C_MV + 1) * CW])
                ins.then_inc(sem("dil_out"), 1)
            for q, (buf, k0, gain) in enumerate(NORM_GROUPS):
                width = HD if buf == "qk" else P
                act.wait_ge(sem("qk_summed"), q + 1)
                nc.scalar.activation(g.t2, cut(bank(2 + 2 * (q % 2), 2), k=4), ACT.Sqrt, bias=g.eps_norm,
                                     scale=1.0 / width).then_inc(sem("qk_root"), 1)
                act.wait_ge(sem("qk_normed"), q + 1)

            for u, unit in enumerate(UNITS):
                n = unit_keys(unit)
                sc = g.sc2[:, u % 2, 0:n]
                s = g.stat[:, 16 + 4 * (u % 2):20 + 4 * (u % 2)]
                scale = float(P if unit[0] == "mem" else HD) ** -0.5
                act.wait_ge(sem("max_set"), u + 1)
                nc.scalar.activation(sc, sc, ACT.Exp, bias=s[:, 1:2], scale=scale, accum_out=s[:, 2:3]) \
                    .then_inc(sem("exp_set"), 1)
                act.wait_ge(sem("probs_turned"), u + 1)
                if u >= 2:
                    act.wait_ge(sem("pv_done"), u - 1)
                nc.scalar.activation(g.pt2[:, u % 2, 0:n], bank(6, 2)[:, 0:n], ACT.Copy) \
                    .then_inc(sem("pt_set"), 1)
            for q in range(4):
                for i in range(NT):
                    n = 2 * q + i
                    act.wait_ge(sem("tok_turned"), n + 1)
                    act.wait_ge(sem("attended"), len(UNITS))
                    nc.scalar.activation((g.tok_a, g.tok_b, g.tok_k, g.tok_v)[q][:, i], bank(2 + n % 2), ACT.Copy) \
                        .then_inc(sem("tok_out"), 1)

            def gate_out(n):
                evacuate(C_GATE + n, g.gates[:, 2 * n:2 * n + 2], ACT.Sigmoid).then_inc(sem("gates_out"), 1)

            for r in range(4):
                for lv in range(LEVELS - 1):
                    for u in (2 * r, 2 * r + 1):
                        e = u % 2
                        act.wait_ge(sem("level_done"), 2 * LEVELS * r + 2 * lv + e + 1)
                        nc.scalar.activation(g.qxn4[:, e].rearrange("p q j n -> p (q j n)"), bank(2 + 3 * e), ACT.Copy) \
                            .then_inc(sem("q_updated"), 1)
                    if lv % 2 == 1:
                        if 2 * r + lv // 2 < 8:
                            gate_out(2 * r + lv // 2)
            for n in range(8, 12):
                gate_out(n)
            act.wait_ge(sem("var_done"), 1)
            nc.scalar.activation(g.kT, cut(bank(2, 2), k=4), ACT.Sqrt, bias=g.eps_gn, scale=1.0 / HD) \
                .then_inc(sem("y_root"), 1)

        @block.tensor
        def _(pe):
            mm, tr = nc.tensor.matmul, nc.tensor.transpose

            turns = [0]

            def row_tile_done(instruction):
                turns[0] += 1
                instruction.then_inc(sem("row_tile_done"), 1)
                pe.wait_ge(sem("row_tile_done"), turns[0])

            def load_wait(n):
                pe.wait_ge(g.arrived[(FIRST + n) % LO], 16 * g.nth(n))

            pe.wait_ge(sem("ident_set"), 1)
            pe.wait_ge(sem("rows_in"), 16 * (len(ROWS) + 2))
            tr(bank(7)[:, 0:NROWS], g.prow, ident[0:NROWS, 0:NROWS]).then_inc(sem("cols_turned"), 1)
            for k, src in enumerate((g.memx, None)):
                for q in range(4):
                    n = 4 * k + q
                    if n >= 2:
                        pe.wait_ge(sem("turned_out"), n - 1)
                    for kk in range(2):
                        for i in range(NT):
                            if q == 0 and kk == 0:
                                pe.wait_ge(sem("normed"), 2 * k + i + 1)
                            row = src[:, i] if k == 0 else g.zs[:, i * D:(i + 1) * D]
                            ins = tr(bank(n % 2)[:, kk * SEQ + i * P:kk * SEQ + (i + 1) * P],
                                     row[:, (2 * q + kk) * P:(2 * q + kk + 1) * P], ident)
                    ins.then_inc(sem("turned"), 1)
            pe.wait_ge(sem("turned_out"), 8)

            def project(n, src, token_major=False):
                load_wait(n)
                w = cut(g.ring(n), k=KD)
                if 2 <= n < C_QK:
                    pe.wait_ge(sem("z_out"), n - 1)
                elif C_QK <= n < C_QK + 2:
                    pe.wait_ge(sem("z_out"), n - 1)
                elif C_QK + 2 <= n < C_GATE + 2:
                    pe.wait_ge(sem("dil_out"), n - 1 - C_QK)
                elif n >= C_GATE + 2:
                    pe.wait_ge(sem("gates_out"), n - 1 - C_GATE)
                for q in range(2):
                    o = bank(n % 2)[:, q * SEQ:(q + 1) * SEQ]
                    for k in range(KD):
                        if token_major:
                            ins = mm(o, src[:, k, q * P:(q + 1) * P], w[:, k, :], start=(k == 0), stop=(k == KD - 1))
                        else:
                            ins = mm(o, w[:, k, q * P:(q + 1) * P], src[:, k, :], start=(k == 0), stop=(k == KD - 1))
                ins.then_inc(sem("proj_done"), 1)

            for n in range(C_QK):
                project(n, hT)
            for n in range(C_QK, C_QK + 2):
                project(n, hT)
            pe.wait_ge(sem("lora_set"), 1)
            pe.wait_ge(sem("lora_in"), 48)
            for k in range(4):
                c = slice(k * P, (k + 1) * P)
                o = slice(k * SEQ, (k + 1) * SEQ)
                mm(bank(2, 2)[:, o], g.lw2[0:64, c], g.lora[0:64, 0], start=True, stop=True)
                mm(bank(4, 2)[:, o], g.lw2[64:128, c], g.lora[64:128, 0], start=True, stop=True)
                ins = mm(bank(6, 2)[:, o], g.lg2[:, c], g.lora[:, 1], start=True, stop=True)
            ins.then_inc(sem("lora_done"), 1)
            project(C_QK + 2, hT)
            pe.wait_ge(sem("g_out"), 1)
            pe.wait_ge(sem("kk_squared"), 1)
            for q in range(2):
                mm(bank(6 + q), g.head_ones, g.t1[:, 2 * q:2 * q + 2], start=True, stop=True) \
                    .then_inc(sem("kk_summed"), 1)
            for n in range(C_QK + 3, C_V):
                project(n, hT)
            for n in range(C_V, C_MQ):
                project(n, hT, True)
            for n in range(C_MQ, C_MK):
                project(n, hT)
            for n in range(C_MK, C_MV):
                project(n, g.memT)
            for n in range(C_MV, C_GATE):
                project(n, g.memT, True)
            pe.wait_ge(sem("rk_set"), 1)
            pe.wait_ge(sem("kk_sum_out"), 2)
            for q in range(2):
                mm(bank(6 + q), g.head_ones, g.t2[:, 2 * q:2 * q + 2], start=True, stop=True) \
                    .then_inc(sem("rk_summed"), 1)
            for q, (buf, k0, gain) in enumerate(NORM_GROUPS):
                pe.wait_ge(sem("squared"), q + 1)
                for h in range(2):
                    ins = mm(bank(2 + 2 * (q % 2) + h), g.head_ones if buf == "qk" else g.ones,
                             g.t1[:, 2 * h:2 * h + 2], start=True, stop=True)
                ins.then_inc(sem("qk_summed"), 1)

            def scores(u):
                kind, h, i = UNITS[u]
                if u < 2:
                    pe.wait_ge(sem("qk_normed"), len(NORM_GROUPS))
                else:
                    pe.wait_ge(sem("max_set"), u - 1)
                pb = 2 + 2 * (u % 2)
                if kind == "mem":
                    ins = mm(bank(pb)[:, 0:SEQ], g.mq[:, h, i * P:(i + 1) * P], g.mk[:, h], start=True, stop=True)
                else:
                    w = P * (i + 1)
                    for gr in range(DG):
                        gh = gr * DH + h
                        r = slice(64 * (gh % 2), 64 * (gh % 2) + 64)
                        ins = mm(bank(pb, 2)[:, gr * SEQ:gr * SEQ + w], g.qk[r, gh // 2, i * P:(i + 1) * P],
                                 g.qk[r, 6 + gh // 2, 0:w], start=True, stop=True)
                ins.then_inc(sem("scored"), 1)

            def attend(u):
                kind, h, i = UNITS[u]
                blocks = unit_keys(UNITS[u]) // P
                pe.wait_ge(sem("probs_set"), u + 1)
                if u == 0:
                    pe.wait_ge(sem("tildes_set"), 1)
                else:
                    pe.wait_ge(sem("pt_set"), u)
                for b in range(blocks):
                    ins = tr(bank(6, 2)[:, b * P:(b + 1) * P], g.sc2[:, u % 2, b * P:(b + 1) * P], ident)
                ins.then_inc(sem("probs_turned"), 1)
                pe.wait_ge(sem("pt_set"), u + 1)
                if u >= 2:
                    pe.wait_ge(sem("attended"), u - 1)
                elif u == 0:
                    pe.wait_ge(sem("dil_out"), C_GATE - C_QK)
                o = bank(u % 2)
                for b in range(blocks):
                    if kind == "mem":
                        ins = mm(o[:, 0:P], g.mv[:, b, h * P:(h + 1) * P], g.pt2[:, u % 2, b * P:(b + 1) * P],
                                 start=(b == 0), stop=(b == blocks - 1))
                    else:
                        gr, kt = b // (i + 1), b % (i + 1)
                        gh = gr * DH + h
                        ins = mm(o[64 * (h % 2):64 * (h % 2) + 64, 0:P], g.vtok[:, kt, gh * HD:(gh + 1) * HD],
                                 g.pt2[:, u % 2, b * P:(b + 1) * P], start=(b == 0), stop=(b == blocks - 1))
                ins.then_inc(sem("pv_done"), 1)

            scores(0)
            for u in range(len(UNITS)):
                if u + 1 < len(UNITS):
                    scores(u + 1)
                attend(u)
            pe.wait_ge(sem("attended"), len(UNITS))
            for q, src in enumerate((g.kkT, g.aT, g.kT, g.vT)):
                for i in range(NT):
                    n = 2 * q + i
                    if n >= 2:
                        pe.wait_ge(sem("tok_out"), n - 1)
                    for k in range(4):
                        ins = tr(bank(2 + n % 2)[:, k * P:(k + 1) * P], src[:, k, i * P:(i + 1) * P], ident)
                    ins.then_inc(sem("tok_turned"), 1)
            pe.wait_ge(sem("tok_out"), 8)
            rows = (slice(0, 64), slice(64, 128))
            for r in range(4):
                units = (2 * r, 2 * r + 1)
                for u in units:
                    e, i, hp = u % 2, u // 4, u % 4
                    b = 2 + 3 * e
                    if u >= 2:
                        pe.wait_ge(sem("wz_out"), u - 1)
                    t = slice(i * P, (i + 1) * P)
                    for q in range(2):
                        A, B, K, R = (v[rows[q], hp, t] for v in (g.kkT, g.aT, g.kT, g.rT))
                        o, o2 = (bank(k)[:, q * SEQ:(q + 1) * SEQ] for k in (b, b + 2))
                        mm(o[:, 0:P], B, A, start=True, stop=True)
                        mm(o[:, P:2 * P], A, B, start=True, stop=True)
                        mm(bank(b + 1)[:, q * P:(q + 1) * P], B, R, start=True, stop=True)
                        mm(o2[:, 0:P], K, A, start=True, stop=True)
                        ins = mm(o2[:, P:2 * P], K, R, start=True, stop=True)
                        if q == 0:
                            row_tile_done(ins)
                    ins.then_inc(sem("grams_done"), 1)
                for lv in range(LEVELS):
                    for u in units:
                        e = u % 2
                        b = 2 + 3 * e
                        if lv == 0:
                            pe.wait_ge(sem("grams_out"), u + 1)
                        else:
                            pe.wait_ge(sem("q_updated"), 2 * (LEVELS - 1) * r + 2 * (lv - 1) + e + 1)
                        if lv > 1:
                            pe.wait_ge(sem("x_updated"), 2 * (LEVELS - 1) * r + 2 * (lv - 2) + e + 1)
                        for q in range(2):
                            Q, N = (g.qxn4[:, e, q, j] for j in range(2))
                            o = bank(b)[:, q * SEQ:(q + 1) * SEQ]
                            if lv < LEVELS - 1:
                                mm(o[:, 0:P], N, Q, start=True, stop=True)
                                ins = mm(o[:, P:2 * P], Q, N, start=True, stop=True)
                            if lv:
                                ins = mm(bank(b + 1)[:, q * P:(q + 1) * P], N, g.xx4[:, e, q], start=True, stop=True)
                        ins.then_inc(sem("level_done"), 1)
                    if lv % 2 == 1 and lv < LEVELS - 1 and 2 * r + lv // 2 < 8:
                        n = 2 * r + lv // 2
                        if n < 2:
                            pe.wait_ge(sem("attended"), len(UNITS))
                        project(C_GATE + n, hT)
                for u in units:
                    e, i, hp = u % 2, u // 4, u % 4
                    o = bank(4 + 3 * e)
                    for q in range(2):
                        hc = slice((2 * hp + q) * HD, (2 * hp + q + 1) * HD)
                        ins = mm(o[:, q * HD:(q + 1) * HD], g.ak4[:, e, q], g.tok_v[:, i, hc], start=True, stop=True)
                    ins.then_inc(sem("mv_done"), 1)
                for u in units:
                    e, i, hp = u % 2, u // 4, u % 4
                    o = bank(4 + 3 * e)
                    pe.wait_ge(sem("mv_out"), u + 1)
                    pe.wait_ge(sem("x_updated"), 2 * (LEVELS - 1) * r + 2 * (LEVELS - 2) + e + 1)
                    for q in range(2):
                        hc = slice((2 * hp + q) * HD, (2 * hp + q + 1) * HD)
                        X = g.xx4[:, e, q]
                        mm(o[:, P + q * HD:P + (q + 1) * HD], X, g.mv2[:, e, q], start=True, stop=True)
                        mm(o[rows[q], 2 * P:3 * P], g.tok_a[:, i, hc], X, start=True, stop=True)
                        ins = mm(o[rows[q], 3 * P:4 * P], g.tok_v[:, i, hc], g.rk4[:, e, q], start=True, stop=True)
                    ins.then_inc(sem("wz_done"), 1)
            pe.wait_ge(sem("wz_out"), 8)
            for c in range(NCH):
                i, cb = c // 2, L * (c % 2)
                cr, ct = slice(cb, cb + L), slice(c * L, (c + 1) * L)
                if c:
                    pe.wait_ge(sem("s_set"), c)
                    for h in (0, 2, 4, 6, 1, 3, 5, 7):
                        q, hp = h % 2, h // 2
                        ins = mm(bank(2)[cr, h * HD:(h + 1) * HD], g.WT[rows[q], hp, ct],
                                 g.S_hist[rows[q], c, hp * HD:(hp + 1) * HD], start=True, stop=True)
                        if h == 6:
                            row_tile_done(ins)
                    ins.then_inc(sem("u_done"), 1)
                project(C_GATE + 8 + c, hT)
                pe.wait_ge(sem("u_set"), c + 1)
                for h in range(RH) if c < NCH - 1 else ():
                    q, hp = h % 2, h // 2
                    hc = slice(h * HD, (h + 1) * HD)
                    o = bank(3)[rows[q], hp * HD:(hp + 1) * HD]
                    mm(o, g.tok_b[cr, i, hc], g.U[cr, i, hc], start=True, stop=False)
                    ins = mm(o, g.tok_k[cr, i, hc], g.tok_v[cr, i, hc], start=False, stop=True)
                    if h == RH - 1:
                        ins.then_inc(sem("s_done"), 1)
            for i in range(NT):
                for h in range(RH):
                    q, hp = h % 2, h // 2
                    ins = mm(bank(4 + i)[rows[q], hp * P:(hp + 1) * P], g.U[:, i, h * HD:(h + 1) * HD],
                             g.mrb[:, 8 * i + h], start=(h < 2), stop=False, skip_group_check=True)
                row_tile_done(ins)
                for h in (0, 2, 4, 6, 1, 3, 5, 7):
                    q, hp = h % 2, h // 2
                    for c in (2 * i, 2 * i + 1):
                        at = hp * P + (c % 2) * L
                        ins = mm(bank(4 + i)[rows[q], at:at + L], g.S_hist[rows[q], c, hp * HD:(hp + 1) * HD],
                                 g.rT[rows[q], hp, c * L:(c + 1) * L], start=False, stop=True, skip_group_check=True)
                    if h == 6:
                        row_tile_done(ins)
                ins.then_inc(sem("y_done"), 1)
            pe.wait_ge(sem("y_summand"), 1)
            for q in range(2):
                mm(bank(6 + q), g.head_ones, g.y_rwkv[:, 2 * q:2 * q + 2], start=True, stop=True) \
                    .then_inc(sem("y_summed"), 1)
            pe.wait_ge(sem("y_squared"), 1)
            for q in range(2):
                ins = mm(bank(2 + q), g.head_ones, g.rT[:, 2 * q:2 * q + 2], start=True, stop=True)
            ins.then_inc(sem("var_done"), 1)
            for q, (gb, first) in enumerate(MIX):
                n, kn = MIX_CHUNKS[q]
                if first == 0 or n != MIX_CHUNKS[q - 1][0]:
                    load_wait(n)
                w = cut(g.ring(n), k=kn)
                if q == 0:
                    pe.wait_ge(sem("y_root"), 1)
                if q >= 2:
                    pe.wait_ge(sem("mix_out"), q - 1)
                if gb == 0 and first == 0:
                    pe.wait_ge(sem("y_rwkv_set"), 1)
                yt = (g.y_rwkv, g.y_dil, g.y_mem)[gb]
                wm = 0 if w.shape[2] == 512 else first
                for mt in range(4):
                    o = bank(2 + 2 * (q % 2), 2)[:, mt * SEQ:(mt + 1) * SEQ]
                    for k in range(kn):
                        ins = mm(o, w[:, k, (wm + mt) * P:(wm + mt + 1) * P], yt[:, k], start=(k == 0),
                                 stop=(k == kn - 1))
                ins.then_inc(sem("mix_done"), 1)
            pe.wait_ge(sem("mixed"), 4)
            for q in range(4):
                n = C_OUT + q
                load_wait(n)
                w = cut(g.ring(n), k=KD)
                if q >= 2:
                    pe.wait_ge(sem("x2_set"), q - 1)
                for i in range(NT):
                    for k in range(KD):
                        ins = mm(bank(q % 2)[:, i * CW:(i + 1) * CW], hT[:, k, i * P:(i + 1) * P], w[:, k],
                                 start=(k == 0), stop=(k == KD - 1))
                ins.then_inc(sem("out_done"), 1)


def moe(nc, a, out, g):
    sem, bank, cut, param = g.sem, g.bank, g.cut, g.param
    x, ident = g.x, g.ident
    whole = g.part is None
    OWN = 8

    slots = [g.ring_lo[:, s] for s in range(LO)] + [g.ring_hi[:, s] for s in range(SLOTS - LO)]
    before_moe = [n if whole else 0 for n in g.lo_loads] + [0] * (SLOTS - LO)
    b1T, posj, gate = g.b1T, g.posj, g.gate

    def w_source(e, j):
        if j < W1C:
            w = a["w1"][0][bass.ds(e, 1), :, j * CW:(j + 1) * CW]
        else:
            w = a["w2"][0][bass.ds(e, 1), :, (j - W1C) * CW:(j - W1C + 1) * CW]
        return w.rearrange("o (k p) n -> p (o k) n", p=P)

    def n_over(engine):
        engine.wait_ge(sem("over_set"), 1)
        return engine.value_load(g.over_i[0:1, 32:33], min_val=0, max_val=MAX_OVER)

    def over_expert(engine, r):
        return engine.value_load(g.over_i[0:1, bass.ds(r + 16, 1)], min_val=0, max_val=E - 1)

    with nc.Block() as block:
        @block.sync
        def _(sp):
            if not whole:
                sp.dma_start(x, a["x"][0].rearrange("(i p) n -> p i n", p=P)).then_inc(sem("x_in2"), 16)
            for j in range(0 if not whole else LO, SLOTS):
                sp.dma_start(cut(slots[j], k=KD), w_source(0, j)).then_inc(g.arrived[j], 16)

            def load_expert(b, e):
                for j in range(SLOTS):
                    sp.wait_ge(sem("w_used"), SLOTS * b + (j + 1 - SLOTS))
                    sp.dma_start(cut(slots[j], k=KD), w_source(e, j)).then_inc(g.arrived[j], 16)

            with sp.Fori(1, E) as b:
                load_expert(b, b)
            count = n_over(sp)
            with sp.If(count > 0):
                with sp.Fori(0, count) as r:
                    load_expert(r + E, over_expert(sp, r))
            for i in range(NT):
                sp.wait_ge(sem("out_set"), i + 1)
                sp.dma_start(out[0][i * P:(i + 1) * P, :], x[:, i]).then_inc(sem("stored"), 16)
            sp.wait_ge(sem("stored"), 16 * NT)

        @block.gpsimd
        def _(pool):
            own = Own(pool, sem("pool_moe_steps"))
            pool.dma_start(cut(g.wr, k=KD), a["w_router"][0].rearrange("(k p) n -> p k n", p=P)) \
                .then_inc(sem("router_in"), 16)
            pool.dma_start(g.brow[0:1, :], a["b_router"]).then_inc(sem("router_in"), 16)
            pool.dma_start(g.b1raw[0:E, :], a["b1"][0]).then_inc(sem("b_in"), 16)
            pool.dma_start(g.b2raw[0:E, :], a["b2"][0]).then_inc(sem("b_in"), 16)
            if not whole:
                pool.dma_start(param("ln2"), a["ln2"][0].rearrange("(k p) -> p k", p=P), allow_slow_non_contiguous=True).then_inc(sem("b_in"), 16)
                nc.gpsimd.memset(g.ones, 1.0)
                nc.gpsimd.memset(g.stat, 0.0)
                nc.gpsimd.memset(g.eps_norm, NORM_EPS)
                own.link(nc.gpsimd.memset(ident, 0.0))
                own.link(nc.gpsimd.affine_select(out=ident, in_=ident, compare_op=ALU.not_equal, fill=1.0, base=0,
                                        pattern=[[-1, P]], channel_multiplier=1))
            own.link(nc.gpsimd.memset(g.before, 1.0))
            own.link(nc.gpsimd.affine_select(out=g.before, in_=g.before, compare_op=ALU.is_gt, fill=0.0, base=0,
                                             pattern=[[1, P]], channel_multiplier=-1))
            own.link(nc.gpsimd.iota(g.eio, pattern=[[1, E]], base=0, channel_multiplier=0,
                                    allow_small_or_imprecise_dtypes=True))
            own.link(nc.gpsimd.iota(g.slot_no, pattern=[[1, CAP]], base=0, channel_multiplier=0,
                                    allow_small_or_imprecise_dtypes=True))
            for j in range(1, NJ):
                own.link(nc.gpsimd.memset(g.rsc[E * (j - 1):E * j, 0:1], float(CAP * j)))
            nc.gpsimd.iota(g.rsc[0:E * (NJ - 1), 1:2], pattern=[[0, 1]], base=E, channel_multiplier=1,
                           allow_small_or_imprecise_dtypes=True).then_inc(sem("moe_consts"), 1)

        @block.vector
        def _(dve):
            own = Own(dve, sem("dve_moe_steps"))
            tt, ts, stt = nc.vector.tensor_tensor, nc.vector.tensor_scalar, nc.vector.scalar_tensor_tensor

            def bc(v, n):
                return v.unsqueeze(2).broadcast_to([P, v.shape[1], n])

            dve.wait_ge(sem("root2_set"), 1)
            own.link(nc.vector.reciprocal(g.stat[:, 8:10], g.stat[:, 4:6]))
            for i in range(NT):
                ts(g.xn[:, i], x[:, i], g.stat[:, 8 + i:9 + i], None, ALU.mult).then_inc(sem("xn_set"), 1)
            if not whole:
                dve.wait_ge(sem("b_in"), 48)
            for q in range(4):
                dve.wait_ge(sem("xn_turned"), q + 1)
                tt(g.xnT[:, 2 * q:2 * q + 2], cut(bank(4 + q % 2), k=2), bc(param("ln2")[:, 2 * q:2 * q + 2], SEQ),
                   ALU.mult).then_inc(sem("xnT_set"), 1)
            dve.wait_ge(sem("moe_consts"), 1)
            dve.wait_ge(sem("logits_done"), 1)
            own.link(nc.vector.tensor_copy(g.logit, bank(6)[:, 0:NT * E].rearrange("p (i e) -> p i e", i=NT)))
            ti = g.ti8.bitcast(mybir.dt.uint32)
            for i in range(NT):
                own.link(nc.vector.max(out=g.top8[:, i], in_=g.logit[:, i]))
                own.link(nc.vector.max_index(ti[:, i], g.top8[:, i], g.logit[:, i]))
            nc.vector.tensor_copy(g.tif, ti)
            ts(g.stat[:, 20:22].unsqueeze(2), g.top8[:, :, 0:1], -1.0, None, ALU.mult).then_inc(sem("top_set"), 1)
            dve.wait_ge(sem("top_exp"), 1)
            own.link(nc.vector.reciprocal(g.stat[:, 24:26], g.stat[:, 22:24]))
            for i in range(NT):
                own.link(ts(g.top8[:, i, 0:TOPK], g.top8[:, i, 0:TOPK], g.stat[:, 24 + i:25 + i], None, ALU.mult))
            for i in range(NT):
                for k in range(TOPK):
                    number, p = g.tif[:, i, k:k + 1], g.top8[:, i, k:k + 1]
                    if k == 0:
                        ts(gate[:, i], g.eio, number, p, ALU.is_equal, ALU.mult)
                        own.link(ts(g.chosen[:, i, 0:E], g.eio, number, None, ALU.is_equal))
                    else:
                        ts(g.oh[:, 0:E], g.eio, number, p, ALU.is_equal, ALU.mult)
                        own.link(ts(g.oh[:, E:2 * E], g.eio, number, None, ALU.is_equal))
                        tt(gate[:, i], gate[:, i], g.oh[:, 0:E], ALU.add)
                        own.link(tt(g.chosen[:, i, 0:E], g.chosen[:, i, 0:E], g.oh[:, E:2 * E], ALU.add))
            for i in range(NT):
                for j in (1, 2):
                    ins = nc.vector.tensor_copy(g.chosen[:, i, E * j:E * j + E], g.chosen[:, i, 0:E])
            ins.then_inc(sem("chosen_set"), 1)
            dve.wait_ge(sem("gateT_done"), 1)
            nc.vector.tensor_copy(g.gateT[0:E, :], bank(4)[0:E, 0:SEQ]).then_inc(sem("gateT_set"), 1)
            nc.vector.tensor_copy(b1T, bank(5).rearrange("p (two j e) -> p two j e", two=2, j=8))
            dve.wait_ge(sem("pos_done"), 1)
            own.link(stt(posj[:, :, 0:E], bank(6)[:, 64:64 + NT * E].rearrange("p (i e) -> p i e", i=NT), 1.0,
                         g.chosen[:, :, 0:E], ALU.add, ALU.mult))
            own.link(ts(posj[:, :, 0:E], posj[:, :, 0:E], -1.0, None, ALU.add))
            for j in range(1, NJ):
                own.link(ts(posj[:, :, E * j:E * j + E], posj[:, :, 0:E], -float(CAP * j), None, ALU.add))
            R = E * (NJ - 1)
            c = g.rsc[0:R]
            own.link(tt(c[:, 2:3], bank(7)[0:R, 0:1], c[:, 0:1], ALU.is_gt))
            stt(c[:, 3:4], c[:, 0:1], -0.5, c[:, 1:2], ALU.mult, ALU.add).then_inc(sem("flag_set"), 1)
            dve.wait_ge(sem("rank_done"), 1)
            own.link(nc.vector.tensor_copy(c[:, 4:5], bank(7)[0:R, 1:2]))
            ts(c[:, 16:32], g.slot_no[0:R, 0:16], c[:, 4:5], c[:, 2:3], ALU.is_equal, ALU.mult) \
                .then_inc(sem("ranked"), 1)
            dve.wait_ge(sem("list_done"), 1)
            nc.vector.tensor_copy(g.over_i[0:1, 0:33], bank(7)[0:1, 16:49]).then_inc(sem("over_set"), 1)

            start = own.n

            def block_of(b, e, column):
                own.base, own.n = b * OWN + start, 0
                for i in range(NT):
                    place = posj[:, i, bass.ds(column, 1)]
                    ts(g.sel[:, i], g.slot_no, place, None, ALU.is_equal)
                    ins = ts(g.selg[:, i], g.slot_no, place, gate[:, i, bass.ds(e, 1)], ALU.is_equal, ALU.mult)
                ins.then_inc(sem("sel_set"), 1)
                dve.wait_ge(sem("gathered"), b + 1)
                tt(g.xg, cut(bank(7), k=KD), bc(param("ln2"), CAP), ALU.mult).then_inc(sem("xg_set"), 1)
                for h in range(2):
                    c = slice(4 * h, 4 * h + 4)
                    bias = [b1T[:, two, c, bass.ds(e, 1)].broadcast_to([P, 4, CAP]) for two in range(2)]
                    dve.wait_ge(sem("w_used"), b * SLOTS + 4 * h + 4)
                    own.link(tt(g.hg[:, c], cut(bank(4 + h), k=8)[:, 0:4], bias[0], ALU.add))
                    ts(g.hg[:, c], g.hg[:, c], 7.0, None, ALU.min).then_inc(sem("glu_set"), 1)
                    own.link(tt(g.hl[:, c], cut(bank(4 + h), k=8)[:, 4:8], bias[1], ALU.add))
                    own.link(ts(g.hl[:, c], g.hl[:, c], 7.0, -7.0, ALU.min, ALU.max))
                    own.link(stt(g.hl[:, c], g.hl[:, c], 1.0, g.hg[:, c], ALU.add, ALU.mult))
                    dve.wait_ge(sem("sigmoid_set"), b * 2 + h + 1)
                    tt(g.actT[:, c], g.hl[:, c], g.hs[:, c], ALU.mult).then_inc(sem("act_set"), 1)
                assert own.n == OWN, own.n

            with dve.Fori(0, E) as b:
                block_of(b, b, b)
            count = n_over(dve)
            with dve.If(count > 0):
                with dve.Fori(0, count) as r:
                    column = dve.value_load(g.over_i[0:1, bass.ds(r, 1)], min_val=E, max_val=NJ * E - 1)
                    block_of(r + E, over_expert(dve, r), column)
            dve.wait_ge(sem("all_added"), 1)
            for i in range(NT):
                tt(x[:, i], x[:, i], bank(2 * i, 2), ALU.add).then_inc(sem("out_set"), 1)

        @block.scalar
        def _(act):
            own = Own(act, sem("act_moe_steps"))
            if not whole:
                act.wait_ge(sem("x_in2"), 16)
                act.wait_ge(sem("moe_consts"), 1)
            sq = g.xnT.rearrange("p k n -> p (k n)")[:, 0:D]
            for i in range(NT):
                own.link(nc.scalar.activation(sq, x[:, i], ACT.Square, accum_out=g.stat[:, i:i + 1]))
            nc.scalar.activation(g.stat[:, 4:6], g.stat[:, 0:2], ACT.Sqrt, bias=g.eps_norm, scale=1.0 / D) \
                .then_inc(sem("root2_set"), 1)
            act.wait_ge(sem("top_set"), 1)
            for i in range(NT):
                ins = nc.scalar.activation(g.top8[:, i, 0:TOPK], g.top8[:, i, 0:TOPK], ACT.Exp,
                                           bias=g.stat[:, 20 + i:21 + i], accum_out=g.stat[:, 22 + i:23 + i])
            ins.then_inc(sem("top_exp"), 1)

            def block_of(b):
                act.wait_ge(sem("selT_done"), b + 1)
                nc.scalar.activation(g.selT[0:CAP, :], bank(6)[0:CAP, 0:SEQ], ACT.Copy).then_inc(sem("selT_set"), 1)
                for h in range(2):
                    c = slice(4 * h, 4 * h + 4)
                    act.wait_ge(sem("glu_set"), b * 2 + h + 1)
                    nc.scalar.activation(g.hs[:, c], g.hg[:, c], ACT.Sigmoid, scale=1.702) \
                        .then_inc(sem("sigmoid_set"), 1)
                for h in range(2):
                    c = slice(4 * h, 4 * h + 4)
                    act.wait_ge(sem("w_used"), b * SLOTS + W1C + 2 * h + 2)
                    nc.scalar.activation(g.yeT[:, c], cut(bank(6 + h)[:, 0:256], k=4), ACT.Copy).then_inc(sem("yT_set"), 1)
                for h in range(2):
                    act.wait_ge(sem("y_turned"), b * 2 + h + 1)
                    nc.scalar.activation(g.ye[0:CAP, 512 * h:512 * h + 512], bank(6 + h)[0:CAP, :], ACT.Copy) \
                        .then_inc(sem("y_set"), 1)

            with act.Fori(0, E) as b:
                block_of(b)
            count = n_over(act)
            with act.If(count > 0):
                with act.Fori(0, count) as r:
                    block_of(r + E)

        @block.tensor
        def _(pe):
            mm, tr = nc.tensor.matmul, nc.tensor.transpose
            pe.wait_ge(sem("b_in"), 32 if whole else 48)
            if not whole:
                pe.wait_ge(sem("moe_consts"), 1)
            for i in range(NT):
                pe.wait_ge(sem("xn_set"), i + 1)
            for q in range(4):
                if q >= 2:
                    pe.wait_ge(sem("xnT_set"), q - 1)
                for kk in range(2):
                    for i in range(NT):
                        ins = tr(bank(4 + q % 2)[:, kk * SEQ + i * P:kk * SEQ + (i + 1) * P],
                                 g.xn[:, i, (2 * q + kk) * P:(2 * q + kk + 1) * P], ident)
                ins.then_inc(sem("xn_turned"), 1)
            pe.wait_ge(sem("router_in"), 32)
            pe.wait_ge(sem("xnT_set"), 4)
            for i in range(NT):
                o = bank(6)[:, i * E:(i + 1) * E]
                mm(o, g.ones[0:1, 0:P], g.brow[0:1, :], start=True, stop=False)
                for k in range(KD):
                    ins = mm(o, g.xnT[:, k, i * P:(i + 1) * P], cut(g.wr, k=KD)[:, k], start=False, stop=(k == KD - 1))
            ins.then_inc(sem("logits_done"), 1)
            for j in range(8):
                for two in range(2):
                    at = (two * 8 + j) * E
                    tr(bank(5)[:, at:at + E], g.b1raw[0:E, j * CW + two:(j + 1) * CW:2], ident[0:E, 0:E])
            pe.wait_ge(sem("chosen_set"), 1)
            for i in range(NT):
                ins = tr(bank(4)[0:E, i * P:(i + 1) * P], gate[:, i], ident)
            ins.then_inc(sem("gateT_done"), 1)
            first, second = g.chosen[:, 0], g.chosen[:, 1]
            mm(bank(6)[:, 64:64 + E], g.before, first[:, 0:E], start=True, stop=True)
            mm(bank(6)[:, 64 + E:64 + 2 * E], g.ones, first[:, 0:E], start=True, stop=False)
            mm(bank(6)[:, 64 + E:64 + 2 * E], g.before, second[:, 0:E], start=False, stop=True)
            R = E * (NJ - 1)
            mm(bank(7)[0:R, 0:1], first, g.ones[:, 0:1], start=True, stop=False)
            mm(bank(7)[0:R, 0:1], second, g.ones[:, 0:1], start=False, stop=True).then_inc(sem("pos_done"), 1)
            pe.wait_ge(sem("gateT_set"), 1)
            for i in range(NT):
                for h in range(2):
                    mm(bank(2 * i + h), g.gateT[0:E, i * P:(i + 1) * P], g.b2raw[0:E, 512 * h:512 * h + 512],
                       start=True, stop=True, skip_group_check=True)
            c = g.rsc[0:R]
            pe.wait_ge(sem("flag_set"), 1)
            mm(bank(7)[0:R, 1:2], g.before[0:R, 0:R], c[:, 2:3], start=True, stop=True).then_inc(sem("rank_done"), 1)
            pe.wait_ge(sem("ranked"), 1)
            mm(bank(7)[0:1, 16:32], c[:, 1:2], c[:, 16:32], start=True, stop=True)
            mm(bank(7)[0:1, 32:48], c[:, 3:4], c[:, 16:32], start=True, stop=True)
            mm(bank(7)[0:1, 48:49], c[:, 2:3], g.ones[0:R, 0:1], start=True, stop=True).then_inc(sem("list_done"), 1)
            pe.wait_ge(sem("over_set"), 1)

            def block_of(b):
                pe.wait_ge(sem("sel_set"), b + 1)
                for k in range(KD):
                    for i in range(NT):
                        ins = mm(bank(7)[:, k * CAP:(k + 1) * CAP], g.xn[:, i, k * P:(k + 1) * P], g.sel[:, i],
                                 start=(i == 0), stop=(i == NT - 1))
                ins.then_inc(sem("gathered"), 1)
                for i in range(NT):
                    ins = tr(bank(6)[0:CAP, i * P:(i + 1) * P], g.selg[:, i], ident)
                ins.then_inc(sem("selT_done"), 1)
                pe.wait_ge(sem("xg_set"), b + 1)
                for j in range(W1C):
                    pe.wait_ge(g.arrived[j], b * 16 + 16 * (before_moe[j] + 1))
                    w = cut(slots[j], k=KD)
                    for two in range(2):
                        for k in range(KD):
                            at = (4 * two + j % 4) * CAP
                            ins = mm(bank(4 + j // 4)[:, at:at + CAP], w[:, k, two:CW:2], g.xg[:, k],
                                     start=(k == 0), stop=(k == KD - 1))
                    ins.then_inc(sem("w_used"), 1)
                pe.wait_ge(sem("selT_set"), b + 1)
                pe.wait_ge(sem("act_set"), b * 2 + 2)
                for j in range(W2C):
                    pe.wait_ge(g.arrived[W1C + j], b * 16 + 16 * (before_moe[W1C + j] + 1))
                    w = cut(slots[W1C + j], k=KD)
                    for q in range(2):
                        for k in range(KD):
                            at = (2 * (j % 2) + q) * CAP
                            ins = mm(bank(6 + j // 2)[:, at:at + CAP], w[:, k, q * P:(q + 1) * P],
                                     g.actT[:, k], start=(k == 0), stop=(k == KD - 1))
                    ins.then_inc(sem("w_used"), 1)
                for h in range(2):
                    pe.wait_ge(sem("yT_set"), b * 2 + 1 + h)
                    for q in range(4):
                        turn = mm if q == 0 else tr
                        ins = turn(bank(6 + h)[0:CAP, q * P:(q + 1) * P], g.yeT[:, 4 * h + q], ident)
                    ins.then_inc(sem("y_turned"), 1)
                for h in range(2):
                    pe.wait_ge(sem("y_set"), b * 2 + h + 1)
                    for i in range(NT):
                        mm(bank(2 * i + h), g.selT[0:CAP, i * P:(i + 1) * P], g.ye[0:CAP, 512 * h:512 * h + 512],
                           start=False, stop=True, skip_group_check=True)

            with pe.Fori(0, E) as b:
                block_of(b)
            count = n_over(pe)
            with pe.If(count > 0):
                with pe.Fori(0, count) as r:
                    block_of(r + E)
            tr(bank(4)[:, 0:P], ident, ident).then_inc(sem("all_added"), 1)


NAMES = ["x", "mem", "ln1", "w_in", "token_mu", "rwkv_w0", "rwkv_w2", "rwkv_a0", "rwkv_a2", "rwkv_g2", "rwkv_k_k",
         "rwkv_k_a", "rwkv_r_k", "rwkv_ln_w", "rwkv_ln_b", "dil_q_norm", "dil_k_norm", "ln_mem", "w_mem_kv",
         "mem_q_norm", "mem_k_norm", "p_rwkv", "p_dil", "p_mem", "w_out", "ln2", "w_router", "b_router", "w1",
         "b1", "w2", "b2"]


def kernel(**inputs):
    import concourse.bacc as bacc
    from concourse.bass_utils import run_bass_kernel_spmd

    nc = bacc.Bacc("TRN2", target_bir_lowering=False, num_devices=1)
    arrays = {n: np.ascontiguousarray(inputs[n]) for n in NAMES}
    a = {n: nc.dram_tensor(n, v.shape, F32, kind="ExternalInput").ap() for n, v in arrays.items()}
    out = nc.dram_tensor("out", (1, SEQ, D), F32, kind="ExternalOutput").ap()
    build(nc, a, out)
    return run_bass_kernel_spmd(nc, [arrays], core_ids=[0]).results[0]["out"]
```

```python
from contextlib import ExitStack

import numpy as np

import concourse.bass as bass
from concourse import mybir

F32 = mybir.dt.float32
F32R = mybir.dt.float32r
BF16 = mybir.dt.bfloat16
ALU = mybir.AluOpType
ACT = mybir.ActivationFunctionType
AX = mybir.AxisListType.X

P = 128
D = 1024
SEQ = 256
NT = SEQ // P
KD = D // P
HD = 64
RH = 8
RT4 = RH * HD // P
L = 64
NCH = SEQ // L
LEVELS = 6
DH = 4
DG = 3
DIL = (1, 4, 16)
SPAN = 128
MH = 4
E = 32
TOPK = 4
FF = 1024
CAP = 64
NJ = SEQ // CAP
MAX_OVER = 15
NORM_EPS = 1e-5
GN_EPS = HD * 1e-5
NEG = -1e30
CW = 256
LO = 6
CHUNKS = 12
DEPTH = 4
W1C = 2 * FF // CW
W2C = D // CW

ROWS = {}
_at = 0
for _name, _n in (("ln1", 8), ("ln_mem", 8), ("ln2", 8), ("token_mu", 14), ("rwkv_w0", 4), ("rwkv_a0", 4),
                  ("rwkv_k_k", 4), ("rwkv_k_a", 4), ("rwkv_r_k", 4), ("rwkv_ln_w", 4), ("rwkv_ln_b", 4),
                  ("dil_q_norm", 1), ("dil_k_norm", 1), ("mem_q_norm", 1), ("mem_k_norm", 1)):
    ROWS[_name] = (_at, _n)
    _at += _n
NROWS = _at

C_RWKV, C_QK, C_V, C_MQ, C_MK, C_MV, C_GATE = 0, 7, 13, 16, 18, 20, 22
C_PMEM, C_PDIL, C_PRWKV, C_OUT, NMIX = 34, 36, 37, 39, 43
MIX = ((2, 0), (2, 4), (1, 0), (1, 4), (0, 0), (0, 4))
MIX_CHUNKS = ((C_PMEM, 4), (C_PMEM + 1, 4), (C_PDIL, 2), (C_PDIL, 2), (C_PRWKV, 4), (C_PRWKV + 1, 4))
FIRST = (-NMIX) % LO


UNITS = [(kind, h, i) for kind in ("mem", "dil") for h in range(4) for i in range(NT)]


def unit_keys(unit):
    return SEQ if unit[0] == "mem" else DG * P * (unit[2] + 1)


NORM_GROUPS = (("qk", 0, ("dil_q_norm", "dil_q_norm")), ("qk", 4, ("dil_q_norm", "dil_k_norm")),
               ("qk", 8, ("dil_k_norm", "dil_k_norm")), ("mq", 0, ("mem_q_norm", "mem_q_norm")),
               ("mk", 0, ("mem_k_norm", "mem_k_norm")))


KEPT = 12288 + 2048 + 2048 + 256 + 1024 + NROWS + 8 + 64
MIXER = 35400


class Own:

    def __init__(self, engine, sem, base=0):
        self.engine, self.sem, self.base, self.n = engine, sem, base, 0

    def __call__(self, instruction):
        instruction.then_inc(self.sem, 1)
        self.n += 1

    def wait(self):
        self.engine.wait_ge(self.sem, self.base + self.n)

    def link(self, instruction):
        self(instruction)
        self.wait()


class Layout:
    pass


def build(nc, a, out, part=None):
    g = Layout()
    with ExitStack() as ctx:
        g.sems = {}

        def sem(name):
            if name not in g.sems:
                g.sems[name] = ctx.enter_context(nc.semaphore(name))
            return g.sems[name]

        def psb(name):
            return ctx.enter_context(nc.psum_tensor(name, [P, 8 * 512], F32))

        g.ps = psb("banks")

        def bank(b, n=1):
            return g.ps[:, b * 512:(b + n) * 512]

        arena = ctx.enter_context(nc.sbuf_tensor("arena", [P, KEPT], F32))
        top = [0]

        def place(n):
            top[0] += n
            assert top[0] <= arena.shape[1], top[0]
            return arena[:, top[0] - n:top[0]]

        def cut(ap, **dims):
            names = list(dims)
            return ap.rearrange(f"p ({' '.join(names)} n) -> p {' '.join(names)} n", **dims)

        g.ring_lo = cut(place(LO * 2048), s=LO)
        g.x = cut(place(NT * D), i=NT)
        g.hT = cut(place(KD * SEQ), k=KD)
        g.ident, g.ones = place(P), place(P)
        g.ln2_row = place(D)
        g.cols = place(NROWS + 8)
        g.eps_norm = g.cols[:, NROWS:NROWS + 1]
        g.eps_gn = g.cols[:, NROWS + 1:NROWS + 2]
        g.stat = place(64)

        def param(name):
            at, n = ROWS[name]
            return g.cols[:, at:at + n]

        def ring(n):
            return g.ring_lo[:, (FIRST + n) % LO]

        g.arrived = [sem(f"slot{s}_arrived") for s in range(LO)]

        def nth(n):
            return (FIRST + n) // LO + (1 if (FIRST + n) % LO >= FIRST else 0)

        g.lo_loads = [nth(NMIX - LO + s) for s in range(LO)]

        w_in, w_kv = a["w_in"][0], a["w_mem_kv"][0]

        def columns(w, at, n=CW):
            return w[:, at:at + n].rearrange("(k p) n -> p k n", p=P)

        def chunk_source(n):
            if n < C_MK:
                return columns(w_in, n * CW)
            if n < C_GATE:
                return columns(w_kv, (n - C_MK) * CW)
            if n < C_PMEM:
                return columns(w_in, (n - C_GATE) * CW + C_MK * CW)
            if n < C_PDIL:
                return columns(a["p_mem"][0], (n - C_PMEM) * 512, 512)
            if n < C_PRWKV:
                return columns(a["p_dil"][0], 0, 1024)
            if n < C_OUT:
                return columns(a["p_rwkv"][0], (n - C_PRWKV) * 512, 512)
            return columns(a["w_out"][0], (n - C_OUT) * CW)

        g.sem, g.bank, g.cut, g.param, g.ring, g.nth, g.chunk_source = sem, bank, cut, param, ring, nth, chunk_source
        g.part = part
        if part != "moe":
            with ExitStack() as own:
                mixer_memory(nc, own, g)
                mixer(nc, a, g)
        if part == "mixer":
            with nc.Block() as block:
                @block.sync
                def _(sp):
                    sp.dma_start(out[0].rearrange("(i p) n -> p i n", p=P), g.x).then_inc(sem("stored"), 16)
                    sp.wait_ge(sem("stored"), 16)
        else:
            with ExitStack() as own:
                moe_memory(nc, own, g)
                moe(nc, a, out, g)


def mixer_memory(nc, ctx, g):
    arena = ctx.enter_context(nc.sbuf_tensor("mixer_arena", [P, MIXER], F32))
    top, cut = [0], g.cut

    def place(n):
        top[0] += n
        assert top[0] <= arena.shape[1], top[0]
        return arena[:, top[0] - n:top[0]]

    g.mask_s, g.mask_l, g.mask_i, g.head_ones = (place(P) for _ in range(4))
    g.amask = cut(place(3 * SEQ), g=3)
    region = top[0]
    g.Zraw = cut(place(14 * 257), k=14)
    g.qk = cut(place(12 * SEQ), k=12)
    g.vtok = cut(place(NT * 768), i=NT)
    g.mq = cut(place(4 * SEQ), k=4)
    g.mk = cut(place(4 * SEQ), k=4)
    g.mv = cut(place(NT * 512), i=NT)
    g.sc2 = cut(place(2 * 768), u=2)
    g.pt2 = cut(place(2 * 768), u=2)
    end_attention = top[0]
    top[0] = region
    g.tokm = cut(place(4 * NT * 512), q=4)
    g.tok_a, g.tok_b, g.tok_k, g.tok_v = (cut(g.tokm[:, q], i=NT) for q in range(4))
    g.WT = cut(place(4 * SEQ), k=4)
    g.Zt = cut(place(NT * 512), i=NT)
    g.mrb = cut(place(16 * P), q=16)
    g.Y0 = cut(place(4 * SEQ), k=4)
    g.S_hist = cut(place((NCH + 1) * 256), c=NCH + 1)
    g.qxn4 = place(4 * 256).rearrange("p (u q j n) -> p u q j n", u=2, q=2, j=2)
    g.xx4 = place(4 * P).rearrange("p (u q n) -> p u q n", u=2, q=2)
    g.ak4 = place(4 * P).rearrange("p (u q n) -> p u q n", u=2, q=2)
    g.rk4 = place(4 * P).rearrange("p (u q n) -> p u q n", u=2, q=2)
    g.mv2 = place(4 * HD).rearrange("p (u q n) -> p u q n", u=2, q=2)
    g.U = cut(place(NT * 512), i=NT)
    top[0] = max(top[0], end_attention)
    g.gates = cut(place(24 * SEQ), k=24)
    g.rT, g.kT, g.aT, g.kkT, g.vT, g.gT, g.dec = (cut(place(4 * SEQ), k=4) for _ in range(7))
    g.lora = cut(place(2 * SEQ), k=2)
    g.tmp = cut(place(4 * SEQ), k=4)
    g.zs = g.Zraw.rearrange("p k n -> p (k n)")
    g.t1, g.t2, g.t3 = (cut(g.zs[:, q * 1024:(q + 1) * 1024], k=4) for q in range(3))
    g.p_last = place(4 * NCH).rearrange("p (k c) -> p k c", k=4)
    g.lw2 = place(512)
    g.lg2 = place(512)
    g.yT = cut(place(10 * SEQ), k=10)
    g.y_rwkv, g.y_dil, g.y_mem = g.yT[:, 0:4], g.yT[:, 4:6], g.yT[:, 6:10]
    gflat = g.gates.rearrange("p k n -> p (k n)")
    g.memx = cut(gflat[:, 0:NT * D], i=NT)
    g.memT = cut(gflat[:, NT * D:2 * NT * D], k=KD)
    g.sq = gflat[:, 4096:5120]
    g.prow = gflat[0:NROWS, 5120:5248]


def mixer(nc, a, g):
    sem, bank, cut, param = g.sem, g.bank, g.cut, g.param
    x, hT, ident, cols = g.x, g.hT, g.ident, g.cols

    with nc.Block() as block:
        @block.sync
        def _(sp):
            def wait_used(n):
                if n < C_PMEM:
                    sp.wait_ge(sem("proj_done"), n + 1)
                elif n < C_OUT:
                    last = max(q for q in range(len(MIX)) if MIX_CHUNKS[q][0] == n)
                    sp.wait_ge(sem("mix_done"), last + 1)
                else:
                    sp.wait_ge(sem("out_done"), n - C_OUT + 1)

            sp.dma_start(x, a["x"][0].rearrange("(i p) n -> p i n", p=P)).then_inc(sem("x_in"), 16)
            sp.dma_start(g.memx, a["mem"][0].rearrange("(i p) n -> p i n", p=P)).then_inc(sem("mem_in"), 16)
            for n in range(NMIX):
                if n >= LO:
                    wait_used(n - LO)
                src = g.chunk_source(n)
                dst = cut(g.ring(n), k=src.shape[1])
                sp.dma_start(dst, src).then_inc(g.arrived[(FIRST + n) % LO], 16)
            for s in range(LO):
                wait_used(NMIX - LO + s)
                sp.dma_start(cut(g.ring_lo[:, s], k=KD), a["w1"][0, 0][:, s * CW:(s + 1) * CW]
                             .rearrange("(k p) n -> p k n", p=P)).then_inc(g.arrived[s], 16)

        @block.gpsimd
        def _(pool):
            own = Own(pool, sem("pool_steps"))
            own.link(nc.gpsimd.memset(ident, 0.0))
            nc.gpsimd.affine_select(out=ident, in_=ident, compare_op=ALU.not_equal, fill=1.0, base=0,
                                    pattern=[[-1, P]], channel_multiplier=1).then_inc(sem("ident_set"), 1)
            for name, (at, n) in ROWS.items():
                src = a[name][0]
                if name == "rwkv_r_k":
                    src = src.rearrange("h d -> (h d)")
                if name.startswith("dil"):
                    for half in range(2):
                        pool.dma_start(g.prow[at:at + 1, half * HD:(half + 1) * HD],
                                       src.rearrange("(a n) -> a n", a=1)).then_inc(sem("rows_in"), 16)
                else:
                    pool.dma_start(g.prow[at:at + n, :], src.rearrange("(a n) -> a n", a=n)) \
                        .then_inc(sem("rows_in"), 16)
            pool.dma_start(g.ln2_row, a["ln2"].broadcast_to([P, D])).then_inc(sem("ln2_in"), 16)
            pool.dma_start(g.lw2[0:64, :], a["rwkv_w2"][0]).then_inc(sem("lora_in"), 16)
            pool.dma_start(g.lw2[64:128, :], a["rwkv_a2"][0]).then_inc(sem("lora_in"), 16)
            pool.dma_start(g.lg2[:, :], a["rwkv_g2"][0]).then_inc(sem("lora_in"), 16)
            own.link(nc.gpsimd.memset(g.ones, 1.0))
            own.link(nc.gpsimd.memset(g.eps_norm, NORM_EPS))
            own.link(nc.gpsimd.memset(g.eps_gn, GN_EPS))
            own.link(nc.gpsimd.memset(g.head_ones, 0.0))
            own.link(nc.gpsimd.memset(g.head_ones[0:64, 0:64], 1.0))
            own.link(nc.gpsimd.memset(g.head_ones[64:128, 64:128], 1.0))
            own.link(nc.gpsimd.memset(g.mask_s, 0.0))
            own.link(nc.gpsimd.memset(g.mask_l, 0.0))
            own.link(nc.gpsimd.memset(g.mask_i, 0.0))
            for q in range(2):
                r = slice(q * L, (q + 1) * L)
                for msk in (g.mask_s, g.mask_l, g.mask_i):
                    own.link(nc.gpsimd.memset(msk[r, r], 1.0))
            own.link(nc.gpsimd.memset(g.amask, 0.0))
            for msk, op, sign in ((g.mask_s, ALU.is_gt, 1), (g.mask_l, ALU.is_gt, -1), (g.mask_i, ALU.is_ge, 1)):
                own.link(nc.gpsimd.affine_select(out=msk, in_=msk, compare_op=op, fill=0.0, base=0,
                                        pattern=[[sign, P]], channel_multiplier=-sign))
            own.link(nc.gpsimd.affine_select(out=g.amask, in_=g.amask, compare_op=ALU.is_ge, fill=NEG, base=P,
                                             pattern=[[0, 3], [-1, SEQ]], channel_multiplier=1))
            own.link(nc.gpsimd.affine_select(out=g.amask[:, 0], in_=g.amask[:, 0], compare_op=ALU.is_ge, fill=NEG,
                                    base=SPAN - P, pattern=[[1, SEQ]], channel_multiplier=-1))
            ti = g.pt2.rearrange("p u n -> p (u n)")[:, 0:SEQ].bitcast(mybir.dt.int32)
            own.link(nc.gpsimd.iota(ti, pattern=[[-1, SEQ]], base=P, channel_multiplier=1))
            nc.gpsimd.memset(g.stat, 0.0).then_inc(sem("consts_set"), 1)

        @block.vector
        def _(dve):
            own = Own(dve, sem("dve_steps"))
            tt, ts, stt = nc.vector.tensor_tensor, nc.vector.tensor_scalar, nc.vector.scalar_tensor_tensor

            def bc(v, n):
                return v.unsqueeze(2).broadcast_to([P, v.shape[1], n])

            dve.wait_ge(sem("consts_set"), 1)
            ti = g.pt2.rearrange("p u n -> p (u n)")[:, 0:SEQ].bitcast(mybir.dt.int32)
            tr = g.pt2.rearrange("p u n -> p (u n)")[:, 256:512].bitcast(mybir.dt.int32)
            neg = g.pt2.rearrange("p u n -> p (u n)")[:, 512:768]
            own.link(ts(neg, ti, 0, NEG, ALU.is_lt, ALU.mult))
            for q in (1, 2):
                own.link(ts(tr, ti, DIL[q] - 1, None, ALU.bitwise_and))
                own.link(ts(g.amask[:, q], tr, 0, NEG, ALU.is_gt, ALU.mult))
                own.link(tt(g.amask[:, q], g.amask[:, q], neg, ALU.min))

            for k, (name, src) in enumerate((("mem", g.memx), ("x", x))):
                dve.wait_ge(sem("root_set"), k + 1)
                own.link(nc.vector.reciprocal(g.stat[:, 8 + 2 * k:10 + 2 * k], g.stat[:, 4 + 2 * k:6 + 2 * k]))
                for i in range(NT):
                    dst = src[:, i] if k == 0 else g.zs[:, i * D:(i + 1) * D]
                    nc.vector.tensor_scalar(dst, src[:, i], g.stat[:, 8 + 2 * k + i:9 + 2 * k + i], None, ALU.mult) \
                        .then_inc(sem("normed"), 1)
            dve.wait_ge(sem("cols_set"), 1)
            for k, (dst, gain) in enumerate(((g.memT, "ln_mem"), (hT, "ln1"))):
                for q in range(4):
                    n = 4 * k + q
                    dve.wait_ge(sem("turned"), n + 1)
                    tt(dst[:, 2 * q:2 * q + 2], cut(bank(n % 2), k=2), bc(param(gain)[:, 2 * q:2 * q + 2], SEQ),
                       ALU.mult).then_inc(sem("turned_out"), 1)

            mu = param("token_mu")
            for q, (dst, first, n) in enumerate(((g.rT, 0, 4), (g.kT, 4, 4), (g.vT, 8, 4), (g.lora, 12, 2))):
                dve.wait_ge(sem("z_out"), first // 2 + (n + 1) // 2)
                z, zp = g.Zraw[:, first:first + n, 1:257], g.Zraw[:, first:first + n, 0:256]
                d = g.tmp[:, 0:n]
                own.link(tt(d, zp, z, ALU.subtract))
                own.link(tt(d, d, bc(mu[:, first:first + n], SEQ), ALU.mult))
                tt(dst, d, z, ALU.add).then_inc(sem("shifted"), 1)
                dve.wait_ge(sem("shifted"), q + 1)
            dve.wait_ge(sem("shifted"), 4)
            own.link(tt(g.kkT, g.kT, bc(param("rwkv_k_k"), SEQ), ALU.mult))
            tt(g.t1, g.kkT, g.kkT, ALU.mult).then_inc(sem("kk_squared"), 1)
            for q in range(2):
                dve.wait_ge(sem("kk_summed"), q + 1)
                ts(g.t1[:, 2 * q:2 * q + 2], cut(bank(6 + q), k=2), 1e-24, None, ALU.max) \
                    .then_inc(sem("kk_sum_out"), 1)
            dve.wait_ge(sem("kk_root"), 1)
            own.link(nc.vector.reciprocal(g.t1, g.t1))
            own.link(tt(g.kkT, g.kkT, g.t1, ALU.mult))
            dve.wait_ge(sem("a_set"), 1)
            own.link(ts(g.t2, g.aT, -1.0, None, ALU.add))
            own.link(tt(g.t2, g.t2, bc(param("rwkv_k_a"), SEQ), ALU.mult))
            own.link(stt(g.kT, g.t2, 1.0, g.kT, ALU.add, ALU.mult))
            own.link(tt(g.t2, g.rT, g.kT, ALU.mult))
            tt(g.t2, g.t2, bc(param("rwkv_r_k"), SEQ), ALU.mult).then_inc(sem("rk_set"), 1)
            own.link(tt(g.aT, g.aT, g.kkT, ALU.mult))
            dve.wait_ge(sem("decay_set"), 1)
            nc.vector.memset(g.t3, 0.0)
            fl = lambda v: v.rearrange("p k n -> p (k n)")
            ch = lambda v: v.rearrange("p k (c t) -> p (k c) t", t=L)
            own.link(nc.vector.memset(g.t1, 0.0))
            own.link(nc.vector.tensor_copy(ch(g.t3)[:, :, 0:1], ch(g.tmp)[:, :, 0:1]))
            own.link(nc.vector.memset(ch(g.tmp)[:, :, 0:1], 0.0))
            own.link(nc.vector.tensor_tensor_scan(fl(g.dec), fl(g.tmp), fl(g.t3), 0.0, ALU.mult, ALU.add))
            own.link(nc.vector.tensor_copy(g.p_last.rearrange("p k c -> p (k c)").unsqueeze(2),
                                           ch(g.dec)[:, :, L - 1:L]))
            nc.vector.tensor_scalar(ch(g.t1)[:, :, 0:1], ch(g.kkT)[:, :, 0:1], -1.0, None, ALU.mult)
            own.link(stt(ch(g.t1)[:, :, 1:L], ch(g.kkT)[:, :, 1:L], -1.0, ch(g.dec)[:, :, 0:L - 1],
                         ALU.mult, ALU.mult))
            nc.vector.tensor_copy(g.kkT, g.t1)
            own.link(tt(g.rT, g.rT, g.dec, ALU.mult))
            own.link(nc.vector.reciprocal(g.dec, g.dec))
            tt(g.kT, g.kT, g.dec, ALU.mult)
            tt(g.aT, g.aT, g.dec, ALU.mult).then_inc(sem("tildes_set"), 1)
            dve.wait_ge(sem("tildes_set"), 1)
            for q in range(2):
                dve.wait_ge(sem("rk_summed"), q + 1)
                own.link(tt(g.dec[:, 2 * q:2 * q + 2], cut(bank(6 + q), k=2), g.vT[:, 2 * q:2 * q + 2], ALU.mult))
            for q, (buf, k0, gain) in enumerate(NORM_GROUPS):
                t = {"qk": g.qk, "mq": g.mq, "mk": g.mk}[buf][:, k0:k0 + 4]
                dve.wait_ge(sem("dil_out"), C_GATE - C_QK)
                if q:
                    dve.wait_ge(sem("qk_summed"), q)
                tt(g.t1, t, t, ALU.mult).then_inc(sem("squared"), 1)
                dve.wait_ge(sem("qk_root"), q + 1)
                own.link(nc.vector.reciprocal(g.t2, g.t2))
                for h in range(2):
                    c = slice(2 * h, 2 * h + 2)
                    ins = stt(t[:, c], t[:, c], param(gain[h]), g.t2[:, c], ALU.mult, ALU.mult)
                ins.then_inc(sem("qk_normed"), 1)
            def attention_out(u):
                kind, h, i = UNITS[u]
                dve.wait_ge(sem("pv_done"), u + 1)
                if kind == "mem":
                    dst, src = g.y_mem[:, h, i * P:(i + 1) * P], bank(u % 2)[:, 0:P]
                else:
                    r = slice(64 * (h % 2), 64 * (h % 2) + 64)
                    dst, src = g.y_dil[r, h // 2, i * P:(i + 1) * P], bank(u % 2)[r, 0:P]
                nc.vector.tensor_copy(dst, src).then_inc(sem("attended"), 1)

            for u, unit in enumerate(UNITS):
                n = unit_keys(unit)
                sc = g.sc2[:, u % 2, 0:n]
                pb = 2 + 2 * (u % 2)
                dve.wait_ge(sem("scored"), u + 1)
                if u >= 2:
                    dve.wait_ge(sem("probs_turned"), u - 1)
                if unit[0] == "mem":
                    own.link(nc.vector.tensor_copy(sc, bank(pb, 2)[:, 0:n]))
                    scale = float(P) ** -0.5
                else:
                    w = n // 3
                    own.link(tt(cut(sc, g=3), bank(pb, 2)[:, 0:3 * SEQ].rearrange("p (g n) -> p g n", g=3)[:, :, 0:w],
                                g.amask[:, :, SEQ - w:SEQ], ALU.add))
                    scale = float(HD) ** -0.5
                s = g.stat[:, 16 + 4 * (u % 2):20 + 4 * (u % 2)]
                own.link(nc.vector.tensor_reduce(out=s[:, 0:1], in_=sc, axis=AX, op=ALU.max))
                ts(s[:, 1:2], s[:, 0:1], -scale, None, ALU.mult).then_inc(sem("max_set"), 1)
                dve.wait_ge(sem("exp_set"), u + 1)
                own.link(nc.vector.reciprocal(s[:, 3:4], s[:, 2:3]))
                ts(sc, sc, s[:, 3:4], None, ALU.mult).then_inc(sem("probs_set"), 1)
                if u:
                    attention_out(u - 1)
            attention_out(len(UNITS) - 1)

            nc.vector.memset(g.S_hist[:, 0], 0.0)
            for r in range(4):
                for u in (2 * r, 2 * r + 1):
                    e, i, hp = u % 2, u // 4, u % 4
                    b = 2 + 3 * e
                    dve.wait_ge(sem("grams_done"), u + 1)
                    if r == 0 and e == 0:
                        dve.wait_ge(sem("tok_out"), 8)
                    w = bank(b).rearrange("p (q j n) -> p q j n", q=2, j=2)
                    v = bank(b + 2).rearrange("p (q n) -> p q n", q=2)
                    qxn = g.qxn4[:, e]
                    m2 = lambda k: k.unsqueeze(1).broadcast_to([P, 2, P])
                    pr = 8 * i + 2 * hp
                    own.link(tt(qxn[:, :, 0], w[:, :, 0], m2(g.mask_s), ALU.mult))
                    tt(qxn[:, :, 1], w[:, :, 1], m2(g.mask_l), ALU.mult)
                    tt(g.mrb[:, pr:pr + 2], bank(b + 1)[:, 0:2 * P].rearrange("p (q n) -> p q n", q=2),
                       m2(g.mask_i), ALU.mult)
                    tt(g.xx4[:, e], qxn[:, :, 0], m2(ident), ALU.add)
                    tt(g.ak4[:, e], v[:, :, 0:P], m2(g.mask_s), ALU.mult)
                    tt(g.rk4[:, e], v[:, :, P:2 * P], m2(g.mask_i), ALU.mult).then_inc(sem("grams_out"), 1)
                for lv in range(1, LEVELS):
                    for u in (2 * r, 2 * r + 1):
                        e = u % 2
                        dve.wait_ge(sem("level_done"), 2 * LEVELS * r + 2 * lv + e + 1)
                        tt(g.xx4[:, e], g.xx4[:, e], bank(3 + 3 * e)[:, 0:2 * P].rearrange("p (q n) -> p q n", q=2),
                           ALU.add) \
                            .then_inc(sem("x_updated"), 1)
                for u in (2 * r, 2 * r + 1):
                    e, i, hp = u % 2, u // 4, u % 4
                    o = bank(4 + 3 * e)
                    dve.wait_ge(sem("mv_done"), u + 1)
                    nc.vector.tensor_copy(g.mv2[:, e], o[:, 0:P].rearrange("p (q n) -> p q n", q=2)) \
                        .then_inc(sem("mv_out"), 1)
                    dve.wait_ge(sem("wz_done"), u + 1)
                    nc.vector.tensor_copy(g.Zt[:, i, hp * P:(hp + 1) * P], o[:, P:2 * P])
                    nc.vector.tensor_copy(g.WT[:, hp, i * P:(i + 1) * P], o[:, 2 * P:3 * P])
                    nc.vector.tensor_copy(g.Y0[:, hp, i * P:(i + 1) * P], o[:, 3 * P:4 * P]) \
                        .then_inc(sem("wz_out"), 1)
            for c in range(NCH):
                i, cb = c // 2, L * (c % 2)
                if c == 0:
                    dve.wait_ge(sem("wz_out"), 8)
                    nc.vector.tensor_copy(g.U[0:L, 0], g.Zt[0:L, 0]).then_inc(sem("u_set"), 1)
                else:
                    dve.wait_ge(sem("u_done"), c)
                    tt(g.U[cb:cb + L, i], bank(2)[cb:cb + L, :], g.Zt[cb:cb + L, i], ALU.add) \
                        .then_inc(sem("u_set"), 1)
                if c == NCH - 1:
                    break
                dve.wait_ge(sem("s_done"), c + 1)
                s1 = g.S_hist[:, c + 1].rearrange("p (k n) -> p k n", k=4)
                own.link(tt(g.S_hist[:, c + 1], bank(3)[:, 0:256], g.S_hist[:, c], ALU.add))
                tt(s1, s1, g.p_last[:, :, c:c + 1].broadcast_to([P, 4, HD]), ALU.mult) \
                    .then_inc(sem("s_set"), 1)
                dve.wait_ge(sem("s_set"), c + 1)
            Y = g.Y0
            for i in range(NT):
                dve.wait_ge(sem("y_done"), i + 1)
                own.link(tt(Y[:, :, i * P:(i + 1) * P], Y[:, :, i * P:(i + 1) * P],
                            bank(4 + i).rearrange("p (k n) -> p k n", k=4), ALU.add))
            dve.wait_ge(sem("dve_steps"), own.n)
            nc.vector.tensor_copy(g.y_rwkv, Y).then_inc(sem("y_summand"), 1)
            for q in range(2):
                dve.wait_ge(sem("y_summed"), q + 1)
                own.link(stt(g.y_rwkv[:, 2 * q:2 * q + 2], cut(bank(6 + q), k=2), -1.0 / HD,
                             Y[:, 2 * q:2 * q + 2], ALU.mult, ALU.add))
            tt(g.rT, g.y_rwkv, g.y_rwkv, ALU.mult).then_inc(sem("y_squared"), 1)
            dve.wait_ge(sem("y_root"), 1)
            own.link(nc.vector.reciprocal(g.kT, g.kT))
            own.link(tt(g.y_rwkv, g.y_rwkv, g.kT, ALU.mult))
            own.link(tt(g.y_rwkv, g.y_rwkv, bc(param("rwkv_ln_w"), SEQ), ALU.mult))
            own.link(tt(g.y_rwkv, g.y_rwkv, bc(param("rwkv_ln_b"), SEQ), ALU.add))
            own.link(tt(g.y_rwkv, g.y_rwkv, g.dec, ALU.add))
            tt(g.y_rwkv, g.y_rwkv, g.gT, ALU.mult).then_inc(sem("y_rwkv_set"), 1)

            for q, (gb, first) in enumerate(MIX):
                b = 2 + 2 * (q % 2)
                t = (g.rT, g.kT)[q % 2]
                dve.wait_ge(sem("mix_done"), q + 1)
                dve.wait_ge(sem("gates_out"), 12)
                dst = hT[:, first:first + 4]
                w = cut(bank(b, 2), k=4)
                if gb == 2:
                    tt(dst, w, g.gates[:, 8 * gb + first:8 * gb + first + 4], ALU.mult) \
                        .then_inc(sem("mix_out"), 1)
                else:
                    tt(t, w, g.gates[:, 8 * gb + first:8 * gb + first + 4], ALU.mult).then_inc(sem("mix_out"), 1)
                    dve.wait_ge(sem("mix_out"), q + 1)
                    tt(dst, dst, t, ALU.add).then_inc(sem("mixed"), 1)
            for q in range(4):
                dve.wait_ge(sem("out_done"), q + 1)
                tt(x[:, :, q * CW:(q + 1) * CW], x[:, :, q * CW:(q + 1) * CW],
                   bank(q % 2).rearrange("p (i n) -> p i n", i=2), ALU.add).then_inc(sem("x2_set"), 1)

        @block.scalar
        def _(act):
            own = Own(act, sem("act_steps"))
            act.wait_ge(sem("consts_set"), 1)
            for k, (name, src) in enumerate((("mem", g.memx), ("x", x))):
                act.wait_ge(sem(name + "_in"), 16)
                for i in range(NT):
                    own.link(nc.scalar.activation(g.sq, src[:, i], ACT.Square,
                                                  accum_out=g.stat[:, 2 * k + i:2 * k + i + 1]))
                nc.scalar.activation(g.stat[:, 4 + 2 * k:6 + 2 * k], g.stat[:, 2 * k:2 * k + 2], ACT.Sqrt,
                                     bias=g.eps_norm, scale=1.0 / D).then_inc(sem("root_set"), 1)
            act.wait_ge(sem("cols_turned"), 1)
            nc.scalar.activation(cols[:, 0:NROWS], bank(7)[:, 0:NROWS], ACT.Copy).then_inc(sem("cols_set"), 1)
            act.wait_ge(sem("normed"), 4)
            act.wait_ge(sem("turned"), 8)
            zero = g.stat[:, 63:64].unsqueeze(2).broadcast_to([P, 14, 1])
            own.link(nc.scalar.activation(g.Zraw[:, :, 0:1], zero, ACT.Copy))

            def evacuate(n, dst, func=ACT.Copy):
                act.wait_ge(sem("proj_done"), n + 1)
                w = bank(n % 2).rearrange("p (q n) -> p q n", q=2)
                return nc.scalar.activation(dst, w, func)

            for n in range(C_QK):
                evacuate(n, g.Zraw[:, 2 * n:2 * n + 2, 1:257]).then_inc(sem("z_out"), 1)
            act.wait_ge(sem("shifted"), 4)
            nc.scalar.activation(g.lora[0:64, 0], g.lora[0:64, 0], ACT.Tanh)
            nc.scalar.activation(g.lora[:, 1], g.lora[:, 1], ACT.Sigmoid).then_inc(sem("lora_set"), 1)
            for n in range(C_QK, C_QK + 2):
                evacuate(n, g.qk[:, 2 * (n - C_QK):2 * (n - C_QK) + 2]).then_inc(sem("dil_out"), 1)
            act.wait_ge(sem("lora_done"), 1)
            for k in range(4):
                own.link(nc.scalar.activation(g.tmp[:, k], bank(2, 2)[:, k * SEQ:(k + 1) * SEQ], ACT.Sigmoid,
                                              bias=param("rwkv_w0")[:, k:k + 1]))
            for k in range(4):
                ins = nc.scalar.activation(g.aT[:, k], bank(4, 2)[:, k * SEQ:(k + 1) * SEQ], ACT.Sigmoid,
                                           bias=param("rwkv_a0")[:, k:k + 1])
            ins.then_inc(sem("a_set"), 1)
            nc.scalar.activation(g.gT, cut(bank(6, 2), k=4), ACT.Copy).then_inc(sem("g_out"), 1)
            nc.scalar.activation(g.tmp, g.tmp, ACT.Exp, scale=-float(np.exp(-0.5))).then_inc(sem("decay_set"), 1)
            act.wait_ge(sem("kk_sum_out"), 2)
            nc.scalar.activation(g.t1, g.t1, ACT.Sqrt).then_inc(sem("kk_root"), 1)
            for n in range(C_QK + 2, C_GATE):
                if n < C_V:
                    ins = evacuate(n, g.qk[:, 2 * (n - C_QK):2 * (n - C_QK) + 2])
                elif n < C_MQ:
                    ins = evacuate(n, g.vtok[:, :, (n - C_V) * CW:(n - C_V + 1) * CW])
                elif n < C_MK:
                    ins = evacuate(n, g.mq[:, 2 * (n - C_MQ):2 * (n - C_MQ) + 2])
                elif n < C_MV:
                    ins = evacuate(n, g.mk[:, 2 * (n - C_MK):2 * (n - C_MK) + 2])
                else:
                    ins = evacuate(n, g.mv[:, :, (n - C_MV) * CW:(n - C_MV + 1) * CW])
                ins.then_inc(sem("dil_out"), 1)
            for q, (buf, k0, gain) in enumerate(NORM_GROUPS):
                width = HD if buf == "qk" else P
                act.wait_ge(sem("qk_summed"), q + 1)
                nc.scalar.activation(g.t2, cut(bank(2 + 2 * (q % 2), 2), k=4), ACT.Sqrt, bias=g.eps_norm,
                                     scale=1.0 / width).then_inc(sem("qk_root"), 1)
                act.wait_ge(sem("qk_normed"), q + 1)

            for u, unit in enumerate(UNITS):
                n = unit_keys(unit)
                sc = g.sc2[:, u % 2, 0:n]
                s = g.stat[:, 16 + 4 * (u % 2):20 + 4 * (u % 2)]
                scale = float(P if unit[0] == "mem" else HD) ** -0.5
                act.wait_ge(sem("max_set"), u + 1)
                nc.scalar.activation(sc, sc, ACT.Exp, bias=s[:, 1:2], scale=scale, accum_out=s[:, 2:3]) \
                    .then_inc(sem("exp_set"), 1)
                act.wait_ge(sem("probs_turned"), u + 1)
                if u >= 2:
                    act.wait_ge(sem("pv_done"), u - 1)
                nc.scalar.activation(g.pt2[:, u % 2, 0:n], bank(6, 2)[:, 0:n], ACT.Copy) \
                    .then_inc(sem("pt_set"), 1)
            for q in range(4):
                for i in range(NT):
                    n = 2 * q + i
                    act.wait_ge(sem("tok_turned"), n + 1)
                    act.wait_ge(sem("attended"), len(UNITS))
                    nc.scalar.activation((g.tok_a, g.tok_b, g.tok_k, g.tok_v)[q][:, i], bank(2 + n % 2), ACT.Copy) \
                        .then_inc(sem("tok_out"), 1)

            def gate_out(n):
                evacuate(C_GATE + n, g.gates[:, 2 * n:2 * n + 2], ACT.Sigmoid).then_inc(sem("gates_out"), 1)

            for r in range(4):
                for lv in range(LEVELS - 1):
                    for u in (2 * r, 2 * r + 1):
                        e = u % 2
                        act.wait_ge(sem("level_done"), 2 * LEVELS * r + 2 * lv + e + 1)
                        nc.scalar.activation(g.qxn4[:, e].rearrange("p q j n -> p (q j n)"), bank(2 + 3 * e), ACT.Copy) \
                            .then_inc(sem("q_updated"), 1)
                    if lv % 2 == 1:
                        if 2 * r + lv // 2 < 8:
                            gate_out(2 * r + lv // 2)
            for n in range(8, 12):
                gate_out(n)
            act.wait_ge(sem("var_done"), 1)
            nc.scalar.activation(g.kT, cut(bank(2, 2), k=4), ACT.Sqrt, bias=g.eps_gn, scale=1.0 / HD) \
                .then_inc(sem("y_root"), 1)

        @block.tensor
        def _(pe):
            mm, tr = nc.tensor.matmul, nc.tensor.transpose

            turns = [0]

            def row_tile_done(instruction):
                turns[0] += 1
                instruction.then_inc(sem("row_tile_done"), 1)
                pe.wait_ge(sem("row_tile_done"), turns[0])

            def load_wait(n):
                pe.wait_ge(g.arrived[(FIRST + n) % LO], 16 * g.nth(n))

            pe.wait_ge(sem("ident_set"), 1)
            pe.wait_ge(sem("rows_in"), 16 * (len(ROWS) + 2))
            tr(bank(7)[:, 0:NROWS], g.prow, ident[0:NROWS, 0:NROWS]).then_inc(sem("cols_turned"), 1)
            for k, src in enumerate((g.memx, None)):
                for q in range(4):
                    n = 4 * k + q
                    if n >= 2:
                        pe.wait_ge(sem("turned_out"), n - 1)
                    for kk in range(2):
                        for i in range(NT):
                            if q == 0 and kk == 0:
                                pe.wait_ge(sem("normed"), 2 * k + i + 1)
                            row = src[:, i] if k == 0 else g.zs[:, i * D:(i + 1) * D]
                            ins = tr(bank(n % 2)[:, kk * SEQ + i * P:kk * SEQ + (i + 1) * P],
                                     row[:, (2 * q + kk) * P:(2 * q + kk + 1) * P], ident)
                    ins.then_inc(sem("turned"), 1)
            pe.wait_ge(sem("turned_out"), 8)

            def project(n, src, token_major=False):
                load_wait(n)
                w = cut(g.ring(n), k=KD)
                if 2 <= n < C_QK:
                    pe.wait_ge(sem("z_out"), n - 1)
                elif C_QK <= n < C_QK + 2:
                    pe.wait_ge(sem("z_out"), n - 1)
                elif C_QK + 2 <= n < C_GATE + 2:
                    pe.wait_ge(sem("dil_out"), n - 1 - C_QK)
                elif n >= C_GATE + 2:
                    pe.wait_ge(sem("gates_out"), n - 1 - C_GATE)
                for q in range(2):
                    o = bank(n % 2)[:, q * SEQ:(q + 1) * SEQ]
                    for k in range(KD):
                        if token_major:
                            ins = mm(o, src[:, k, q * P:(q + 1) * P], w[:, k, :], start=(k == 0), stop=(k == KD - 1))
                        else:
                            ins = mm(o, w[:, k, q * P:(q + 1) * P], src[:, k, :], start=(k == 0), stop=(k == KD - 1))
                ins.then_inc(sem("proj_done"), 1)

            for n in range(C_QK):
                project(n, hT)
            for n in range(C_QK, C_QK + 2):
                project(n, hT)
            pe.wait_ge(sem("lora_set"), 1)
            pe.wait_ge(sem("lora_in"), 48)
            for k in range(4):
                c = slice(k * P, (k + 1) * P)
                o = slice(k * SEQ, (k + 1) * SEQ)
                mm(bank(2, 2)[:, o], g.lw2[0:64, c], g.lora[0:64, 0], start=True, stop=True)
                mm(bank(4, 2)[:, o], g.lw2[64:128, c], g.lora[64:128, 0], start=True, stop=True)
                ins = mm(bank(6, 2)[:, o], g.lg2[:, c], g.lora[:, 1], start=True, stop=True)
            ins.then_inc(sem("lora_done"), 1)
            project(C_QK + 2, hT)
            pe.wait_ge(sem("g_out"), 1)
            pe.wait_ge(sem("kk_squared"), 1)
            for q in range(2):
                mm(bank(6 + q), g.head_ones, g.t1[:, 2 * q:2 * q + 2], start=True, stop=True) \
                    .then_inc(sem("kk_summed"), 1)
            for n in range(C_QK + 3, C_V):
                project(n, hT)
            for n in range(C_V, C_MQ):
                project(n, hT, True)
            for n in range(C_MQ, C_MK):
                project(n, hT)
            for n in range(C_MK, C_MV):
                project(n, g.memT)
            for n in range(C_MV, C_GATE):
                project(n, g.memT, True)
            pe.wait_ge(sem("rk_set"), 1)
            pe.wait_ge(sem("kk_sum_out"), 2)
            for q in range(2):
                mm(bank(6 + q), g.head_ones, g.t2[:, 2 * q:2 * q + 2], start=True, stop=True) \
                    .then_inc(sem("rk_summed"), 1)
            for q, (buf, k0, gain) in enumerate(NORM_GROUPS):
                pe.wait_ge(sem("squared"), q + 1)
                for h in range(2):
                    ins = mm(bank(2 + 2 * (q % 2) + h), g.head_ones if buf == "qk" else g.ones,
                             g.t1[:, 2 * h:2 * h + 2], start=True, stop=True)
                ins.then_inc(sem("qk_summed"), 1)

            def scores(u):
                kind, h, i = UNITS[u]
                if u < 2:
                    pe.wait_ge(sem("qk_normed"), len(NORM_GROUPS))
                else:
                    pe.wait_ge(sem("max_set"), u - 1)
                pb = 2 + 2 * (u % 2)
                if kind == "mem":
                    ins = mm(bank(pb)[:, 0:SEQ], g.mq[:, h, i * P:(i + 1) * P], g.mk[:, h], start=True, stop=True)
                else:
                    w = P * (i + 1)
                    for gr in range(DG):
                        gh = gr * DH + h
                        r = slice(64 * (gh % 2), 64 * (gh % 2) + 64)
                        ins = mm(bank(pb, 2)[:, gr * SEQ:gr * SEQ + w], g.qk[r, gh // 2, i * P:(i + 1) * P],
                                 g.qk[r, 6 + gh // 2, 0:w], start=True, stop=True)
                ins.then_inc(sem("scored"), 1)

            def attend(u):
                kind, h, i = UNITS[u]
                blocks = unit_keys(UNITS[u]) // P
                pe.wait_ge(sem("probs_set"), u + 1)
                if u == 0:
                    pe.wait_ge(sem("tildes_set"), 1)
                else:
                    pe.wait_ge(sem("pt_set"), u)
                for b in range(blocks):
                    ins = tr(bank(6, 2)[:, b * P:(b + 1) * P], g.sc2[:, u % 2, b * P:(b + 1) * P], ident)
                ins.then_inc(sem("probs_turned"), 1)
                pe.wait_ge(sem("pt_set"), u + 1)
                if u >= 2:
                    pe.wait_ge(sem("attended"), u - 1)
                elif u == 0:
                    pe.wait_ge(sem("dil_out"), C_GATE - C_QK)
                o = bank(u % 2)
                for b in range(blocks):
                    if kind == "mem":
                        ins = mm(o[:, 0:P], g.mv[:, b, h * P:(h + 1) * P], g.pt2[:, u % 2, b * P:(b + 1) * P],
                                 start=(b == 0), stop=(b == blocks - 1))
                    else:
                        gr, kt = b // (i + 1), b % (i + 1)
                        gh = gr * DH + h
                        ins = mm(o[64 * (h % 2):64 * (h % 2) + 64, 0:P], g.vtok[:, kt, gh * HD:(gh + 1) * HD],
                                 g.pt2[:, u % 2, b * P:(b + 1) * P], start=(b == 0), stop=(b == blocks - 1))
                ins.then_inc(sem("pv_done"), 1)

            scores(0)
            for u in range(len(UNITS)):
                if u + 1 < len(UNITS):
                    scores(u + 1)
                attend(u)
            pe.wait_ge(sem("attended"), len(UNITS))
            for q, src in enumerate((g.kkT, g.aT, g.kT, g.vT)):
                for i in range(NT):
                    n = 2 * q + i
                    if n >= 2:
                        pe.wait_ge(sem("tok_out"), n - 1)
                    for k in range(4):
                        ins = tr(bank(2 + n % 2)[:, k * P:(k + 1) * P], src[:, k, i * P:(i + 1) * P], ident)
                    ins.then_inc(sem("tok_turned"), 1)
            pe.wait_ge(sem("tok_out"), 8)
            rows = (slice(0, 64), slice(64, 128))
            for r in range(4):
                units = (2 * r, 2 * r + 1)
                for u in units:
                    e, i, hp = u % 2, u // 4, u % 4
                    b = 2 + 3 * e
                    if u >= 2:
                        pe.wait_ge(sem("wz_out"), u - 1)
                    t = slice(i * P, (i + 1) * P)
                    for q in range(2):
                        A, B, K, R = (v[rows[q], hp, t] for v in (g.kkT, g.aT, g.kT, g.rT))
                        o, o2 = (bank(k)[:, q * SEQ:(q + 1) * SEQ] for k in (b, b + 2))
                        mm(o[:, 0:P], B, A, start=True, stop=True)
                        mm(o[:, P:2 * P], A, B, start=True, stop=True)
                        mm(bank(b + 1)[:, q * P:(q + 1) * P], B, R, start=True, stop=True)
                        mm(o2[:, 0:P], K, A, start=True, stop=True)
                        ins = mm(o2[:, P:2 * P], K, R, start=True, stop=True)
                        if q == 0:
                            row_tile_done(ins)
                    ins.then_inc(sem("grams_done"), 1)
                for lv in range(LEVELS):
                    for u in units:
                        e = u % 2
                        b = 2 + 3 * e
                        if lv == 0:
                            pe.wait_ge(sem("grams_out"), u + 1)
                        else:
                            pe.wait_ge(sem("q_updated"), 2 * (LEVELS - 1) * r + 2 * (lv - 1) + e + 1)
                        if lv > 1:
                            pe.wait_ge(sem("x_updated"), 2 * (LEVELS - 1) * r + 2 * (lv - 2) + e + 1)
                        for q in range(2):
                            Q, N = (g.qxn4[:, e, q, j] for j in range(2))
                            o = bank(b)[:, q * SEQ:(q + 1) * SEQ]
                            if lv < LEVELS - 1:
                                mm(o[:, 0:P], N, Q, start=True, stop=True)
                                ins = mm(o[:, P:2 * P], Q, N, start=True, stop=True)
                            if lv:
                                ins = mm(bank(b + 1)[:, q * P:(q + 1) * P], N, g.xx4[:, e, q], start=True, stop=True)
                        ins.then_inc(sem("level_done"), 1)
                    if lv % 2 == 1 and lv < LEVELS - 1 and 2 * r + lv // 2 < 8:
                        n = 2 * r + lv // 2
                        if n < 2:
                            pe.wait_ge(sem("attended"), len(UNITS))
                        project(C_GATE + n, hT)
                for u in units:
                    e, i, hp = u % 2, u // 4, u % 4
                    o = bank(4 + 3 * e)
                    for q in range(2):
                        hc = slice((2 * hp + q) * HD, (2 * hp + q + 1) * HD)
                        ins = mm(o[:, q * HD:(q + 1) * HD], g.ak4[:, e, q], g.tok_v[:, i, hc], start=True, stop=True)
                    ins.then_inc(sem("mv_done"), 1)
                for u in units:
                    e, i, hp = u % 2, u // 4, u % 4
                    o = bank(4 + 3 * e)
                    pe.wait_ge(sem("mv_out"), u + 1)
                    pe.wait_ge(sem("x_updated"), 2 * (LEVELS - 1) * r + 2 * (LEVELS - 2) + e + 1)
                    for q in range(2):
                        hc = slice((2 * hp + q) * HD, (2 * hp + q + 1) * HD)
                        X = g.xx4[:, e, q]
                        mm(o[:, P + q * HD:P + (q + 1) * HD], X, g.mv2[:, e, q], start=True, stop=True)
                        mm(o[rows[q], 2 * P:3 * P], g.tok_a[:, i, hc], X, start=True, stop=True)
                        ins = mm(o[rows[q], 3 * P:4 * P], g.tok_v[:, i, hc], g.rk4[:, e, q], start=True, stop=True)
                    ins.then_inc(sem("wz_done"), 1)
            pe.wait_ge(sem("wz_out"), 8)
            for c in range(NCH):
                i, cb = c // 2, L * (c % 2)
                cr, ct = slice(cb, cb + L), slice(c * L, (c + 1) * L)
                if c:
                    pe.wait_ge(sem("s_set"), c)
                    for h in (0, 2, 4, 6, 1, 3, 5, 7):
                        q, hp = h % 2, h // 2
                        ins = mm(bank(2)[cr, h * HD:(h + 1) * HD], g.WT[rows[q], hp, ct],
                                 g.S_hist[rows[q], c, hp * HD:(hp + 1) * HD], start=True, stop=True)
                        if h == 6:
                            row_tile_done(ins)
                    ins.then_inc(sem("u_done"), 1)
                project(C_GATE + 8 + c, hT)
                pe.wait_ge(sem("u_set"), c + 1)
                for h in range(RH) if c < NCH - 1 else ():
                    q, hp = h % 2, h // 2
                    hc = slice(h * HD, (h + 1) * HD)
                    o = bank(3)[rows[q], hp * HD:(hp + 1) * HD]
                    mm(o, g.tok_b[cr, i, hc], g.U[cr, i, hc], start=True, stop=False)
                    ins = mm(o, g.tok_k[cr, i, hc], g.tok_v[cr, i, hc], start=False, stop=True)
                    if h == RH - 1:
                        ins.then_inc(sem("s_done"), 1)
            for i in range(NT):
                for h in range(RH):
                    q, hp = h % 2, h // 2
                    ins = mm(bank(4 + i)[rows[q], hp * P:(hp + 1) * P], g.U[:, i, h * HD:(h + 1) * HD],
                             g.mrb[:, 8 * i + h], start=(h < 2), stop=False, skip_group_check=True)
                row_tile_done(ins)
                for h in (0, 2, 4, 6, 1, 3, 5, 7):
                    q, hp = h % 2, h // 2
                    for c in (2 * i, 2 * i + 1):
                        at = hp * P + (c % 2) * L
                        ins = mm(bank(4 + i)[rows[q], at:at + L], g.S_hist[rows[q], c, hp * HD:(hp + 1) * HD],
                                 g.rT[rows[q], hp, c * L:(c + 1) * L], start=False, stop=True, skip_group_check=True)
                    if h == 6:
                        row_tile_done(ins)
                ins.then_inc(sem("y_done"), 1)
            pe.wait_ge(sem("y_summand"), 1)
            for q in range(2):
                mm(bank(6 + q), g.head_ones, g.y_rwkv[:, 2 * q:2 * q + 2], start=True, stop=True) \
                    .then_inc(sem("y_summed"), 1)
            pe.wait_ge(sem("y_squared"), 1)
            for q in range(2):
                ins = mm(bank(2 + q), g.head_ones, g.rT[:, 2 * q:2 * q + 2], start=True, stop=True)
            ins.then_inc(sem("var_done"), 1)
            for q, (gb, first) in enumerate(MIX):
                n, kn = MIX_CHUNKS[q]
                if first == 0 or n != MIX_CHUNKS[q - 1][0]:
                    load_wait(n)
                w = cut(g.ring(n), k=kn)
                if q == 0:
                    pe.wait_ge(sem("y_root"), 1)
                if q >= 2:
                    pe.wait_ge(sem("mix_out"), q - 1)
                if gb == 0 and first == 0:
                    pe.wait_ge(sem("y_rwkv_set"), 1)
                yt = (g.y_rwkv, g.y_dil, g.y_mem)[gb]
                wm = 0 if w.shape[2] == 512 else first
                for mt in range(4):
                    o = bank(2 + 2 * (q % 2), 2)[:, mt * SEQ:(mt + 1) * SEQ]
                    for k in range(kn):
                        ins = mm(o, w[:, k, (wm + mt) * P:(wm + mt + 1) * P], yt[:, k], start=(k == 0),
                                 stop=(k == kn - 1))
                ins.then_inc(sem("mix_done"), 1)
            pe.wait_ge(sem("mixed"), 4)
            for q in range(4):
                n = C_OUT + q
                load_wait(n)
                w = cut(g.ring(n), k=KD)
                if q >= 2:
                    pe.wait_ge(sem("x2_set"), q - 1)
                for i in range(NT):
                    for k in range(KD):
                        ins = mm(bank(q % 2)[:, i * CW:(i + 1) * CW], hT[:, k, i * P:(i + 1) * P], w[:, k],
                                 start=(k == 0), stop=(k == KD - 1))
                ins.then_inc(sem("out_done"), 1)


def moe_memory(nc, ctx, g):
    def tensor(name, *shape, dtype=F32):
        return ctx.enter_context(nc.sbuf_tensor(name, [P] + list(shape), dtype))[(slice(None),) * (1 + len(shape))]

    g.w_high = tensor("w_high", DEPTH, 2048, dtype=F32R)
    g.w_low = tensor("w_low", DEPTH, 2048, dtype=F32R)
    g.x_parts = tensor("x_parts", KD, 2 * CAP, dtype=F32R)
    g.a_parts = tensor("a_parts", KD, 2 * CAP, dtype=F32R)
    g.xn_parts = [tensor(f"xn_part{n}", NT, D, dtype=BF16) for n in range(3)]
    g.xn_rest = tensor("xn_rest", NT, D)
    g.sel = tensor("sel", NT, CAP, dtype=BF16)
    g.selg = tensor("selg", NT, 2 * CAP)
    g.selT = tensor("selT", SEQ)
    g.fold = tensor("fold", P)
    g.b1_parts = tensor("b1_parts", 2 * FF, dtype=F32R)
    g.pick = tensor("pick", E)
    g.picked = tensor("picked", CAP, dtype=F32R)
    g.posj = tensor("posj", NT, NJ * E)
    g.gate = tensor("gate", NT, NJ * E)
    g.chosen = tensor("chosen", NT, (NJ - 1) * E)
    g.order_i = tensor("order_i", 64, dtype=mybir.dt.int32)
    g.slot_no = tensor("slot_no", 2 * CAP)
    g.before = tensor("before", P)
    g.small = tensor("small", 256)
    w = tensor("scratch", 5120 + KD * E)
    g.xnT = g.cut(w[:, 0:KD * SEQ], k=KD)
    g.b1raw, g.b2raw, g.wr = w[:, 2048:4096], w[:, 4096:5120], w[:, 5120:5120 + KD * E]
    g.gateT = w[0:E, 1536:1792]
    g.hsb = w[:, 0:1024].rearrange("p (u n) -> p u n", u=2)
    g.ye = w[:, 4096:5120]
    g.hg, g.hl, g.hs, g.ha = (w[:, 1024 + 128 * q:1152 + 128 * q].rearrange("p (t n) -> p t n", t=2)
                              for q in range(4))
    g.xn = g.hT.rearrange("p k n -> p (k n)").rearrange("p (i n) -> p i n", i=NT)


def moe(nc, a, out, g):
    sem, bank, cut, param = g.sem, g.bank, g.cut, g.param
    x, ident = g.x, g.ident
    whole = g.part is None
    OWN = 12
    FREED = DEPTH + 1

    slots = [g.ring_lo[:, c % LO] for c in range(CHUNKS)]
    filled = [g.lo_loads[c % LO] if whole else 0 for c in range(CHUNKS)]
    posj, gate, small = g.posj, g.gate, g.small
    logit, top8, tif, eio = (small[:, 0:64].rearrange("p (i e) -> p i e", i=NT),
                             small[:, 64:80].rearrange("p (i e) -> p i e", i=NT),
                             small[:, 80:96].rearrange("p (i e) -> p i e", i=NT), small[:, 96:128])
    oh, rsc, brow = small[:, 128:192], small[:, 192:224], small[0:1, 224:256]
    R = E * (NJ - 1)

    def w_source(e, j):
        if j < W1C:
            w = a["w1"][0][bass.ds(e, 1), :, j * CW:(j + 1) * CW]
        else:
            w = a["w2"][0][bass.ds(e, 1), :, (j - W1C) * CW:(j - W1C + 1) * CW]
        return w.rearrange("o (k p) n -> p (o k) n", p=P)

    def further_blocks(engine):
        engine.wait_ge(sem("order_set"), 1)
        return engine.value_load(g.order_i[0:1, 40:41], min_val=0, max_val=MAX_OVER)

    def further_column(engine, r):
        return engine.value_load(g.order_i[0:1, bass.ds(r, 1)], min_val=0, max_val=NJ * E - 1)

    def further_expert(engine, r):
        return engine.value_load(g.order_i[0:1, bass.ds(r + 20, 1)], min_val=0, max_val=E - 1)

    with nc.Block() as block:
        @block.sync
        def _(sp):
            if not whole:
                sp.dma_start(x, a["x"][0].rearrange("(i p) n -> p i n", p=P)).then_inc(sem("x_in2"), 16)
                for j in range(LO):
                    sp.dma_start(cut(slots[j], k=KD), w_source(0, j)).then_inc(g.arrived[j], 16)

            def load_expert(b, e, first=0):
                for j in range(first, CHUNKS):
                    sp.wait_ge(sem("low_set"), CHUNKS * b + (j + 1 - LO))
                    sp.dma_start(cut(slots[j], k=KD), w_source(e, j)).then_inc(g.arrived[j % LO], 16)

            load_expert(0, 0, LO)
            with sp.Fori(1, E) as b:
                load_expert(b, b)
            count = further_blocks(sp)
            with sp.If(count > 0):
                with sp.Fori(0, count) as r:
                    load_expert(r + E, further_expert(sp, r))
            for i in range(NT):
                sp.wait_ge(sem("out_set"), i + 1)
                sp.dma_start(out[0][i * P:(i + 1) * P, :], x[:, i]).then_inc(sem("stored"), 16)
            sp.wait_ge(sem("stored"), 16 * NT)

        @block.gpsimd
        def _(pool):
            own = Own(pool, sem("pool_moe_steps"))
            pool.dma_start(cut(g.wr, k=KD), a["w_router"][0].rearrange("(k p) n -> p k n", p=P)) \
                .then_inc(sem("router_in"), 16)
            pool.dma_start(brow, a["b_router"]).then_inc(sem("router_in"), 16)
            for half in range(2):
                pool.dma_start(g.b1raw[half * E:(half + 1) * E, :], a["b1"][0]).then_inc(sem("b1_in"), 16)
            pool.dma_start(g.b2raw[0:E, :], a["b2"][0]).then_inc(sem("b_in"), 16)
            if not whole:
                pool.dma_start(g.ln2_row, a["ln2"].broadcast_to([P, D])).then_inc(sem("ln2_in"), 16)
                own.link(nc.gpsimd.memset(g.ones, 1.0))
                own.link(nc.gpsimd.memset(g.stat, 0.0))
                own.link(nc.gpsimd.memset(g.eps_norm, NORM_EPS))
                own.link(nc.gpsimd.memset(ident, 0.0))
                own.link(nc.gpsimd.affine_select(out=ident, in_=ident, compare_op=ALU.not_equal, fill=1.0, base=0,
                                                 pattern=[[-1, P]], channel_multiplier=1))
            own.link(nc.gpsimd.memset(g.before, 1.0))
            own.link(nc.gpsimd.affine_select(out=g.before, in_=g.before, compare_op=ALU.is_gt, fill=0.0, base=0,
                                             pattern=[[1, P]], channel_multiplier=-1))
            own.link(nc.gpsimd.iota(eio, pattern=[[1, E]], base=0, channel_multiplier=0,
                                    allow_small_or_imprecise_dtypes=True))
            own.link(nc.gpsimd.iota(g.slot_no, pattern=[[0, 2], [1, CAP]], base=0, channel_multiplier=0,
                                    allow_small_or_imprecise_dtypes=True))
            for j in range(1, NJ):
                own.link(nc.gpsimd.memset(rsc[E * (j - 1):E * j, 0:1], float(CAP * j)))
            own.link(nc.gpsimd.iota(rsc[0:R, 1:2], pattern=[[0, 1]], base=E, channel_multiplier=1,
                                    allow_small_or_imprecise_dtypes=True))
            nc.gpsimd.memset(g.selT, 0.0).then_inc(sem("selT_set"), 1)
            pool.wait_ge(sem("selT_set"), 1)
            own.link(nc.gpsimd.memset(g.order_i, 0))
            own.link(nc.gpsimd.memset(g.fold, 0.0))
            for shift in (-CAP, CAP):
                own.link(nc.gpsimd.affine_select(out=g.fold, in_=g.fold, compare_op=ALU.not_equal, fill=1.0,
                                                 base=shift, pattern=[[-1, P]], channel_multiplier=1))
            nc.gpsimd.affine_select(out=g.fold, in_=g.fold, compare_op=ALU.not_equal, fill=1.0, base=0,
                                    pattern=[[-1, P]], channel_multiplier=1).then_inc(sem("moe_consts"), 1)

        @block.vector
        def _(dve):
            own = Own(dve, sem("dve_moe_steps"))
            tt, ts, stt = nc.vector.tensor_tensor, nc.vector.tensor_scalar, nc.vector.scalar_tensor_tensor
            copy = nc.vector.tensor_copy

            dve.wait_ge(sem("ln2_in"), 16)
            dve.wait_ge(sem("root2_set"), 1)
            own.link(nc.vector.reciprocal(g.stat[:, 8:10], g.stat[:, 4:6]))
            for i in range(NT):
                stt(g.xn[:, i], x[:, i], g.stat[:, 8 + i:9 + i], g.ln2_row, ALU.mult, ALU.mult) \
                    .then_inc(sem("xn_set"), 1)
            dve.wait_ge(sem("xn_set"), 2)
            own.link(copy(g.xn_parts[0], g.xn))
            own.link(tt(g.xn_rest, g.xn, g.xn_parts[0], ALU.subtract))
            own.link(copy(g.xn_parts[1], g.xn_rest))
            own.link(tt(g.xn_parts[2], g.xn_rest, g.xn_parts[1], ALU.subtract))
            dve.wait_ge(sem("moe_consts"), 1)
            dve.wait_ge(sem("logits_done"), 1)
            own.link(copy(logit, bank(6)[:, 0:NT * E].rearrange("p (i e) -> p i e", i=NT)))
            ti = small[:, 240:256].rearrange("p (i e) -> p i e", i=NT).bitcast(mybir.dt.uint32)
            for i in range(NT):
                own.link(nc.vector.max(out=top8[:, i], in_=logit[:, i]))
                own.link(nc.vector.max_index(ti[:, i], top8[:, i], logit[:, i]))
            own.link(copy(tif, ti))
            ts(g.stat[:, 20:22].unsqueeze(2), top8[:, :, 0:1], -1.0, None, ALU.mult).then_inc(sem("top_set"), 1)
            dve.wait_ge(sem("top_exp"), 1)
            own.link(nc.vector.reciprocal(g.stat[:, 24:26], g.stat[:, 22:24]))
            for i in range(NT):
                own.link(ts(top8[:, i, 0:TOPK], top8[:, i, 0:TOPK], g.stat[:, 24 + i:25 + i], None, ALU.mult))
            for i in range(NT):
                for k in range(TOPK):
                    number, p = tif[:, i, k:k + 1], top8[:, i, k:k + 1]
                    if k == 0:
                        ts(gate[:, i, 0:E], eio, number, p, ALU.is_equal, ALU.mult)
                        own.link(ts(g.chosen[:, i, 0:E], eio, number, None, ALU.is_equal))
                    else:
                        ts(oh[:, 0:E], eio, number, p, ALU.is_equal, ALU.mult)
                        own.link(ts(oh[:, E:2 * E], eio, number, None, ALU.is_equal))
                        tt(gate[:, i, 0:E], gate[:, i, 0:E], oh[:, 0:E], ALU.add)
                        own.link(tt(g.chosen[:, i, 0:E], g.chosen[:, i, 0:E], oh[:, E:2 * E], ALU.add))
            for i in range(NT):
                for j in range(1, NJ):
                    ins = copy(gate[:, i, E * j:E * j + E], gate[:, i, 0:E])
                    if j < NJ - 1:
                        ins = copy(g.chosen[:, i, E * j:E * j + E], g.chosen[:, i, 0:E])
            ins.then_inc(sem("chosen_set"), 1)
            dve.wait_ge(sem("gateT_done"), 1)
            copy(g.gateT, bank(4)[0:E, 0:SEQ]).then_inc(sem("gateT_set"), 1)
            dve.wait_ge(sem("b1_in"), 32)
            raw = g.b1raw[0:2 * E, :]
            own.link(ts(raw[:, 1::2], raw[:, 1::2], 1.0, None, ALU.add))
            own.link(copy(g.b1_parts[0:2 * E, :], raw))
            own.link(tt(g.b1_parts[E:2 * E, :], raw[E:2 * E, :], g.b1_parts[E:2 * E, :].bitcast(F32), ALU.subtract))
            for half in range(2):
                rows = slice(half * E, (half + 1) * E)
                ins = copy(g.pick[rows, :], ident[rows, rows])
            ins.then_inc(sem("b1_set"), 1)
            dve.wait_ge(sem("b1_set"), 1)
            dve.wait_ge(sem("pos_done"), 1)
            own.link(stt(posj[:, :, 0:E], bank(6)[:, 64:64 + NT * E].rearrange("p (i e) -> p i e", i=NT), 1.0,
                         g.chosen[:, :, 0:E], ALU.add, ALU.mult))
            own.link(ts(posj[:, :, 0:E], posj[:, :, 0:E], -1.0, None, ALU.add))
            for j in range(1, NJ):
                own.link(ts(posj[:, :, E * j:E * j + E], posj[:, :, 0:E], -float(CAP * j), None, ALU.add))

            def select(column):
                for i in range(NT):
                    ins = ts(g.sel[:, i, :], g.slot_no[:, 0:CAP], posj[:, i, bass.ds(column, 1)], None,
                             ALU.is_equal)
                ins.then_inc(sem("sel_set"), 1)

            def select_gates(b, column):
                dve.wait_ge(sem("places_turned"), b + 1)
                for i in range(NT):
                    ins = ts(g.selg[:, i, :], g.slot_no[:, :], posj[:, i, bass.ds(column, 1)],
                             gate[:, i, bass.ds(column, 1)], ALU.is_equal, ALU.mult)
                ins.then_inc(sem("selg_set"), 1)

            def tokens_low(n):
                dve.wait_ge(sem("x_high_set"), n)
                tt(g.x_parts[:, :, CAP:2 * CAP], cut(bank(7), k=KD), g.x_parts[:, :, 0:CAP].bitcast(F32),
                   ALU.subtract).then_inc(sem("x_set"), 1)

            select(0)
            c = rsc[0:R]
            own.link(tt(c[:, 2:3], bank(7)[0:R, 0:1], c[:, 0:1], ALU.is_gt))
            stt(c[:, 3:4], c[:, 0:1], -0.5, c[:, 1:2], ALU.mult, ALU.add).then_inc(sem("flag_set"), 1)
            dve.wait_ge(sem("rank_done"), 1)
            own.link(copy(c[:, 4:5], bank(7)[0:R, 1:2]))
            ts(c[:, 8:24], g.slot_no[0:R, 0:16], c[:, 4:5], c[:, 2:3], ALU.is_equal, ALU.mult) \
                .then_inc(sem("ranked"), 1)
            dve.wait_ge(sem("list_done"), 1)
            copy(g.order_i[0:1, 0:16], bank(7)[0:1, 16:32])
            copy(g.order_i[0:1, 20:36], bank(7)[0:1, 32:48])
            copy(g.order_i[0:1, 40:41], bank(7)[0:1, 48:49]).then_inc(sem("order_set"), 1)
            tokens_low(1)

            start = own.n

            def block_of(b, e, column, following):
                own.base, own.n = b * OWN + start, 0

                def low(c):
                    dve.wait_ge(sem("high_set"), b * CHUNKS + (c + 1))
                    tt(g.w_low[:, c % DEPTH, :], slots[c], g.w_high[:, c % DEPTH, :].bitcast(F32), ALU.subtract) \
                        .then_inc(sem("low_set"), 1)

                def clip(q):
                    dve.wait_ge(sem("h_turned"), b * 4 + (q + 1))
                    h = bank(7 - q % 2).rearrange("p (t two n) -> p t two n", t=2, two=2)
                    ts(g.hg, h[:, :, 0, 0:CAP], 7.0, None, ALU.min)
                    ts(g.hl, h[:, :, 1, 0:CAP], 8.0, -6.0, ALU.min, ALU.max).then_inc(sem("glu_set"), 1)
                    dve.wait_ge(sem("glu_set"), b * 4 + (q + 1))
                    own.link(tt(g.hl, g.hl, g.hg, ALU.mult))

                def activate(q):
                    dve.wait_ge(sem("sigmoid_set"), b * 4 + (q + 1))
                    own.link(tt(g.ha, g.hl, g.hs, ALU.mult))
                    c = slice(2 * q, 2 * q + 2)
                    own.link(copy(g.a_parts[:, c, 0:CAP], g.ha))
                    tt(g.a_parts[:, c, CAP:2 * CAP], g.ha, g.a_parts[:, c, 0:CAP].bitcast(F32), ALU.subtract) \
                        .then_inc(sem("act_set"), 1)

                copy(g.picked[0:2 * E, :], g.pick[0:2 * E, bass.ds(e, 1)].broadcast_to([2 * E, CAP])) \
                    .then_inc(sem("picked_set"), 1)
                for c in range(4):
                    low(c)
                clip(0)
                low(4)
                activate(0)
                low(5)
                clip(1)
                low(6)
                activate(1)
                select_gates(b, column)
                dve.wait_ge(sem("gathered"), b + 1)
                select(following)
                low(7)
                clip(2)
                low(8)
                activate(2)
                clip(3)
                low(9)
                activate(3)
                low(10)
                tokens_low(b + 2)
                low(11)
                assert own.n == OWN, own.n

            with dve.Fori(0, E - 1) as b:
                block_of(b, b, b, b + 1)
            count = further_blocks(dve)
            block_of(E - 1, E - 1, E - 1, further_column(dve, 0))
            with dve.If(count > 0):
                with dve.Fori(0, count) as r:
                    block_of(r + E, further_expert(dve, r), further_column(dve, r), further_column(dve, r + 1))
            for i in range(NT):
                dve.wait_ge(sem("all_added"), 1)
                tt(x[:, i], x[:, i], bank(2 * i, 2), ALU.add).then_inc(sem("out_set"), 1)

        @block.scalar
        def _(act):
            own = Own(act, sem("act_moe_steps"))
            if not whole:
                act.wait_ge(sem("x_in2"), 16)
                act.wait_ge(sem("moe_consts"), 1)
            sq = g.xnT.rearrange("p k n -> p (k n)")[:, 0:D]
            for i in range(NT):
                own.link(nc.scalar.activation(sq, x[:, i], ACT.Square, accum_out=g.stat[:, i:i + 1]))
            nc.scalar.activation(g.stat[:, 4:6], g.stat[:, 0:2], ACT.Sqrt, bias=g.eps_norm, scale=1.0 / D) \
                .then_inc(sem("root2_set"), 1)
            for q in range(4):
                act.wait_ge(sem("xn_turned"), q + 1)
                nc.scalar.activation(g.xnT[:, 2 * q:2 * q + 2], cut(bank(4 + q % 2), k=2), ACT.Copy) \
                    .then_inc(sem("xnT_set"), 1)
            act.wait_ge(sem("top_set"), 1)
            for i in range(NT):
                ins = nc.scalar.activation(top8[:, i, 0:TOPK], top8[:, i, 0:TOPK], ACT.Exp,
                                           bias=g.stat[:, 20 + i:21 + i], accum_out=g.stat[:, 22 + i:23 + i])
            ins.then_inc(sem("top_exp"), 1)

            def tokens_out(n):
                act.wait_ge(sem("gathered"), n)
                nc.scalar.activation(g.x_parts[:, :, 0:CAP], cut(bank(7), k=KD), ACT.Copy) \
                    .then_inc(sem("x_high_set"), 1)

            def y_out(b, h):
                act.wait_ge(sem("w_used"), b * CHUNKS + (FREED + 2 * h + 2 - 4))
                nc.scalar.activation(g.ye[:, 512 * h:512 * h + 512], bank(4 + h), ACT.Copy) \
                    .then_inc(sem("y_set"), 1)

            def block_of(b):
                def high(c):
                    act.wait_ge(g.arrived[c % LO], b * 32 + 16 * (filled[c] + c // LO + 1))
                    act.wait_ge(sem("w_used"), b * CHUNKS + (FREED - DEPTH + c + 1))
                    nc.scalar.activation(g.w_high[:, c % DEPTH, :], slots[c], ACT.Copy).then_inc(sem("high_set"), 1)

                def h_out(q):
                    act.wait_ge(sem("w_used"), b * CHUNKS + (FREED + 2 * q + 2))
                    nc.scalar.activation(g.hsb[:, q % 2], bank(4 + q % 2), ACT.Copy).then_inc(sem("h_set"), 1)

                def sigmoid(q):
                    act.wait_ge(sem("glu_set"), b * 4 + (q + 1))
                    nc.scalar.activation(g.hs, g.hg, ACT.Sigmoid, scale=1.702).then_inc(sem("sigmoid_set"), 1)

                high(0)
                y_out(b, 0)
                high(1)
                high(2)
                y_out(b, 1)
                high(3)
                h_out(0)
                high(4)
                high(5)
                sigmoid(0)
                h_out(1)
                high(6)
                sigmoid(1)
                high(7)
                h_out(2)
                high(8)
                sigmoid(2)
                high(9)
                h_out(3)
                high(10)
                sigmoid(3)
                tokens_out(b + 2)
                high(11)
                act.wait_ge(sem("places_turned"), b + 2)
                nc.scalar.activation(g.selT[:, :], bank(6)[:, 0:SEQ], ACT.Copy).then_inc(sem("selT_set"), 1)

            tokens_out(1)
            with act.Fori(0, E) as b:
                block_of(b)
            count = further_blocks(act)
            with act.If(count > 0):
                with act.Fori(0, count) as r:
                    block_of(r + E)
            y_out(count + E, 0)
            y_out(count + E, 1)

        @block.tensor
        def _(pe):
            mm, tr = nc.tensor.matmul, nc.tensor.transpose
            pe.wait_ge(sem("b_in"), 16)
            if not whole:
                pe.wait_ge(sem("moe_consts"), 1)
            for i in range(NT):
                pe.wait_ge(sem("xn_set"), i + 1)
            for q in range(4):
                if q >= 2:
                    pe.wait_ge(sem("xnT_set"), q - 1)
                for kk in range(2):
                    for i in range(NT):
                        ins = tr(bank(4 + q % 2)[:, kk * SEQ + i * P:kk * SEQ + (i + 1) * P],
                                 g.xn[:, i, (2 * q + kk) * P:(2 * q + kk + 1) * P], ident)
                ins.then_inc(sem("xn_turned"), 1)
            pe.wait_ge(sem("router_in"), 32)
            pe.wait_ge(sem("xnT_set"), 4)
            for i in range(NT):
                o = bank(6)[:, i * E:(i + 1) * E]
                mm(o, g.ones[0:1, 0:P], brow, start=True, stop=False)
                for k in range(KD):
                    ins = mm(o, g.xnT[:, k, i * P:(i + 1) * P], cut(g.wr, k=KD)[:, k], start=False, stop=(k == KD - 1))
            ins.then_inc(sem("logits_done"), 1)
            pe.wait_ge(sem("chosen_set"), 1)
            for i in range(NT):
                ins = tr(bank(4)[0:E, i * P:(i + 1) * P], gate[:, i, 0:E], ident)
            ins.then_inc(sem("gateT_done"), 1)
            first, second = g.chosen[:, 0, :], g.chosen[:, 1, :]
            mm(bank(6)[:, 64:64 + E], g.before[:, :], first[:, 0:E], start=True, stop=True)
            mm(bank(6)[:, 64 + E:64 + 2 * E], g.ones, first[:, 0:E], start=True, stop=False)
            mm(bank(6)[:, 64 + E:64 + 2 * E], g.before[:, :], second[:, 0:E], start=False, stop=True)
            mm(bank(7)[0:R, 0:1], first, g.ones[:, 0:1], start=True, stop=False)
            mm(bank(7)[0:R, 0:1], second, g.ones[:, 0:1], start=False, stop=True).then_inc(sem("pos_done"), 1)
            pe.wait_ge(sem("gateT_set"), 1)
            for i in range(NT):
                for h in range(2):
                    mm(bank(2 * i + h), g.gateT[:, i * P:(i + 1) * P], g.b2raw[0:E, 512 * h:512 * h + 512],
                       start=True, stop=True, skip_group_check=True)
            c = rsc[0:R]
            pe.wait_ge(sem("flag_set"), 1)
            mm(bank(7)[0:R, 1:2], g.before[0:R, 0:R], c[:, 2:3], start=True, stop=True).then_inc(sem("rank_done"), 1)
            pe.wait_ge(sem("ranked"), 1)
            mm(bank(7)[0:1, 16:32], c[:, 1:2], c[:, 8:24], start=True, stop=True)
            mm(bank(7)[0:1, 32:48], c[:, 3:4], c[:, 8:24], start=True, stop=True)
            mm(bank(7)[0:1, 48:49], c[:, 2:3], g.ones[0:R, 0:1], start=True, stop=True).then_inc(sem("list_done"), 1)
            pe.wait_ge(sem("order_set"), 1)

            def gather():
                for k in range(KD):
                    for n, src in enumerate(g.xn_parts):
                        for i in range(NT):
                            ins = mm(bank(7)[:, k * CAP:(k + 1) * CAP], src[:, i, k * P:(k + 1) * P], g.sel[:, i, :],
                                     start=(n == 0 and i == 0), stop=(n == 2 and i == NT - 1))
                ins.then_inc(sem("gathered"), 1)

            def turn_places(b):
                pe.wait_ge(sem("selg_set"), b + 1)
                for i in range(NT):
                    ins = tr(bank(6)[:, i * P:(i + 1) * P], g.selg[:, i, :], ident)
                ins.then_inc(sem("places_turned"), 1)

            def scatter(b):
                pe.wait_ge(sem("selT_set"), b + 1)
                pe.wait_ge(sem("y_set"), b * 2 + 2)
                for h in range(2):
                    for i in range(NT):
                        mm(bank(2 * i + h), g.selT[:, i * P:(i + 1) * P], g.ye[:, 512 * h:512 * h + 512],
                           start=False, stop=True, skip_group_check=True)

            for q in range(FREED):
                tr(bank(4 + q % 2)[:, 0:P], ident, ident).then_inc(sem("w_used"), 1)
            tr(bank(4)[:, 0:P], ident, ident).then_inc(sem("places_turned"), 1)
            pe.wait_ge(sem("sel_set"), 1)
            gather()

            pe.wait_ge(sem("b1_set"), 1)

            def block_of(b):
                def product(c, o, tokens):
                    pe.wait_ge(sem("low_set"), b * CHUNKS + (c + 1))
                    for k in range(KD):
                        for n, w in enumerate((g.w_high, g.w_low)):
                            ins = mm(o, tokens[:, k, :], w[:, c % DEPTH, k * CW:(k + 1) * CW],
                                     start=(k == 0 and n == 0), stop=(k == KD - 1 and n == 1))
                    if c < W1C:
                        ins = mm(o[0:CAP], g.picked[0:2 * E, :],
                                 g.b1_parts[0:2 * E, c * CW:(c + 1) * CW], start=False, stop=True,
                                 skip_group_check=True)
                    ins.then_inc(sem("w_used"), 1)

                def turn(q):
                    pe.wait_ge(sem("h_set"), b * 4 + (q + 1))
                    if q == 1:
                        pe.wait_ge(sem("selT_set"), b + 1)
                    elif q >= 2:
                        pe.wait_ge(sem("glu_set"), b * 4 + (q - 1))
                    for t in range(2):
                        for two in range(2):
                            at = (2 * t + two) * P
                            ins = mm(bank(7 - q % 2)[:, at:at + P], g.hsb[:, q % 2, t * CW + two:(t + 1) * CW:2],
                                     g.fold[:, :], start=True, stop=True)
                    ins.then_inc(sem("h_turned"), 1)

                pe.wait_ge(sem("x_set"), b + 1)
                pe.wait_ge(sem("picked_set"), b + 1)
                for q in range(4):
                    if q < 2:
                        pe.wait_ge(sem("y_set"), b * 2 + (q + 1))
                    else:
                        pe.wait_ge(sem("h_set"), b * 4 + (q - 1))
                    for t in range(2):
                        product(2 * q + t, bank(4 + q % 2)[:, t * CW:(t + 1) * CW], g.x_parts)
                        if q and not t:
                            turn(q - 1)
                turn(3)
                pe.wait_ge(sem("sel_set"), b + 2)
                pe.wait_ge(sem("glu_set"), b * 4 + 3)
                gather()
                scatter(b)
                pe.wait_ge(sem("act_set"), b * 4 + 4)
                turn_places(b)
                for c in range(W1C, CHUNKS):
                    h, t = (c - W1C) // 2, c % 2
                    product(c, bank(4 + h)[:, t * CW:(t + 1) * CW], g.a_parts)

            with pe.Fori(0, E) as b:
                block_of(b)
            count = further_blocks(pe)
            with pe.If(count > 0):
                with pe.Fori(0, count) as r:
                    block_of(r + E)
            scatter(count + E)
            tr(bank(4)[:, 0:P], ident, ident).then_inc(sem("all_added"), 1)


NAMES = ["x", "mem", "ln1", "w_in", "token_mu", "rwkv_w0", "rwkv_w2", "rwkv_a0", "rwkv_a2", "rwkv_g2", "rwkv_k_k",
         "rwkv_k_a", "rwkv_r_k", "rwkv_ln_w", "rwkv_ln_b", "dil_q_norm", "dil_k_norm", "ln_mem", "w_mem_kv",
         "mem_q_norm", "mem_k_norm", "p_rwkv", "p_dil", "p_mem", "w_out", "ln2", "w_router", "b_router", "w1",
         "b1", "w2", "b2"]


def kernel(**inputs):
    import concourse.bacc as bacc
    from concourse.bass_utils import run_bass_kernel_spmd

    nc = bacc.Bacc("TRN2", target_bir_lowering=False, num_devices=1)
    arrays = {n: np.ascontiguousarray(inputs[n]) for n in NAMES}
    a = {n: nc.dram_tensor(n, v.shape, F32, kind="ExternalInput").ap() for n, v in arrays.items()}
    out = nc.dram_tensor("out", (1, SEQ, D), F32, kind="ExternalOutput").ap()
    build(nc, a, out)
    return run_bass_kernel_spmd(nc, [arrays], core_ids=[0]).results[0]["out"]
```

```python
from contextlib import ExitStack

import numpy as np

import concourse.bass as bass
from concourse import mybir

F32 = mybir.dt.float32
F32R = mybir.dt.float32r
BF16 = mybir.dt.bfloat16
ALU = mybir.AluOpType
ACT = mybir.ActivationFunctionType
AX = mybir.AxisListType.X

P = 128
D = 1024
SEQ = 256
NT = SEQ // P
KD = D // P
HD = 64
RH = 8
RT4 = RH * HD // P
L = 64
NCH = SEQ // L
LEVELS = 6
DH = 4
DG = 3
DIL = (1, 4, 16)
SPAN = 128
MH = 4
E = 32
TOPK = 4
FF = 1024
CAP = 64
NJ = SEQ // CAP
MAX_OVER = 15
SWIGLU_ALPHA = 1.702
NORM_EPS = 1e-5
GN_EPS = HD * 1e-5
NEG = -1e30
CW = 256
LO = 6
CHUNKS = 12
DEPTH = 4
EW = 512
EK = EW // P
W1C = 2 * (2 * FF // EW)

ROWS = {}
_at = 0
for _name, _n in (("ln1", 8), ("ln_mem", 8), ("ln2", 8), ("token_mu", 14), ("rwkv_w0", 4), ("rwkv_a0", 4),
                  ("rwkv_k_k", 4), ("rwkv_k_a", 4), ("rwkv_r_k", 4), ("rwkv_ln_w", 4), ("rwkv_ln_b", 4),
                  ("dil_q_norm", 1), ("dil_k_norm", 1), ("mem_q_norm", 1), ("mem_k_norm", 1)):
    ROWS[_name] = (_at, _n)
    _at += _n
NROWS = _at

C_RWKV, C_QK, C_V, C_MQ, C_MK, C_MV, C_GATE = 0, 7, 13, 16, 18, 20, 22
C_PMEM, C_PDIL, C_PRWKV, C_OUT, NMIX = 34, 36, 37, 39, 43
MIX = ((2, 0), (2, 4), (1, 0), (1, 4), (0, 0), (0, 4))
MIX_CHUNKS = ((C_PMEM, 4), (C_PMEM + 1, 4), (C_PDIL, 2), (C_PDIL, 2), (C_PRWKV, 4), (C_PRWKV + 1, 4))
FIRST = (-NMIX) % LO


UNITS = [(kind, h, i) for kind in ("mem", "dil") for h in range(4) for i in range(NT)]


def unit_keys(unit):
    return SEQ if unit[0] == "mem" else DG * P * (unit[2] + 1)


NORM_GROUPS = (("qk", 0, ("dil_q_norm", "dil_q_norm")), ("qk", 4, ("dil_q_norm", "dil_k_norm")),
               ("qk", 8, ("dil_k_norm", "dil_k_norm")), ("mq", 0, ("mem_q_norm", "mem_q_norm")),
               ("mk", 0, ("mem_k_norm", "mem_k_norm")))


KEPT = 12288 + 2048 + 2048 + 256 + 1024 + NROWS + 8 + 64
MIXER = 35400


NORM_AT = {C_MQ: (0,), C_MQ + 1: (1,), C_MK: (2,), C_MV: (3,), C_GATE: (4,)}
NORM_AFTER = (C_QK + 2, C_QK + 4, C_QK + 6, C_MK, C_MV)


GATE_PLACES = {("norms", 0): 6}
for _u, _unit in enumerate(UNITS):
    GATE_PLACES["attention", _u, 0] = 1 if _u >= 10 else 0
    GATE_PLACES["attention", _u, 1] = 1 if _unit[0] == "dil" else 0
for _r in range(4):
    for _lv in range(LEVELS - 1):
        GATE_PLACES["level", _r, _lv] = 2 if _lv == 0 else 1
for _c in range(NCH):
    GATE_PLACES["chain", _c] = 1
assert sum(GATE_PLACES.values()) == 4 * (C_PMEM - C_GATE)


def gate_quarters(place):
    before = sum(list(GATE_PLACES.values())[:list(GATE_PLACES).index(place)])
    return [divmod(n, 4) for n in range(before, before + GATE_PLACES[place])]


RAW_GATES = sum(n for place, n in GATE_PLACES.items() if place[0] in ("norms", "attention")) // 4


class Own:

    def __init__(self, engine, sem, base=0):
        self.engine, self.sem, self.base, self.n = engine, sem, base, 0

    def __call__(self, instruction):
        instruction.then_inc(self.sem, 1)
        self.n += 1

    def wait(self):
        self.engine.wait_ge(self.sem, self.base + self.n)

    def link(self, instruction):
        self(instruction)
        self.wait()


class Layout:
    pass


def build(nc, a, out, part=None):
    g = Layout()
    with ExitStack() as ctx:
        g.sems = {}

        def sem(name):
            if name not in g.sems:
                g.sems[name] = ctx.enter_context(nc.semaphore(name))
            return g.sems[name]

        g.ps = ctx.enter_context(nc.psum_tensor("banks", [P, 8 * 512], F32))

        def bank(b, n=1):
            return g.ps[:, b * 512:(b + n) * 512]

        arena = ctx.enter_context(nc.sbuf_tensor("arena", [P, KEPT], F32))
        top = [0]

        def place(n):
            top[0] += n
            assert top[0] <= arena.shape[1], top[0]
            return arena[:, top[0] - n:top[0]]

        def cut(ap, **dims):
            names = list(dims)
            return ap.rearrange(f"p ({' '.join(names)} n) -> p {' '.join(names)} n", **dims)

        g.ring_lo = cut(place(LO * 2048), s=LO)
        g.x = cut(place(NT * D), i=NT)
        g.hT = cut(place(KD * SEQ), k=KD)
        g.ident, g.ones = place(P), place(P)
        g.ln2_row = place(D)
        g.cols = place(NROWS + 8)
        g.eps_norm = g.cols[:, NROWS:NROWS + 1]
        g.eps_gn = g.cols[:, NROWS + 1:NROWS + 2]
        g.stat = place(64)

        def param(name):
            at, n = ROWS[name]
            return g.cols[:, at:at + n]

        def ring(n):
            return g.ring_lo[:, (FIRST + n) % LO]

        g.arrived = [sem(f"slot{s}_arrived") for s in range(LO)]

        def nth(n):
            return (FIRST + n) // LO + (1 if (FIRST + n) % LO >= FIRST else 0)

        g.lo_loads = [nth(NMIX - LO + s) for s in range(LO)]

        w_in, w_kv = a["w_in"][0], a["w_mem_kv"][0]

        def columns(w, at, n=CW):
            return w[:, at:at + n].rearrange("(k p) n -> p k n", p=P)

        def chunk_source(n):
            if n < C_MK:
                return columns(w_in, n * CW)
            if n < C_GATE:
                return columns(w_kv, (n - C_MK) * CW)
            if n < C_PMEM:
                return columns(w_in, (n - C_GATE) * CW + C_MK * CW)
            if n < C_PDIL:
                return columns(a["p_mem"][0], (n - C_PMEM) * 512, 512)
            if n < C_PRWKV:
                return columns(a["p_dil"][0], 0, 1024)
            if n < C_OUT:
                return columns(a["p_rwkv"][0], (n - C_PRWKV) * 512, 512)
            return columns(a["w_out"][0], (n - C_OUT) * CW)

        g.sem, g.bank, g.cut, g.param, g.ring, g.nth, g.chunk_source = sem, bank, cut, param, ring, nth, chunk_source
        g.part = part
        if part != "moe":
            with ExitStack() as own:
                mixer_memory(nc, own, g)
                mixer(nc, a, g)
        if part == "mixer":
            with nc.Block() as block:
                @block.sync
                def _(sp):
                    sp.dma_start(out[0].rearrange("(i p) n -> p i n", p=P), g.x).then_inc(sem("stored"), 16)
                    sp.wait_ge(sem("stored"), 16)
        else:
            with ExitStack() as own:
                moe_memory(nc, own, g)
                moe(nc, a, out, g)


def mixer_memory(nc, ctx, g):
    arena = ctx.enter_context(nc.sbuf_tensor("mixer_arena", [P, MIXER], F32))
    top, cut = [0], g.cut

    def place(n):
        top[0] += n
        assert top[0] <= arena.shape[1], top[0]
        return arena[:, top[0] - n:top[0]]

    g.mask_s, g.mask_l, g.mask_i, g.head_ones = (place(P) for _ in range(4))
    g.amask = cut(place(3 * SEQ), g=3)
    region = top[0]
    g.Zraw = cut(place(14 * 257), k=14)
    g.qk = cut(place(12 * SEQ), k=12)
    g.vtok = cut(place(NT * 768), i=NT)
    g.mq = cut(place(4 * SEQ), k=4)
    g.mk = cut(place(4 * SEQ), k=4)
    g.mv = cut(place(NT * 512), i=NT)
    g.sc2 = cut(place(2 * 768), u=2)
    g.pt2 = cut(place(2 * 768), u=2)
    end_attention = top[0]
    top[0] = region
    g.tokm = cut(place(4 * NT * 512), q=4)
    g.tok_a, g.tok_b, g.tok_k, g.tok_v = (cut(g.tokm[:, q], i=NT) for q in range(4))
    g.WT = cut(place(4 * SEQ), k=4)
    g.Zt = cut(place(NT * 512), i=NT)
    g.mrb = cut(place(16 * P), q=16)
    g.Y0 = cut(place(4 * SEQ), k=4)
    g.S_hist = cut(place((NCH + 1) * 256), c=NCH + 1)
    g.qxn4 = place(4 * 256).rearrange("p (u q j n) -> p u q j n", u=2, q=2, j=2)
    g.xx4 = place(4 * P).rearrange("p (u q n) -> p u q n", u=2, q=2)
    g.ak4 = place(4 * P).rearrange("p (u q n) -> p u q n", u=2, q=2)
    g.rk4 = place(4 * P).rearrange("p (u q n) -> p u q n", u=2, q=2)
    g.mv2 = place(4 * HD).rearrange("p (u q n) -> p u q n", u=2, q=2)
    g.U = cut(place(NT * 512), i=NT)
    top[0] = max(top[0], end_attention)
    g.gates = cut(place(24 * SEQ), k=24)
    g.rT, g.kT, g.aT, g.kkT, g.vT, g.gT, g.dec = (cut(place(4 * SEQ), k=4) for _ in range(7))
    g.lora = cut(place(2 * SEQ), k=2)
    g.tmp = cut(place(4 * SEQ), k=4)
    g.zs = g.Zraw.rearrange("p k n -> p (k n)")
    g.t1, g.t2, g.t3 = (cut(g.zs[:, q * 1024:(q + 1) * 1024], k=4) for q in range(3))
    g.p_last = place(4 * NCH).rearrange("p (k c) -> p k c", k=4)
    g.lw2 = place(512)
    g.lg2 = place(512)
    g.yT = cut(place(10 * SEQ), k=10)
    g.y_rwkv, g.y_dil, g.y_mem = g.yT[:, 0:4], g.yT[:, 4:6], g.yT[:, 6:10]
    gflat = g.gates.rearrange("p k n -> p (k n)")
    g.memx = cut(gflat[:, 0:NT * D], i=NT)
    g.memT = cut(gflat[:, NT * D:2 * NT * D], k=KD)
    g.sq = gflat[:, 4096:5120]
    g.prow = gflat[0:NROWS, 5120:5248]


def mixer(nc, a, g):
    sem, bank, cut, param = g.sem, g.bank, g.cut, g.param
    x, hT, ident, cols = g.x, g.hT, g.ident, g.cols
    POOL_ROWS = 5

    def wait_rows(engine):
        engine.wait_ge(sem("first_rows_in"), 16 * POOL_ROWS)
        engine.wait_ge(sem("rows_in"), 16 * (len(ROWS) + 2 - POOL_ROWS))

    def load_rows(engine, names, loaded):
        for name in names:
            at, n = ROWS[name]
            src = a[name][0]
            if name == "rwkv_r_k":
                src = src.rearrange("h d -> (h d)")
            for half in range(2 if name.startswith("dil") else 1):
                dst = g.prow[at:at + 1, half * HD:(half + 1) * HD] if name.startswith("dil") else g.prow[at:at + n, :]
                engine.dma_start(dst, src.rearrange("(a n) -> a n", a=n)).then_inc(sem(loaded), 16)

    with nc.Block() as block:
        @block.sync
        def _(sp):
            def wait_used(n):
                if n < C_PMEM:
                    sp.wait_ge(sem("proj_done"), n + 1)
                elif n < C_OUT:
                    last = max(q for q in range(len(MIX)) if MIX_CHUNKS[q][0] == n)
                    sp.wait_ge(sem("mix_done"), last + 1)
                else:
                    sp.wait_ge(sem("out_done"), n - C_OUT + 1)

            sp.dma_start(x, a["x"][0].rearrange("(i p) n -> p i n", p=P)).then_inc(sem("x_in"), 16)
            wait_rows(sp)
            for n in range(NMIX):
                if n == 2:
                    sp.dma_start(g.memx, a["mem"][0].rearrange("(i p) n -> p i n", p=P)) \
                        .then_inc(sem("mem_in"), 16)
                if n >= LO:
                    wait_used(n - LO)
                src = g.chunk_source(n)
                dst = cut(g.ring(n), k=src.shape[1])
                sp.dma_start(dst, src).then_inc(g.arrived[(FIRST + n) % LO], 16)
            for s in range(LO):
                wait_used(NMIX - LO + s)
                sp.dma_start(cut(g.ring_lo[:, s], k=EK), expert_chunk(a, 0, s).rearrange("(k p) n -> p k n", p=P)) \
                    .then_inc(g.arrived[s], 16)

        @block.gpsimd
        def _(pool):
            own = Own(pool, sem("pool_steps"))
            own.link(nc.gpsimd.memset(ident, 0.0))
            nc.gpsimd.affine_select(out=ident, in_=ident, compare_op=ALU.not_equal, fill=1.0, base=0,
                                    pattern=[[-1, P]], channel_multiplier=1).then_inc(sem("ident_set"), 1)
            own.link(nc.gpsimd.memset(g.eps_norm, NORM_EPS))
            own.link(nc.gpsimd.memset(g.eps_gn, GN_EPS))
            nc.gpsimd.memset(g.stat, 0.0).then_inc(sem("eps_set"), 1)
            load_rows(pool, list(ROWS)[:POOL_ROWS], "first_rows_in")
            own.link(nc.gpsimd.memset(g.ones, 1.0))
            own.link(nc.gpsimd.memset(g.head_ones, 0.0))
            own.link(nc.gpsimd.memset(g.head_ones[0:64, 0:64], 1.0))
            own.link(nc.gpsimd.memset(g.head_ones[64:128, 64:128], 1.0))
            own.link(nc.gpsimd.memset(g.mask_s, 0.0))
            own.link(nc.gpsimd.memset(g.mask_l, 0.0))
            own.link(nc.gpsimd.memset(g.mask_i, 0.0))
            for q in range(2):
                r = slice(q * L, (q + 1) * L)
                for msk in (g.mask_s, g.mask_l, g.mask_i):
                    own.link(nc.gpsimd.memset(msk[r, r], 1.0))
            own.link(nc.gpsimd.memset(g.amask, 0.0))
            for msk, op, sign in ((g.mask_s, ALU.is_gt, 1), (g.mask_l, ALU.is_gt, -1), (g.mask_i, ALU.is_ge, 1)):
                own.link(nc.gpsimd.affine_select(out=msk, in_=msk, compare_op=op, fill=0.0, base=0,
                                        pattern=[[sign, P]], channel_multiplier=-sign))
            own.link(nc.gpsimd.affine_select(out=g.amask, in_=g.amask, compare_op=ALU.is_ge, fill=NEG, base=P,
                                             pattern=[[0, 3], [-1, SEQ]], channel_multiplier=1))
            own.link(nc.gpsimd.affine_select(out=g.amask[:, 0], in_=g.amask[:, 0], compare_op=ALU.is_ge, fill=NEG,
                                    base=SPAN - P, pattern=[[1, SEQ]], channel_multiplier=-1))
            ti = g.pt2.rearrange("p u n -> p (u n)")[:, 0:SEQ].bitcast(mybir.dt.int32)
            nc.gpsimd.iota(ti, pattern=[[-1, SEQ]], base=P, channel_multiplier=1).then_inc(sem("consts_set"), 1)
            pool.dma_start(g.ln2_row, a["ln2"].broadcast_to([P, D])).then_inc(sem("ln2_in"), 16)
            pool.dma_start(g.lw2[0:64, :], a["rwkv_w2"][0]).then_inc(sem("lora_in"), 16)
            pool.dma_start(g.lw2[64:128, :], a["rwkv_a2"][0]).then_inc(sem("lora_in"), 16)
            pool.dma_start(g.lg2[:, :], a["rwkv_g2"][0]).then_inc(sem("lora_in"), 16)

        @block.vector
        def _(dve):
            own = Own(dve, sem("dve_steps"))
            tt, ts, stt = nc.vector.tensor_tensor, nc.vector.tensor_scalar, nc.vector.scalar_tensor_tensor

            def bc(v, n):
                return v.unsqueeze(2).broadcast_to([P, v.shape[1], n])

            def norm(k, src, dst, name):
                dve.wait_ge(sem("root_set"), k + 1)
                own.link(nc.vector.reciprocal(g.stat[:, 12 + 2 * k:14 + 2 * k], g.stat[:, 4 + 4 * k:6 + 4 * k]))
                for i in range(NT):
                    ts(dst[:, i], src[:, i], g.stat[:, 12 + 2 * k + i:13 + 2 * k + i], None, ALU.mult) \
                        .then_inc(sem(name + "_normed"), 1)

            def turned_out(name, dst, gain, first):
                for q in range(4):
                    dve.wait_ge(sem(name + "_turned"), q + 1)
                    tt(dst[:, 2 * q:2 * q + 2], cut(bank(first + q % 2), k=2),
                       bc(param(gain)[:, 2 * q:2 * q + 2], SEQ), ALU.mult).then_inc(sem(name + "_turned_out"), 1)

            norm(0, x, cut(g.zs[:, 0:NT * D], i=NT), "x")
            dve.wait_ge(sem("cols_set"), 1)
            turned_out("x", hT, "ln1", 0)
            norm(1, g.memx, g.memx, "mem")
            dve.wait_ge(sem("consts_set"), 1)
            ti = g.pt2.rearrange("p u n -> p (u n)")[:, 0:SEQ].bitcast(mybir.dt.int32)
            tr = g.pt2.rearrange("p u n -> p (u n)")[:, 256:512].bitcast(mybir.dt.int32)
            neg = g.pt2.rearrange("p u n -> p (u n)")[:, 512:768]
            own.link(ts(neg, ti, 0, NEG, ALU.is_lt, ALU.mult))
            for q in (1, 2):
                own.link(ts(tr, ti, DIL[q] - 1, None, ALU.bitwise_and))
                own.link(ts(g.amask[:, q], tr, 0, NEG, ALU.is_gt, ALU.mult))
                own.link(tt(g.amask[:, q], g.amask[:, q], neg, ALU.min))

            turned_out("mem", g.memT, "ln_mem", 2)

            mu = param("token_mu")
            for q, (dst, first, n) in enumerate(((g.rT, 0, 4), (g.kT, 4, 4), (g.vT, 8, 4), (g.lora, 12, 2))):
                dve.wait_ge(sem("z_out"), first // 2 + (n + 1) // 2)
                z, zp = g.Zraw[:, first:first + n, 1:257], g.Zraw[:, first:first + n, 0:256]
                d = g.tmp[:, 0:n]
                own.link(tt(d, zp, z, ALU.subtract))
                own.link(tt(d, d, bc(mu[:, first:first + n], SEQ), ALU.mult))
                tt(dst, d, z, ALU.add).then_inc(sem("shifted"), 1)
                dve.wait_ge(sem("shifted"), q + 1)
            dve.wait_ge(sem("shifted"), 4)
            own.link(tt(g.kkT, g.kT, bc(param("rwkv_k_k"), SEQ), ALU.mult))
            tt(g.t1, g.kkT, g.kkT, ALU.mult).then_inc(sem("kk_squared"), 1)
            for q in range(2):
                dve.wait_ge(sem("kk_summed"), q + 1)
                ts(g.t1[:, 2 * q:2 * q + 2], cut(bank(6 + q), k=2), 1e-24, None, ALU.max) \
                    .then_inc(sem("kk_sum_out"), 1)
            dve.wait_ge(sem("kk_root"), 1)
            own.link(nc.vector.reciprocal(g.t1, g.t1))
            own.link(tt(g.kkT, g.kkT, g.t1, ALU.mult))
            dve.wait_ge(sem("a_set"), 1)
            own.link(ts(g.t2, g.aT, -1.0, None, ALU.add))
            own.link(tt(g.t2, g.t2, bc(param("rwkv_k_a"), SEQ), ALU.mult))
            own.link(stt(g.kT, g.t2, 1.0, g.kT, ALU.add, ALU.mult))
            own.link(tt(g.t2, g.rT, g.kT, ALU.mult))
            tt(g.t2, g.t2, bc(param("rwkv_r_k"), SEQ), ALU.mult).then_inc(sem("rk_set"), 1)
            own.link(tt(g.aT, g.aT, g.kkT, ALU.mult))
            dve.wait_ge(sem("decay_set"), 1)
            nc.vector.memset(g.t3, 0.0)
            fl = lambda v: v.rearrange("p k n -> p (k n)")
            ch = lambda v: v.rearrange("p k (c t) -> p (k c) t", t=L)
            own.link(nc.vector.memset(g.t1, 0.0))
            own.link(nc.vector.tensor_copy(ch(g.t3)[:, :, 0:1], ch(g.tmp)[:, :, 0:1]))
            own.link(nc.vector.memset(ch(g.tmp)[:, :, 0:1], 0.0))
            own.link(nc.vector.tensor_tensor_scan(fl(g.dec), fl(g.tmp), fl(g.t3), 0.0, ALU.mult, ALU.add))
            own.link(nc.vector.tensor_copy(g.p_last.rearrange("p k c -> p (k c)").unsqueeze(2),
                                           ch(g.dec)[:, :, L - 1:L]))
            nc.vector.tensor_scalar(ch(g.t1)[:, :, 0:1], ch(g.kkT)[:, :, 0:1], -1.0, None, ALU.mult)
            own.link(stt(ch(g.t1)[:, :, 1:L], ch(g.kkT)[:, :, 1:L], -1.0, ch(g.dec)[:, :, 0:L - 1],
                         ALU.mult, ALU.mult))
            nc.vector.tensor_copy(g.kkT, g.t1)
            own.link(tt(g.rT, g.rT, g.dec, ALU.mult))
            own.link(nc.vector.reciprocal(g.dec, g.dec))
            tt(g.kT, g.kT, g.dec, ALU.mult)
            tt(g.aT, g.aT, g.dec, ALU.mult).then_inc(sem("tildes_set"), 1)
            dve.wait_ge(sem("tildes_set"), 1)
            for q in range(2):
                dve.wait_ge(sem("rk_summed"), q + 1)
                own.link(tt(g.dec[:, 2 * q:2 * q + 2], cut(bank(6 + q), k=2), g.vT[:, 2 * q:2 * q + 2], ALU.mult))
            squares, roots = (g.t1, g.t3), (g.t2, g.tmp)

            def group(q):
                buf, k0, _ = NORM_GROUPS[q]
                return {"qk": g.qk, "mq": g.mq, "mk": g.mk}[buf][:, k0:k0 + 4]

            def square(q):
                dve.wait_ge(sem("dil_out"), NORM_AFTER[q] - C_QK)
                if q >= 2:
                    dve.wait_ge(sem("qk_summed"), q - 1)
                tt(squares[q % 2], group(q), group(q), ALU.mult).then_inc(sem("squared"), 1)

            square(0)
            for q, (buf, k0, gain) in enumerate(NORM_GROUPS):
                if q + 1 < len(NORM_GROUPS):
                    square(q + 1)
                t = group(q)
                dve.wait_ge(sem("qk_root"), q + 1)
                own.link(nc.vector.reciprocal(roots[q % 2], roots[q % 2]))
                for h in range(2):
                    c = slice(2 * h, 2 * h + 2)
                    ins = stt(t[:, c], t[:, c], param(gain[h]), roots[q % 2][:, c], ALU.mult, ALU.mult)
                ins.then_inc(sem("qk_normed"), 1)

            def attention_out(u):
                kind, h, i = UNITS[u]
                dve.wait_ge(sem("pv_done"), u + 1)
                if kind == "mem":
                    dst, src = g.y_mem[:, h, i * P:(i + 1) * P], bank(1)[:, 0:P]
                else:
                    r = slice(64 * (h % 2), 64 * (h % 2) + 64)
                    dst, src = g.y_dil[r, h // 2, i * P:(i + 1) * P], bank(1)[r, 0:P]
                nc.vector.tensor_copy(dst, src).then_inc(sem("attended"), 1)

            for u, unit in enumerate(UNITS):
                n = unit_keys(unit)
                sc = g.sc2[:, u % 2, 0:n]
                pb = 2 + 2 * (u % 2)
                dve.wait_ge(sem("scored"), u + 1)
                if u >= 2:
                    dve.wait_ge(sem("probs_turned"), u - 1)
                if unit[0] == "mem":
                    own.link(nc.vector.tensor_copy(sc, bank(pb, 2)[:, 0:n]))
                    scale = float(P) ** -0.5
                else:
                    w = n // 3
                    own.link(tt(cut(sc, g=3), bank(pb, 2)[:, 0:3 * SEQ].rearrange("p (g n) -> p g n", g=3)[:, :, 0:w],
                                g.amask[:, :, SEQ - w:SEQ], ALU.add))
                    scale = float(HD) ** -0.5
                s = g.stat[:, 16 + 4 * (u % 2):20 + 4 * (u % 2)]
                own.link(nc.vector.tensor_reduce(out=s[:, 0:1], in_=sc, axis=AX, op=ALU.max))
                ts(s[:, 1:2], s[:, 0:1], -scale, None, ALU.mult).then_inc(sem("max_set"), 1)
                dve.wait_ge(sem("exp_set"), u + 1)
                own.link(nc.vector.reciprocal(s[:, 3:4], s[:, 2:3]))
                ts(sc, sc, s[:, 3:4], None, ALU.mult).then_inc(sem("probs_set"), 1)
                if u:
                    attention_out(u - 1)
            attention_out(len(UNITS) - 1)

            nc.vector.memset(g.S_hist[:, 0], 0.0)
            for r in range(4):
                for u in (2 * r, 2 * r + 1):
                    e, i, hp = u % 2, u // 4, u % 4
                    b = 2 + 3 * e
                    dve.wait_ge(sem("grams_done"), u + 1)
                    if r == 0 and e == 0:
                        dve.wait_ge(sem("tok_out"), 8)
                    w = bank(b).rearrange("p (q j n) -> p q j n", q=2, j=2)
                    v = bank(b + 2).rearrange("p (q n) -> p q n", q=2)
                    qxn = g.qxn4[:, e]
                    m2 = lambda k: k.unsqueeze(1).broadcast_to([P, 2, P])
                    pr = 8 * i + 2 * hp
                    own.link(tt(qxn[:, :, 0], w[:, :, 0], m2(g.mask_s), ALU.mult))
                    tt(qxn[:, :, 1], w[:, :, 1], m2(g.mask_l), ALU.mult)
                    tt(g.mrb[:, pr:pr + 2], bank(b + 1)[:, 0:2 * P].rearrange("p (q n) -> p q n", q=2),
                       m2(g.mask_i), ALU.mult)
                    tt(g.xx4[:, e], qxn[:, :, 0], m2(ident), ALU.add)
                    tt(g.ak4[:, e], v[:, :, 0:P], m2(g.mask_s), ALU.mult)
                    tt(g.rk4[:, e], v[:, :, P:2 * P], m2(g.mask_i), ALU.mult).then_inc(sem("grams_out"), 1)
                for lv in range(1, LEVELS):
                    for u in (2 * r, 2 * r + 1):
                        e = u % 2
                        dve.wait_ge(sem("level_done"), 2 * LEVELS * r + 2 * lv + e + 1)
                        tt(g.xx4[:, e], g.xx4[:, e], bank(3 + 3 * e)[:, 0:2 * P].rearrange("p (q n) -> p q n", q=2),
                           ALU.add) \
                            .then_inc(sem("x_updated"), 1)
                for u in (2 * r, 2 * r + 1):
                    e, i, hp = u % 2, u // 4, u % 4
                    o = bank(4 + 3 * e)
                    dve.wait_ge(sem("mv_done"), u + 1)
                    nc.vector.tensor_copy(g.mv2[:, e], o[:, 0:P].rearrange("p (q n) -> p q n", q=2)) \
                        .then_inc(sem("mv_out"), 1)
                    dve.wait_ge(sem("wz_done"), u + 1)
                    nc.vector.tensor_copy(g.Zt[:, i, hp * P:(hp + 1) * P], o[:, P:2 * P])
                    nc.vector.tensor_copy(g.WT[:, hp, i * P:(i + 1) * P], o[:, 2 * P:3 * P])
                    nc.vector.tensor_copy(g.Y0[:, hp, i * P:(i + 1) * P], o[:, 3 * P:4 * P]) \
                        .then_inc(sem("wz_out"), 1)
            for c in range(NCH):
                i, cb = c // 2, L * (c % 2)
                if c == 0:
                    dve.wait_ge(sem("wz_out"), 8)
                    nc.vector.tensor_copy(g.U[0:L, 0], g.Zt[0:L, 0]).then_inc(sem("u_set"), 1)
                else:
                    dve.wait_ge(sem("u_done"), c)
                    tt(g.U[cb:cb + L, i], bank(2)[cb:cb + L, :], g.Zt[cb:cb + L, i], ALU.add) \
                        .then_inc(sem("u_set"), 1)
                if c == NCH - 1:
                    break
                dve.wait_ge(sem("s_done"), c + 1)
                s1 = g.S_hist[:, c + 1].rearrange("p (k n) -> p k n", k=4)
                own.link(tt(g.S_hist[:, c + 1], bank(3)[:, 0:256], g.S_hist[:, c], ALU.add))
                tt(s1, s1, g.p_last[:, :, c:c + 1].broadcast_to([P, 4, HD]), ALU.mult) \
                    .then_inc(sem("s_set"), 1)
                dve.wait_ge(sem("s_set"), c + 1)
            Y = g.Y0
            for i in range(NT):
                dve.wait_ge(sem("y_done"), i + 1)
                own.link(tt(Y[:, :, i * P:(i + 1) * P], Y[:, :, i * P:(i + 1) * P],
                            bank(4 + i).rearrange("p (k n) -> p k n", k=4), ALU.add))
            dve.wait_ge(sem("dve_steps"), own.n)
            nc.vector.tensor_copy(g.y_rwkv, Y).then_inc(sem("y_summand"), 1)
            for q in range(2):
                dve.wait_ge(sem("y_summed"), q + 1)
                own.link(stt(g.y_rwkv[:, 2 * q:2 * q + 2], cut(bank(6 + q), k=2), -1.0 / HD,
                             Y[:, 2 * q:2 * q + 2], ALU.mult, ALU.add))
            tt(g.rT, g.y_rwkv, g.y_rwkv, ALU.mult).then_inc(sem("y_squared"), 1)

            def mix_out(q):
                gb, first = MIX[q]
                t = (g.rT, g.kT)[q % 2]
                dve.wait_ge(sem("mix_done"), q + 1)
                if q == 0:
                    dve.wait_ge(sem("gates_out"), C_PMEM - C_GATE)
                    dve.wait_ge(sem("raw_gates_set"), 1)
                dst = hT[:, first:first + 4]
                w = cut(bank(2 + 2 * (q % 2), 2), k=4)
                gates = g.gates[:, 8 * gb + first:8 * gb + first + 4]
                if gb == 2:
                    tt(dst, w, gates, ALU.mult).then_inc(sem("mix_out"), 1)
                else:
                    tt(t, w, gates, ALU.mult).then_inc(sem("mix_out"), 1)
                    dve.wait_ge(sem("mix_out"), q + 1)
                    tt(dst, dst, t, ALU.add).then_inc(sem("mixed"), 1)

            mix_out(0)
            dve.wait_ge(sem("y_root"), 1)
            own.link(tt(g.y_rwkv, g.y_rwkv, g.kT, ALU.mult))
            own.link(tt(g.y_rwkv, g.y_rwkv, bc(param("rwkv_ln_w"), SEQ), ALU.mult))
            own.link(tt(g.y_rwkv, g.y_rwkv, bc(param("rwkv_ln_b"), SEQ), ALU.add))
            own.link(tt(g.y_rwkv, g.y_rwkv, g.dec, ALU.add))
            tt(g.y_rwkv, g.y_rwkv, g.gT, ALU.mult).then_inc(sem("y_rwkv_set"), 1)

            for q in range(1, len(MIX)):
                mix_out(q)
            for q in range(4):
                dve.wait_ge(sem("out_done"), q + 1)
                tt(x[:, :, q * CW:(q + 1) * CW], x[:, :, q * CW:(q + 1) * CW],
                   bank(q % 2).rearrange("p (i n) -> p i n", i=2), ALU.add).then_inc(sem("x2_set"), 1)

        @block.scalar
        def _(act):
            own = Own(act, sem("act_steps"))
            load_rows(act, list(ROWS)[POOL_ROWS:], "rows_in")
            act.wait_ge(sem("eps_set"), 1)

            def mean_square(k, src):
                for i in range(NT):
                    own.link(nc.scalar.activation(g.sq, src[:, i], ACT.Square,
                                                  accum_out=g.stat[:, 2 * k + i:2 * k + i + 1]))
                nc.scalar.activation(g.stat[:, 4 + 4 * k:6 + 4 * k], g.stat[:, 2 * k:2 * k + 2], ACT.Sqrt,
                                     bias=g.eps_norm, scale=1.0 / D).then_inc(sem("root_set"), 1)

            act.wait_ge(sem("x_in"), 16)
            mean_square(0, x)
            act.wait_ge(sem("cols_turned"), 1)
            nc.scalar.activation(cols[:, 0:NROWS], bank(7)[:, 0:NROWS], ACT.Copy).then_inc(sem("cols_set"), 1)
            act.wait_ge(sem("x_turned"), 4)
            zero = g.stat[:, 63:64].unsqueeze(2).broadcast_to([P, 14, 1])
            own.link(nc.scalar.activation(g.Zraw[:, :, 0:1], zero, ACT.Copy))
            act.wait_ge(sem("mem_in"), 16)
            mean_square(1, g.memx)

            def evacuate(n, dst, func=ACT.Copy):
                act.wait_ge(sem("proj_done"), n + 1)
                w = bank(n % 2).rearrange("p (q n) -> p q n", q=2)
                return nc.scalar.activation(dst, w, func)

            for n in range(C_QK):
                evacuate(n, g.Zraw[:, 2 * n:2 * n + 2, 1:257]).then_inc(sem("z_out"), 1)
            act.wait_ge(sem("shifted"), 4)
            nc.scalar.activation(g.lora[0:64, 0], g.lora[0:64, 0], ACT.Tanh)
            nc.scalar.activation(g.lora[:, 1], g.lora[:, 1], ACT.Sigmoid).then_inc(sem("lora_set"), 1)
            for n in range(C_QK, C_QK + 2):
                evacuate(n, g.qk[:, 2 * (n - C_QK):2 * (n - C_QK) + 2]).then_inc(sem("dil_out"), 1)
            act.wait_ge(sem("lora_done"), 1)
            for k in range(4):
                own.link(nc.scalar.activation(g.tmp[:, k], bank(2, 2)[:, k * SEQ:(k + 1) * SEQ], ACT.Sigmoid,
                                              bias=param("rwkv_w0")[:, k:k + 1]))
            for k in range(4):
                ins = nc.scalar.activation(g.aT[:, k], bank(4, 2)[:, k * SEQ:(k + 1) * SEQ], ACT.Sigmoid,
                                           bias=param("rwkv_a0")[:, k:k + 1])
            ins.then_inc(sem("a_set"), 1)
            nc.scalar.activation(g.gT, cut(bank(6, 2), k=4), ACT.Copy).then_inc(sem("g_out"), 1)
            nc.scalar.activation(g.tmp, g.tmp, ACT.Exp, scale=-float(np.exp(-0.5))).then_inc(sem("decay_set"), 1)
            act.wait_ge(sem("kk_sum_out"), 2)
            nc.scalar.activation(g.t1, g.t1, ACT.Sqrt).then_inc(sem("kk_root"), 1)

            def qk_root(q):
                root = (g.t2, g.tmp)[q % 2]
                act.wait_ge(sem("qk_summed"), q + 1)
                if q >= 2:
                    act.wait_ge(sem("qk_normed"), q - 1)
                nc.scalar.activation(root, cut(bank(2 + 2 * (q % 2), 2), k=4), ACT.Sqrt, bias=g.eps_norm,
                                     scale=1.0 / (HD if NORM_GROUPS[q][0] == "qk" else P)).then_inc(sem("qk_root"), 1)

            for n in range(C_QK + 2, C_GATE):
                if n < C_V:
                    ins = evacuate(n, g.qk[:, 2 * (n - C_QK):2 * (n - C_QK) + 2])
                elif n < C_MQ:
                    ins = evacuate(n, g.vtok[:, :, (n - C_V) * CW:(n - C_V + 1) * CW])
                elif n < C_MK:
                    ins = evacuate(n, g.mq[:, 2 * (n - C_MQ):2 * (n - C_MQ) + 2])
                elif n < C_MV:
                    ins = evacuate(n, g.mk[:, 2 * (n - C_MK):2 * (n - C_MK) + 2])
                else:
                    ins = evacuate(n, g.mv[:, :, (n - C_MV) * CW:(n - C_MV + 1) * CW])
                ins.then_inc(sem("dil_out"), 1)
                for q in NORM_AT.get(n + 1, ()):
                    qk_root(q)
            def gates_out(place, func):
                for n, quarter in gate_quarters(place):
                    if quarter == 3:
                        act.wait_ge(sem("proj_done"), C_GATE + n + 1)
                        nc.scalar.activation(g.gates[:, 2 * n:2 * n + 2], cut(bank(0), q=2), func) \
                            .then_inc(sem("gates_out"), 1)

            gates_out(("norms", 0), ACT.Copy)
            for u, unit in enumerate(UNITS):
                n = unit_keys(unit)
                sc = g.sc2[:, u % 2, 0:n]
                s = g.stat[:, 16 + 4 * (u % 2):20 + 4 * (u % 2)]
                scale = float(P if unit[0] == "mem" else HD) ** -0.5
                act.wait_ge(sem("max_set"), u + 1)
                nc.scalar.activation(sc, sc, ACT.Exp, bias=s[:, 1:2], scale=scale, accum_out=s[:, 2:3]) \
                    .then_inc(sem("exp_set"), 1)
                act.wait_ge(sem("probs_turned"), u + 1)
                if u >= 2:
                    act.wait_ge(sem("pv_done"), u - 1)
                nc.scalar.activation(g.pt2[:, u % 2, 0:n], bank(6, 2)[:, 0:n], ACT.Copy) \
                    .then_inc(sem("pt_set"), 1)
                for place in range(2):
                    gates_out(("attention", u, place), ACT.Copy)
            for q in range(4):
                for i in range(NT):
                    n = 2 * q + i
                    act.wait_ge(sem("tok_turned"), n + 1)
                    act.wait_ge(sem("attended"), len(UNITS))
                    nc.scalar.activation((g.tok_a, g.tok_b, g.tok_k, g.tok_v)[q][:, i], bank(2 + n % 2), ACT.Copy) \
                        .then_inc(sem("tok_out"), 1)

            act.wait_ge(sem("gates_out"), RAW_GATES)
            nc.scalar.activation(g.gates[:, 0:2 * RAW_GATES], g.gates[:, 0:2 * RAW_GATES], ACT.Sigmoid) \
                .then_inc(sem("raw_gates_set"), 1)
            for r in range(4):
                for lv in range(LEVELS - 1):
                    for u in (2 * r, 2 * r + 1):
                        e = u % 2
                        act.wait_ge(sem("level_done"), 2 * LEVELS * r + 2 * lv + e + 1)
                        nc.scalar.activation(g.qxn4[:, e].rearrange("p q j n -> p (q j n)"), bank(2 + 3 * e), ACT.Copy) \
                            .then_inc(sem("q_updated"), 1)
                    gates_out(("level", r, lv), ACT.Sigmoid)
            for c in range(NCH):
                gates_out(("chain", c), ACT.Sigmoid)
            act.wait_ge(sem("var_done"), 1)
            own.link(nc.scalar.activation(g.kT, cut(bank(6, 2), k=4), ACT.Ln, bias=g.eps_gn, scale=1.0 / HD))
            nc.scalar.activation(g.kT, g.kT, ACT.Exp, scale=-0.5).then_inc(sem("y_root"), 1)

        @block.tensor
        def _(pe):
            mm, tr = nc.tensor.matmul, nc.tensor.transpose

            turns = [0]

            def row_tile_done(instruction):
                turns[0] += 1
                instruction.then_inc(sem("row_tile_done"), 1)
                pe.wait_ge(sem("row_tile_done"), turns[0])

            def load_wait(n):
                pe.wait_ge(g.arrived[(FIRST + n) % LO], 16 * g.nth(n))

            pe.wait_ge(sem("ident_set"), 1)
            wait_rows(pe)
            tr(bank(7)[:, 0:NROWS], g.prow, ident[0:NROWS, 0:NROWS]).then_inc(sem("cols_turned"), 1)
            def turn_rows(name, row, first):
                for q in range(4):
                    if q >= 2:
                        pe.wait_ge(sem(name + "_turned_out"), q - 1)
                    for kk in range(2):
                        for i in range(NT):
                            if q == 0 and kk == 0:
                                pe.wait_ge(sem(name + "_normed"), i + 1)
                            ins = tr(bank(first + q % 2)[:, kk * SEQ + i * P:kk * SEQ + (i + 1) * P],
                                     row[:, i, (2 * q + kk) * P:(2 * q + kk + 1) * P], ident)
                    ins.then_inc(sem(name + "_turned"), 1)

            turn_rows("x", cut(g.zs[:, 0:NT * D], i=NT), 0)
            pe.wait_ge(sem("x_turned_out"), 4)

            def project(n, src, token_major=False):
                load_wait(n)
                w = cut(g.ring(n), k=KD)
                if 2 <= n < C_QK:
                    pe.wait_ge(sem("z_out"), n - 1)
                elif C_QK <= n < C_QK + 2:
                    pe.wait_ge(sem("z_out"), n - 1)
                elif n >= C_QK + 2:
                    pe.wait_ge(sem("dil_out"), n - 1 - C_QK)
                for q in range(2):
                    o = bank(n % 2)[:, q * SEQ:(q + 1) * SEQ]
                    for k in range(KD):
                        if token_major:
                            ins = mm(o, src[:, k, q * P:(q + 1) * P], w[:, k, :], start=(k == 0), stop=(k == KD - 1))
                        else:
                            ins = mm(o, w[:, k, q * P:(q + 1) * P], src[:, k, :], start=(k == 0), stop=(k == KD - 1))
                ins.then_inc(sem("proj_done"), 1)

            for n in range(C_QK + 2):
                project(n, hT)
                if n == 1:
                    turn_rows("mem", g.memx, 2)
            pe.wait_ge(sem("mem_turned_out"), 4)
            pe.wait_ge(sem("lora_set"), 1)
            pe.wait_ge(sem("lora_in"), 48)
            for k in range(4):
                c = slice(k * P, (k + 1) * P)
                o = slice(k * SEQ, (k + 1) * SEQ)
                mm(bank(2, 2)[:, o], g.lw2[0:64, c], g.lora[0:64, 0], start=True, stop=True)
                mm(bank(4, 2)[:, o], g.lw2[64:128, c], g.lora[64:128, 0], start=True, stop=True)
                ins = mm(bank(6, 2)[:, o], g.lg2[:, c], g.lora[:, 1], start=True, stop=True)
            ins.then_inc(sem("lora_done"), 1)
            project(C_QK + 2, hT)
            pe.wait_ge(sem("g_out"), 1)
            pe.wait_ge(sem("kk_squared"), 1)
            for q in range(2):
                mm(bank(6 + q), g.head_ones, g.t1[:, 2 * q:2 * q + 2], start=True, stop=True) \
                    .then_inc(sem("kk_summed"), 1)
            def sum_squares(q):
                pe.wait_ge(sem("squared"), q + 1)
                if q >= 2:
                    pe.wait_ge(sem("qk_root"), q - 1)
                squares = (g.t1, g.t3)[q % 2]
                for h in range(2):
                    ins = mm(bank(2 + 2 * (q % 2) + h), g.head_ones if NORM_GROUPS[q][0] == "qk" else g.ones,
                             squares[:, 2 * h:2 * h + 2], start=True, stop=True)
                ins.then_inc(sem("qk_summed"), 1)

            for n in range(C_QK + 3, C_GATE):
                project(n, hT if n < C_MK else g.memT, C_V <= n < C_MQ or n >= C_MV)
                if n + 1 == C_MQ:
                    pe.wait_ge(sem("rk_set"), 1)
                    pe.wait_ge(sem("kk_sum_out"), 2)
                    for q in range(2):
                        mm(bank(6 + q), g.head_ones, g.t2[:, 2 * q:2 * q + 2], start=True, stop=True) \
                            .then_inc(sem("rk_summed"), 1)
                for q in NORM_AT.get(n + 1, ()):
                    sum_squares(q)

            def gate(place):
                for n, quarter in gate_quarters(place):
                    if quarter == 0:
                        load_wait(C_GATE + n)
                        if n == 0:
                            pe.wait_ge(sem("dil_out"), C_GATE - C_QK)
                        else:
                            pe.wait_ge(sem("gates_out"), n)
                    w = cut(g.ring(C_GATE + n), k=KD)
                    q, k0 = quarter // 2, KD // 2 * (quarter % 2)
                    for k in range(k0, k0 + KD // 2):
                        ins = mm(bank(0)[:, q * SEQ:(q + 1) * SEQ], w[:, k, q * P:(q + 1) * P], hT[:, k],
                                 start=(k == 0), stop=(k == KD - 1))
                    if quarter == 3:
                        ins.then_inc(sem("proj_done"), 1)

            def scores(u):
                kind, h, i = UNITS[u]
                if u < 2:
                    pe.wait_ge(sem("qk_normed"), len(NORM_GROUPS))
                else:
                    pe.wait_ge(sem("max_set"), u - 1)
                pb = 2 + 2 * (u % 2)
                if kind == "mem":
                    ins = mm(bank(pb)[:, 0:SEQ], g.mq[:, h, i * P:(i + 1) * P], g.mk[:, h], start=True, stop=True)
                else:
                    w = P * (i + 1)
                    for gr in range(DG):
                        gh = gr * DH + h
                        r = slice(64 * (gh % 2), 64 * (gh % 2) + 64)
                        ins = mm(bank(pb, 2)[:, gr * SEQ:gr * SEQ + w], g.qk[r, gh // 2, i * P:(i + 1) * P],
                                 g.qk[r, 6 + gh // 2, 0:w], start=True, stop=True)
                ins.then_inc(sem("scored"), 1)

            def attend(u):
                kind, h, i = UNITS[u]
                blocks = unit_keys(UNITS[u]) // P
                pe.wait_ge(sem("probs_set"), u + 1)
                if u == 0:
                    pe.wait_ge(sem("tildes_set"), 1)
                else:
                    pe.wait_ge(sem("pt_set"), u)
                for b in range(blocks):
                    ins = tr(bank(6, 2)[:, b * P:(b + 1) * P], g.sc2[:, u % 2, b * P:(b + 1) * P], ident)
                ins.then_inc(sem("probs_turned"), 1)
                gate(("attention", u, 1))
                pe.wait_ge(sem("pt_set"), u + 1)
                if u:
                    pe.wait_ge(sem("attended"), u)
                else:
                    pe.wait_ge(sem("dil_out"), C_GATE - C_QK)
                o = bank(1)
                for b in range(blocks):
                    if kind == "mem":
                        ins = mm(o[:, 0:P], g.mv[:, b, h * P:(h + 1) * P], g.pt2[:, u % 2, b * P:(b + 1) * P],
                                 start=(b == 0), stop=(b == blocks - 1))
                    else:
                        gr, kt = b // (i + 1), b % (i + 1)
                        gh = gr * DH + h
                        ins = mm(o[64 * (h % 2):64 * (h % 2) + 64, 0:P], g.vtok[:, kt, gh * HD:(gh + 1) * HD],
                                 g.pt2[:, u % 2, b * P:(b + 1) * P], start=(b == 0), stop=(b == blocks - 1))
                ins.then_inc(sem("pv_done"), 1)

            gate(("norms", 0))
            scores(0)
            for u in range(len(UNITS)):
                if u + 1 < len(UNITS):
                    scores(u + 1)
                gate(("attention", u, 0))
                attend(u)
            pe.wait_ge(sem("attended"), len(UNITS))
            for q, src in enumerate((g.kkT, g.aT, g.kT, g.vT)):
                for i in range(NT):
                    n = 2 * q + i
                    if n >= 2:
                        pe.wait_ge(sem("tok_out"), n - 1)
                    for k in range(4):
                        ins = tr(bank(2 + n % 2)[:, k * P:(k + 1) * P], src[:, k, i * P:(i + 1) * P], ident)
                    ins.then_inc(sem("tok_turned"), 1)
            pe.wait_ge(sem("tok_out"), 8)
            rows = (slice(0, 64), slice(64, 128))
            for r in range(4):
                units = (2 * r, 2 * r + 1)
                for u in units:
                    e, i, hp = u % 2, u // 4, u % 4
                    b = 2 + 3 * e
                    if u >= 2:
                        pe.wait_ge(sem("wz_out"), u - 1)
                    t = slice(i * P, (i + 1) * P)
                    for q in range(2):
                        A, B, K, R = (v[rows[q], hp, t] for v in (g.kkT, g.aT, g.kT, g.rT))
                        o, o2 = (bank(k)[:, q * SEQ:(q + 1) * SEQ] for k in (b, b + 2))
                        mm(o[:, 0:P], B, A, start=True, stop=True)
                        mm(o[:, P:2 * P], A, B, start=True, stop=True)
                        mm(bank(b + 1)[:, q * P:(q + 1) * P], B, R, start=True, stop=True)
                        mm(o2[:, 0:P], K, A, start=True, stop=True)
                        ins = mm(o2[:, P:2 * P], K, R, start=True, stop=True)
                        if q == 0:
                            row_tile_done(ins)
                    ins.then_inc(sem("grams_done"), 1)
                for lv in range(LEVELS):
                    for u in units:
                        e = u % 2
                        b = 2 + 3 * e
                        if lv == 0:
                            pe.wait_ge(sem("grams_out"), u + 1)
                        else:
                            pe.wait_ge(sem("q_updated"), 2 * (LEVELS - 1) * r + 2 * (lv - 1) + e + 1)
                        if lv > 1:
                            pe.wait_ge(sem("x_updated"), 2 * (LEVELS - 1) * r + 2 * (lv - 2) + e + 1)
                        for q in range(2):
                            Q, N = (g.qxn4[:, e, q, j] for j in range(2))
                            o = bank(b)[:, q * SEQ:(q + 1) * SEQ]
                            if lv < LEVELS - 1:
                                mm(o[:, 0:P], N, Q, start=True, stop=True)
                                ins = mm(o[:, P:2 * P], Q, N, start=True, stop=True)
                            if lv:
                                ins = mm(bank(b + 1)[:, q * P:(q + 1) * P], N, g.xx4[:, e, q], start=True, stop=True)
                        ins.then_inc(sem("level_done"), 1)
                    if lv < LEVELS - 1:
                        gate(("level", r, lv))
                for u in units:
                    e, i, hp = u % 2, u // 4, u % 4
                    o = bank(4 + 3 * e)
                    for q in range(2):
                        hc = slice((2 * hp + q) * HD, (2 * hp + q + 1) * HD)
                        ins = mm(o[:, q * HD:(q + 1) * HD], g.ak4[:, e, q], g.tok_v[:, i, hc], start=True, stop=True)
                    ins.then_inc(sem("mv_done"), 1)
                for u in units:
                    e, i, hp = u % 2, u // 4, u % 4
                    o = bank(4 + 3 * e)
                    pe.wait_ge(sem("mv_out"), u + 1)
                    pe.wait_ge(sem("x_updated"), 2 * (LEVELS - 1) * r + 2 * (LEVELS - 2) + e + 1)
                    for q in range(2):
                        hc = slice((2 * hp + q) * HD, (2 * hp + q + 1) * HD)
                        X = g.xx4[:, e, q]
                        mm(o[:, P + q * HD:P + (q + 1) * HD], X, g.mv2[:, e, q], start=True, stop=True)
                        mm(o[rows[q], 2 * P:3 * P], g.tok_a[:, i, hc], X, start=True, stop=True)
                        ins = mm(o[rows[q], 3 * P:4 * P], g.tok_v[:, i, hc], g.rk4[:, e, q], start=True, stop=True)
                    ins.then_inc(sem("wz_done"), 1)
            pe.wait_ge(sem("wz_out"), 8)
            for c in range(NCH):
                i, cb = c // 2, L * (c % 2)
                cr, ct = slice(cb, cb + L), slice(c * L, (c + 1) * L)
                if c:
                    pe.wait_ge(sem("s_set"), c)
                    for h in (0, 2, 4, 6, 1, 3, 5, 7):
                        q, hp = h % 2, h // 2
                        ins = mm(bank(2)[cr, h * HD:(h + 1) * HD], g.WT[rows[q], hp, ct],
                                 g.S_hist[rows[q], c, hp * HD:(hp + 1) * HD], start=True, stop=True)
                        if h == 6:
                            row_tile_done(ins)
                    ins.then_inc(sem("u_done"), 1)
                gate(("chain", c))
                pe.wait_ge(sem("u_set"), c + 1)
                for h in range(RH) if c < NCH - 1 else ():
                    q, hp = h % 2, h // 2
                    hc = slice(h * HD, (h + 1) * HD)
                    o = bank(3)[rows[q], hp * HD:(hp + 1) * HD]
                    mm(o, g.tok_b[cr, i, hc], g.U[cr, i, hc], start=True, stop=False)
                    ins = mm(o, g.tok_k[cr, i, hc], g.tok_v[cr, i, hc], start=False, stop=True)
                    if h == RH - 1:
                        ins.then_inc(sem("s_done"), 1)
            for i in range(NT):
                for h in range(RH):
                    q, hp = h % 2, h // 2
                    ins = mm(bank(4 + i)[rows[q], hp * P:(hp + 1) * P], g.U[:, i, h * HD:(h + 1) * HD],
                             g.mrb[:, 8 * i + h], start=(h < 2), stop=False, skip_group_check=True)
                row_tile_done(ins)
                for h in (0, 2, 4, 6, 1, 3, 5, 7):
                    q, hp = h % 2, h // 2
                    for c in (2 * i, 2 * i + 1):
                        at = hp * P + (c % 2) * L
                        ins = mm(bank(4 + i)[rows[q], at:at + L], g.S_hist[rows[q], c, hp * HD:(hp + 1) * HD],
                                 g.rT[rows[q], hp, c * L:(c + 1) * L], start=False, stop=True, skip_group_check=True)
                    if h == 6:
                        row_tile_done(ins)
                ins.then_inc(sem("y_done"), 1)
            pe.wait_ge(sem("y_summand"), 1)
            for q in range(2):
                mm(bank(6 + q), g.head_ones, g.y_rwkv[:, 2 * q:2 * q + 2], start=True, stop=True) \
                    .then_inc(sem("y_summed"), 1)

            def mix(q):
                gb, first = MIX[q]
                n, kn = MIX_CHUNKS[q]
                if first == 0 or n != MIX_CHUNKS[q - 1][0]:
                    load_wait(n)
                w = cut(g.ring(n), k=kn)
                if q >= 2:
                    pe.wait_ge(sem("mix_out"), q - 1)
                if gb == 0 and first == 0:
                    pe.wait_ge(sem("y_rwkv_set"), 1)
                yt = (g.y_rwkv, g.y_dil, g.y_mem)[gb]
                wm = 0 if w.shape[2] == 512 else first
                for mt in range(4):
                    o = bank(2 + 2 * (q % 2), 2)[:, mt * SEQ:(mt + 1) * SEQ]
                    for k in range(kn):
                        ins = mm(o, w[:, k, (wm + mt) * P:(wm + mt + 1) * P], yt[:, k], start=(k == 0),
                                 stop=(k == kn - 1))
                ins.then_inc(sem("mix_done"), 1)

            mix(0)
            pe.wait_ge(sem("y_squared"), 1)
            for q in range(2):
                ins = mm(bank(6 + q), g.head_ones, g.rT[:, 2 * q:2 * q + 2], start=True, stop=True)
            ins.then_inc(sem("var_done"), 1)
            for q in range(1, len(MIX)):
                mix(q)
            pe.wait_ge(sem("mixed"), 4)
            for q in range(4):
                n = C_OUT + q
                load_wait(n)
                w = cut(g.ring(n), k=KD)
                if q >= 2:
                    pe.wait_ge(sem("x2_set"), q - 1)
                for i in range(NT):
                    for k in range(KD):
                        ins = mm(bank(q % 2)[:, i * CW:(i + 1) * CW], hT[:, k, i * P:(i + 1) * P], w[:, k],
                                 start=(k == 0), stop=(k == KD - 1))
                ins.then_inc(sem("out_done"), 1)


def expert_chunk(a, e, j):
    w, q = (a["w1"], j // 2) if j < W1C else (a["w2"], (j - W1C) // 2)
    return w[0][e, j % 2 * EW:(j % 2 + 1) * EW, q * EW:(q + 1) * EW]


def moe_memory(nc, ctx, g):
    def tensor(name, *shape, dtype=F32):
        return ctx.enter_context(nc.sbuf_tensor(name, [P] + list(shape), dtype))[(slice(None),) * (1 + len(shape))]

    g.w_high = tensor("w_high", DEPTH, 2048, dtype=F32R)
    g.w_low = tensor("w_low", DEPTH, 2048, dtype=F32R)
    g.x_parts = tensor("x_parts", KD, 2 * CAP, dtype=F32R)
    g.a_parts = tensor("a_parts", KD, 2 * CAP, dtype=F32R)
    g.xn_parts = [tensor(f"xn_part{n}", NT, D, dtype=BF16) for n in range(3)]
    g.xn_rest = tensor("xn_rest", NT, D)
    g.sel = tensor("sel", NT, CAP, dtype=BF16)
    g.selg = tensor("selg", NT, 2 * CAP)
    g.selT = tensor("selT", SEQ)
    g.fold = tensor("fold", P)
    g.b1_parts = tensor("b1_parts", 2 * FF, dtype=F32R)
    g.pick = tensor("pick", E)
    g.picked = tensor("picked", CAP, dtype=F32R)
    g.posj = tensor("posj", NT, NJ * E)
    g.gate = tensor("gate", NT, NJ * E)
    g.chosen = tensor("chosen", NT, (NJ - 1) * E)
    g.order_i = tensor("order_i", 64, dtype=mybir.dt.int32)
    g.slot_no = tensor("slot_no", 2 * CAP)
    g.before = tensor("before", P)
    g.small = tensor("small", 256)
    w = tensor("scratch", 5120 + KD * E)
    g.xnT = g.cut(w[:, 0:KD * SEQ], k=KD)
    g.b1raw, g.b2raw, g.wr = w[:, 2048:4096], w[:, 4096:5120], w[:, 5120:5120 + KD * E]
    g.gateT = w[0:E, 1536:1792]
    g.hot = w[:, 0:NT * TOPK * E].rearrange("p (i k e) -> p i k e", i=NT, k=TOPK)
    g.hsb = w[:, 0:1024].rearrange("p (u n) -> p u n", u=2)
    g.ye = w[:, 4096:5120]
    g.hg, g.hl, g.hs, g.ha = (w[:, 1024 + 128 * q:1152 + 128 * q].rearrange("p (t n) -> p t n", t=2)
                              for q in range(4))
    g.xn = g.hT.rearrange("p k n -> p (k n)").rearrange("p (i n) -> p i n", i=NT)


def moe(nc, a, out, g):
    sem, bank, cut, param = g.sem, g.bank, g.cut, g.param
    x, ident = g.x, g.ident
    whole = g.part is None
    OWN = 8
    FREED = DEPTH + 1

    slots = [g.ring_lo[:, c % LO] for c in range(CHUNKS)]
    filled = [g.lo_loads[c % LO] if whole else 0 for c in range(CHUNKS)]
    posj, gate, small = g.posj, g.gate, g.small
    logit, top8, tif, eio = (small[:, 0:64].rearrange("p (i e) -> p i e", i=NT),
                             small[:, 64:80].rearrange("p (i e) -> p i e", i=NT),
                             small[:, 80:96].rearrange("p (i e) -> p i e", i=NT), small[:, 96:128])
    oh, rsc, brow = small[:, 128:192], small[:, 192:224], small[0:1, 224:256]
    R = E * (NJ - 1)

    def w_source(e, j):
        return expert_chunk(a, bass.ds(e, 1), j).rearrange("o (k p) n -> p (o k) n", p=P)

    def further_blocks(engine):
        engine.wait_ge(sem("order_set"), 1)
        return engine.value_load(g.order_i[0:1, 40:41], min_val=0, max_val=MAX_OVER)

    def further_column(engine, r):
        return engine.value_load(g.order_i[0:1, bass.ds(r, 1)], min_val=0, max_val=NJ * E - 1)

    def further_expert(engine, r):
        return engine.value_load(g.order_i[0:1, bass.ds(r + 20, 1)], min_val=0, max_val=E - 1)

    with nc.Block() as block:
        @block.sync
        def _(sp):
            if not whole:
                sp.dma_start(x, a["x"][0].rearrange("(i p) n -> p i n", p=P)).then_inc(sem("x_in2"), 16)
                for j in range(LO):
                    sp.dma_start(cut(slots[j], k=EK), w_source(0, j)).then_inc(g.arrived[j], 16)

            def load_expert(b, e, first=0):
                for j in range(first, CHUNKS):
                    sp.wait_ge(sem("low_set"), CHUNKS * b + (j + 1 - LO))
                    sp.dma_start(cut(slots[j], k=EK), w_source(e, j)).then_inc(g.arrived[j % LO], 16)

            load_expert(0, 0, LO)
            with sp.Fori(1, E) as b:
                load_expert(b, b)
            count = further_blocks(sp)
            with sp.If(count > 0):
                with sp.Fori(0, count) as r:
                    load_expert(r + E, further_expert(sp, r))
            for i in range(NT):
                sp.wait_ge(sem("out_set"), i + 1)
                sp.dma_start(out[0][i * P:(i + 1) * P, :], x[:, i]).then_inc(sem("stored"), 16)
            sp.wait_ge(sem("stored"), 16 * NT)

        @block.gpsimd
        def _(pool):
            own = Own(pool, sem("pool_moe_steps"))
            pool.dma_start(cut(g.wr, k=KD), a["w_router"][0].rearrange("(k p) n -> p k n", p=P)) \
                .then_inc(sem("router_in"), 16)
            pool.dma_start(brow, a["b_router"]).then_inc(sem("router_in"), 16)
            for half in range(2):
                pool.dma_start(g.b1raw[half * E:(half + 1) * E, :], a["b1"][0]).then_inc(sem("b1_in"), 16)
            pool.dma_start(g.b2raw[0:E, :], a["b2"][0]).then_inc(sem("b_in"), 16)
            if not whole:
                pool.dma_start(g.ln2_row, a["ln2"].broadcast_to([P, D])).then_inc(sem("ln2_in"), 16)
                own.link(nc.gpsimd.memset(g.ones, 1.0))
                own.link(nc.gpsimd.memset(g.stat, 0.0))
                own.link(nc.gpsimd.memset(g.eps_norm, NORM_EPS))
                own.link(nc.gpsimd.memset(ident, 0.0))
                own.link(nc.gpsimd.affine_select(out=ident, in_=ident, compare_op=ALU.not_equal, fill=1.0, base=0,
                                                 pattern=[[-1, P]], channel_multiplier=1))
            own.link(nc.gpsimd.memset(g.before, 1.0))
            own.link(nc.gpsimd.affine_select(out=g.before, in_=g.before, compare_op=ALU.is_gt, fill=0.0, base=0,
                                             pattern=[[1, P]], channel_multiplier=-1))
            own.link(nc.gpsimd.iota(eio, pattern=[[1, E]], base=0, channel_multiplier=0,
                                    allow_small_or_imprecise_dtypes=True))
            own.link(nc.gpsimd.iota(g.slot_no, pattern=[[0, 2], [1, CAP]], base=0, channel_multiplier=0,
                                    allow_small_or_imprecise_dtypes=True))
            for j in range(1, NJ):
                own.link(nc.gpsimd.memset(rsc[E * (j - 1):E * j, 0:1], float(CAP * j)))
            own.link(nc.gpsimd.iota(rsc[0:R, 1:2], pattern=[[0, 1]], base=E, channel_multiplier=1,
                                    allow_small_or_imprecise_dtypes=True))
            nc.gpsimd.memset(g.selT, 0.0).then_inc(sem("selT_set"), 1)
            pool.wait_ge(sem("selT_set"), 1)
            own.link(nc.gpsimd.memset(g.order_i, 0))
            own.link(nc.gpsimd.memset(g.fold, 0.0))
            for shift in (-CAP, CAP):
                own.link(nc.gpsimd.affine_select(out=g.fold, in_=g.fold, compare_op=ALU.not_equal, fill=1.0,
                                                 base=shift, pattern=[[-1, P]], channel_multiplier=1))
            nc.gpsimd.affine_select(out=g.fold, in_=g.fold, compare_op=ALU.not_equal, fill=1.0, base=0,
                                    pattern=[[-1, P]], channel_multiplier=1).then_inc(sem("moe_consts"), 1)

        @block.vector
        def _(dve):
            own = Own(dve, sem("dve_moe_steps"))
            tt, ts, stt = nc.vector.tensor_tensor, nc.vector.tensor_scalar, nc.vector.scalar_tensor_tensor
            copy = nc.vector.tensor_copy

            dve.wait_ge(sem("ln2_in"), 16)
            dve.wait_ge(sem("root2_set"), 1)
            own.link(nc.vector.reciprocal(g.stat[:, 8:10], g.stat[:, 4:6]))
            for i in range(NT):
                stt(g.xn[:, i], x[:, i], g.stat[:, 8 + i:9 + i], g.ln2_row, ALU.mult, ALU.mult) \
                    .then_inc(sem("xn_set"), 1)
            dve.wait_ge(sem("xn_set"), 2)
            own.link(copy(g.xn_parts[0], g.xn))
            own.link(tt(g.xn_rest, g.xn, g.xn_parts[0], ALU.subtract))
            own.link(copy(g.xn_parts[1], g.xn_rest))
            own.link(tt(g.xn_parts[2], g.xn_rest, g.xn_parts[1], ALU.subtract))
            def low(b, c):
                dve.wait_ge(sem("high_set"), b * CHUNKS + (c + 1))
                tt(g.w_low[:, c % DEPTH, :], slots[c], g.w_high[:, c % DEPTH, :].bitcast(F32), ALU.subtract) \
                    .then_inc(sem("low_set"), 1)

            low(0, 0)
            low(0, 1)
            dve.wait_ge(sem("moe_consts"), 1)
            dve.wait_ge(sem("logits_done"), 1)
            own.link(copy(logit, bank(6)[:, 0:NT * E].rearrange("p (i e) -> p i e", i=NT)))
            ti = small[:, 240:256].rearrange("p (i e) -> p i e", i=NT).bitcast(mybir.dt.uint32)
            nc.vector.max(out=top8[:, 0], in_=logit[:, 0])
            own.link(nc.vector.max(out=top8[:, 1], in_=logit[:, 1]))
            nc.vector.max_index(ti[:, 0], top8[:, 0], logit[:, 0])
            own.link(nc.vector.max_index(ti[:, 1], top8[:, 1], logit[:, 1]))
            ts(g.stat[:, 20:22].unsqueeze(2), top8[:, :, 0:1], -1.0, None, ALU.mult).then_inc(sem("top_set"), 1)
            own.link(copy(tif, ti))

            def to_four(v):
                return v.broadcast_to([P, NT, TOPK, E])

            own.link(tt(g.hot, to_four(eio.unsqueeze(1).unsqueeze(1)), to_four(tif[:, :, 0:TOPK].unsqueeze(3)),
                        ALU.is_equal))
            by_j = lambda v: v.rearrange("p i (j e) -> p i j e", e=E)
            own.link(nc.vector.tensor_reduce(out=by_j(g.chosen)[:, :, 0], in_=g.hot.rearrange("p i k e -> p i e k"),
                                             axis=AX, op=ALU.add))
            dve.wait_ge(sem("top_exp"), 1)
            own.link(nc.vector.reciprocal(g.stat[:, 24:26], g.stat[:, 22:24]))
            own.link(tt(top8[:, :, 0:TOPK], top8[:, :, 0:TOPK],
                        g.stat[:, 24:26].unsqueeze(2).broadcast_to([P, NT, TOPK]), ALU.mult))
            own.link(tt(g.hot, g.hot, to_four(top8[:, :, 0:TOPK].unsqueeze(3)), ALU.mult))
            own.link(nc.vector.tensor_reduce(out=by_j(gate)[:, :, 0], in_=g.hot.rearrange("p i k e -> p i e k"),
                                             axis=AX, op=ALU.add))
            for v, n in ((g.chosen, NJ - 1), (gate, NJ)):
                ins = copy(by_j(v)[:, :, 1:n], by_j(v)[:, :, 0:1].broadcast_to([P, NT, n - 1, E]))
            ins.then_inc(sem("chosen_set"), 1)
            dve.wait_ge(sem("pos_done"), 1)
            own.link(stt(posj[:, :, 0:E], bank(6)[:, 64:64 + NT * E].rearrange("p (i e) -> p i e", i=NT), 1.0,
                         g.chosen[:, :, 0:E], ALU.add, ALU.mult))
            own.link(ts(posj[:, :, 0:E], posj[:, :, 0:E], -1.0, None, ALU.add))
            for j in range(1, NJ):
                ins = ts(posj[:, :, E * j:E * j + E], posj[:, :, 0:E], -float(CAP * j), None, ALU.add)
            own.link(ins)

            def select(column):
                for i in range(NT):
                    ins = ts(g.sel[:, i, :], g.slot_no[:, 0:CAP], posj[:, i, bass.ds(column, 1)], None,
                             ALU.is_equal)
                ins.then_inc(sem("sel_set"), 1)

            def select_gates(b, column):
                dve.wait_ge(sem("places_turned"), b + 1)
                for i in range(NT):
                    ins = ts(g.selg[:, i, :], g.slot_no[:, :], posj[:, i, bass.ds(column, 1)],
                             gate[:, i, bass.ds(column, 1)], ALU.is_equal, ALU.mult)
                ins.then_inc(sem("selg_set"), 1)

            def pick(e):
                copy(g.picked[0:2 * E, :], g.pick[0:2 * E, bass.ds(e, 1)].broadcast_to([2 * E, CAP])) \
                    .then_inc(sem("picked_set"), 1)

            def tokens_low(n):
                dve.wait_ge(sem("x_high_set"), n)
                tt(g.x_parts[:, :, CAP:2 * CAP], cut(bank(7), k=KD), g.x_parts[:, :, 0:CAP].bitcast(F32),
                   ALU.subtract).then_inc(sem("x_set"), 1)

            select(0)
            dve.wait_ge(sem("gateT_done"), 1)
            copy(g.gateT, bank(4)[0:E, 0:SEQ]).then_inc(sem("gateT_set"), 1)
            c = rsc[0:R]
            dve.wait_ge(sem("counted"), 1)
            own.link(tt(c[:, 2:3], bank(5)[0:R, 0:1], c[:, 0:1], ALU.is_gt))
            stt(c[:, 3:4], c[:, 0:1], -0.5, c[:, 1:2], ALU.mult, ALU.add).then_inc(sem("flag_set"), 1)
            tokens_low(1)
            dve.wait_ge(sem("rank_done"), 1)
            own.link(copy(c[:, 4:5], bank(5)[0:R, 1:2]))
            ts(c[:, 8:24], g.slot_no[0:R, 0:16], c[:, 4:5], c[:, 2:3], ALU.is_equal, ALU.mult) \
                .then_inc(sem("ranked"), 1)
            dve.wait_ge(sem("b1_in"), 32)
            raw = g.b1raw[0:2 * E, :]
            own.link(ts(raw[:, 1::2], raw[:, 1::2], 1.0, None, ALU.add))
            own.link(copy(g.b1_parts[0:2 * E, :], raw))
            dve.wait_ge(sem("list_done"), 1)
            copy(g.order_i[0:1, 0:16], bank(5)[0:1, 16:32])
            copy(g.order_i[0:1, 20:36], bank(5)[0:1, 32:48])
            copy(g.order_i[0:1, 40:41], bank(5)[0:1, 48:49]).then_inc(sem("order_set"), 1)
            tt(g.b1_parts[E:2 * E, :], raw[E:2 * E, :], g.b1_parts[E:2 * E, :].bitcast(F32), ALU.subtract)
            for half in range(2):
                rows = slice(half * E, (half + 1) * E)
                ins = copy(g.pick[rows, :], ident[rows, rows])
            ins.then_inc(sem("b1_set"), 1)
            dve.wait_ge(sem("b1_set"), 1)
            pick(0)
            low(0, 2)
            low(0, 3)

            start = own.n

            def block_of(b, column, following):
                own.base, own.n = b * OWN + start, 0

                def clip(q):
                    dve.wait_ge(sem("h_turned"), b * 4 + (q + 1))
                    h = bank(7 - q % 2).rearrange("p (t two n) -> p t two n", t=2, two=2)
                    ts(g.hg, h[:, :, 0, 0:CAP], 7.0, None, ALU.min)
                    ts(g.hl, h[:, :, 1, 0:CAP], 8.0, -6.0, ALU.min, ALU.max).then_inc(sem("glu_set"), 1)

                def activate(q):
                    dve.wait_ge(sem("sigmoid_set"), b * 4 + (q + 1))
                    own.link(stt(g.ha, g.hs, 1.0 / SWIGLU_ALPHA, g.hl, ALU.mult, ALU.mult))
                    c = slice(2 * q, 2 * q + 2)
                    own.link(copy(g.a_parts[:, c, 0:CAP], g.ha))
                    tt(g.a_parts[:, c, CAP:2 * CAP], g.ha, g.a_parts[:, c, 0:CAP].bitcast(F32), ALU.subtract) \
                        .then_inc(sem("act_set"), 1)

                clip(0)
                low(b, 4)
                activate(0)
                low(b, 5)
                clip(1)
                low(b, 6)
                activate(1)
                select_gates(b, column)
                dve.wait_ge(sem("gathered"), b + 1)
                select(following)
                low(b, 7)
                clip(2)
                low(b, 8)
                activate(2)
                clip(3)
                low(b, 9)
                activate(3)
                low(b, 10)
                tokens_low(b + 2)
                low(b, 11)
                assert own.n == OWN, own.n

            def first_lows(b, e):
                pick(e)
                for c in range(DEPTH):
                    low(b, c)

            with dve.Fori(0, E - 1) as b:
                block_of(b, b, b + 1)
                first_lows(b + 1, b + 1)
            count = further_blocks(dve)
            block_of(E - 1, E - 1, further_column(dve, 0))
            with dve.If(count > 0):
                with dve.Fori(0, count) as r:
                    expert = further_expert(dve, r)
                    first_lows(r + E, expert)
                    block_of(r + E, further_column(dve, r), further_column(dve, r + 1))
            for i in range(NT):
                dve.wait_ge(sem("all_added"), 1)
                tt(x[:, i], x[:, i], bank(2 * i, 2), ALU.add).then_inc(sem("out_set"), 1)

        @block.scalar
        def _(act):
            own = Own(act, sem("act_moe_steps"))
            if not whole:
                act.wait_ge(sem("x_in2"), 16)
                act.wait_ge(sem("moe_consts"), 1)
            sq = g.xnT.rearrange("p k n -> p (k n)")[:, 0:D]
            for i in range(NT):
                own.link(nc.scalar.activation(sq, x[:, i], ACT.Square, accum_out=g.stat[:, i:i + 1]))
            nc.scalar.activation(g.stat[:, 4:6], g.stat[:, 0:2], ACT.Sqrt, bias=g.eps_norm, scale=1.0 / D) \
                .then_inc(sem("root2_set"), 1)
            for q in range(4):
                act.wait_ge(sem("xn_turned"), q + 1)
                nc.scalar.activation(g.xnT[:, 2 * q:2 * q + 2], cut(bank(4 + q % 2), k=2), ACT.Copy) \
                    .then_inc(sem("xnT_set"), 1)

            def high(b, c, free=True):
                act.wait_ge(g.arrived[c % LO], b * 32 + 16 * (filled[c] + c // LO + 1))
                if free:
                    act.wait_ge(sem("w_used"), b * CHUNKS + (FREED - DEPTH + c + 1))
                nc.scalar.activation(g.w_high[:, c % DEPTH, :], slots[c], ACT.Copy).then_inc(sem("high_set"), 1)

            high(0, 0, False)
            high(0, 1, False)
            act.wait_ge(sem("top_set"), 1)
            for i in range(NT):
                ins = nc.scalar.activation(top8[:, i, 0:TOPK], top8[:, i, 0:TOPK], ACT.Exp,
                                           bias=g.stat[:, 20 + i:21 + i], accum_out=g.stat[:, 22 + i:23 + i])
            ins.then_inc(sem("top_exp"), 1)
            high(0, 2, False)
            high(0, 3, False)

            def tokens_out(n):
                act.wait_ge(sem("gathered"), n)
                nc.scalar.activation(g.x_parts[:, :, 0:CAP], cut(bank(7), k=KD), ACT.Copy) \
                    .then_inc(sem("x_high_set"), 1)

            def y_out(b, h):
                act.wait_ge(sem("w_used"), b * CHUNKS + (FREED + 2 * h + 2 - 4))
                nc.scalar.activation(g.ye[:, 512 * h:512 * h + 512], bank(4 + h), ACT.Copy) \
                    .then_inc(sem("y_set"), 1)

            def block_of(b):
                def h_out(q):
                    act.wait_ge(sem("w_used"), b * CHUNKS + (FREED + 2 * q + 2))
                    nc.scalar.activation(g.hsb[:, q % 2], bank(4 + q % 2), ACT.Copy).then_inc(sem("h_set"), 1)

                def sigmoid(q):
                    act.wait_ge(sem("glu_set"), b * 4 + (q + 1))
                    nc.scalar.activation(g.hs, g.hg, ACT.Silu, scale=SWIGLU_ALPHA).then_inc(sem("sigmoid_set"), 1)

                h_out(0)
                high(b, 4)
                high(b, 5)
                sigmoid(0)
                h_out(1)
                high(b, 6)
                sigmoid(1)
                high(b, 7)
                h_out(2)
                high(b, 8)
                sigmoid(2)
                high(b, 9)
                h_out(3)
                high(b, 10)
                sigmoid(3)
                tokens_out(b + 2)
                high(b, 11)
                act.wait_ge(sem("places_turned"), b + 2)
                nc.scalar.activation(g.selT[:, :], bank(6)[:, 0:SEQ], ACT.Copy).then_inc(sem("selT_set"), 1)

            def first_highs(b):
                high(b, 0)
                y_out(b, 0)
                high(b, 1)
                high(b, 2)
                y_out(b, 1)
                high(b, 3)

            tokens_out(1)
            y_out(0, 0)
            y_out(0, 1)
            with act.Fori(0, E - 1) as b:
                block_of(b)
                first_highs(b + 1)
            block_of(E - 1)
            count = further_blocks(act)
            with act.If(count > 0):
                with act.Fori(0, count) as r:
                    first_highs(r + E)
                    block_of(r + E)
            y_out(count + E, 0)
            y_out(count + E, 1)

        @block.tensor
        def _(pe):
            mm, tr = nc.tensor.matmul, nc.tensor.transpose
            if not whole:
                pe.wait_ge(sem("moe_consts"), 1)
            for i in range(NT):
                pe.wait_ge(sem("xn_set"), i + 1)
            for q in range(4):
                if q >= 2:
                    pe.wait_ge(sem("xnT_set"), q - 1)
                for kk in range(2):
                    for i in range(NT):
                        ins = tr(bank(4 + q % 2)[:, kk * SEQ + i * P:kk * SEQ + (i + 1) * P],
                                 g.xn[:, i, (2 * q + kk) * P:(2 * q + kk + 1) * P], ident)
                ins.then_inc(sem("xn_turned"), 1)
            pe.wait_ge(sem("router_in"), 32)
            pe.wait_ge(sem("xnT_set"), 4)
            for i in range(NT):
                o = bank(6)[:, i * E:(i + 1) * E]
                mm(o, g.ones[0:1, 0:P], brow, start=True, stop=False)
                for k in range(KD):
                    ins = mm(o, g.xnT[:, k, i * P:(i + 1) * P], cut(g.wr, k=KD)[:, k], start=False, stop=(k == KD - 1))
            ins.then_inc(sem("logits_done"), 1)
            pe.wait_ge(sem("chosen_set"), 1)
            first, second = g.chosen[:, 0, :], g.chosen[:, 1, :]
            mm(bank(6)[:, 64:64 + E], g.before, first[:, 0:E], start=True, stop=True)
            mm(bank(6)[:, 64 + E:64 + 2 * E], g.ones, first[:, 0:E], start=True, stop=False)
            mm(bank(6)[:, 64 + E:64 + 2 * E], g.before, second[:, 0:E], start=False, stop=True) \
                .then_inc(sem("pos_done"), 1)
            mm(bank(5)[0:R, 0:1], first, g.ones[:, 0:1], start=True, stop=False)
            mm(bank(5)[0:R, 0:1], second, g.ones[:, 0:1], start=False, stop=True).then_inc(sem("counted"), 1)
            for i in range(NT):
                ins = tr(bank(4)[0:E, i * P:(i + 1) * P], gate[:, i, 0:E], ident)
            ins.then_inc(sem("gateT_done"), 1)

            def gather():
                for k in range(KD):
                    for n, src in enumerate(g.xn_parts):
                        for i in range(NT):
                            ins = mm(bank(7)[:, k * CAP:(k + 1) * CAP], src[:, i, k * P:(k + 1) * P], g.sel[:, i, :],
                                     start=(n == 0 and i == 0), stop=(n == 2 and i == NT - 1))
                ins.then_inc(sem("gathered"), 1)

            def turn_places(b):
                pe.wait_ge(sem("selg_set"), b + 1)
                for i in range(NT):
                    ins = tr(bank(6)[:, i * P:(i + 1) * P], g.selg[:, i, :], ident)
                ins.then_inc(sem("places_turned"), 1)

            def scatter(b):
                pe.wait_ge(sem("selT_set"), b + 1)
                pe.wait_ge(sem("y_set"), b * 2 + 2)
                for h in range(2):
                    for i in range(NT):
                        mm(bank(2 * i + h), g.selT[:, i * P:(i + 1) * P], g.ye[:, 512 * h:512 * h + 512],
                           start=False, stop=True, skip_group_check=True)

            pe.wait_ge(sem("sel_set"), 1)
            gather()
            c = rsc[0:R]
            pe.wait_ge(sem("flag_set"), 1)
            mm(bank(5)[0:R, 1:2], g.before[0:R, 0:R], c[:, 2:3], start=True, stop=True).then_inc(sem("rank_done"), 1)
            pe.wait_ge(sem("gateT_set"), 1)
            pe.wait_ge(sem("b_in"), 16)
            for i in range(NT):
                for h in range(2):
                    mm(bank(2 * i + h), g.gateT[:, i * P:(i + 1) * P], g.b2raw[0:E, 512 * h:512 * h + 512],
                       start=True, stop=True, skip_group_check=True)
            pe.wait_ge(sem("ranked"), 1)
            mm(bank(5)[0:1, 16:32], c[:, 1:2], c[:, 8:24], start=True, stop=True)
            mm(bank(5)[0:1, 32:48], c[:, 3:4], c[:, 8:24], start=True, stop=True)
            mm(bank(5)[0:1, 48:49], c[:, 2:3], g.ones[0:R, 0:1], start=True, stop=True).then_inc(sem("list_done"), 1)
            pe.wait_ge(sem("order_set"), 1)
            tr(bank(4)[:, 0:P], ident, ident).then_inc(sem("places_turned"), 1)
            for q in range(FREED):
                tr(bank(4 + q // 3)[:, 0:P], ident, ident).then_inc(sem("w_used"), 1)
            pe.wait_ge(sem("b1_set"), 1)

            def block_of(b):
                def product(c, tokens, first):
                    o = bank(4 + (c - first) // 2 % 2)
                    pe.wait_ge(sem("low_set"), b * CHUNKS + (c + 1))
                    for k in range(EK):
                        for n, w in enumerate((g.w_high, g.w_low)):
                            ins = mm(o, tokens[:, c % 2 * EK + k, :], w[:, c % DEPTH, k * EW:(k + 1) * EW],
                                     start=(c % 2 == 0 and k == 0 and n == 0),
                                     stop=(c % 2 == 1 and k == EK - 1 and n == 1))
                    if c < W1C and c % 2 == 1:
                        ins = mm(o[0:CAP], g.picked[0:2 * E, :],
                                 g.b1_parts[0:2 * E, c // 2 * EW:(c // 2 + 1) * EW], start=False, stop=True,
                                 skip_group_check=True)
                    ins.then_inc(sem("w_used"), 1)

                def turn(q):
                    pe.wait_ge(sem("h_set"), b * 4 + (q + 1))
                    if q == 1:
                        pe.wait_ge(sem("selT_set"), b + 1)
                    elif q >= 2:
                        pe.wait_ge(sem("glu_set"), b * 4 + (q - 1))
                    for t in range(2):
                        for two in range(2):
                            at = (2 * t + two) * P
                            ins = mm(bank(7 - q % 2)[:, at:at + P], g.hsb[:, q % 2, t * CW + two:(t + 1) * CW:2],
                                     g.fold[:, :], start=True, stop=True)
                    ins.then_inc(sem("h_turned"), 1)

                pe.wait_ge(sem("x_set"), b + 1)
                pe.wait_ge(sem("picked_set"), b + 1)
                for q in range(4):
                    if q < 2:
                        pe.wait_ge(sem("y_set"), b * 2 + (q + 1))
                    else:
                        pe.wait_ge(sem("h_set"), b * 4 + (q - 1))
                    for t in range(2):
                        product(2 * q + t, g.x_parts, 0)
                        if q and not t:
                            turn(q - 1)
                turn(3)
                pe.wait_ge(sem("sel_set"), b + 2)
                pe.wait_ge(sem("glu_set"), b * 4 + 3)
                gather()
                scatter(b)
                pe.wait_ge(sem("glu_set"), b * 4 + 4)
                turn_places(b)
                for c in range(W1C, CHUNKS):
                    if c < W1C + 2:
                        pe.wait_ge(sem("act_set"), b * 4 + 2 * (c - W1C + 1))
                    product(c, g.a_parts, W1C)

            with pe.Fori(0, E) as b:
                block_of(b)
            count = further_blocks(pe)
            with pe.If(count > 0):
                with pe.Fori(0, count) as r:
                    block_of(r + E)
            scatter(count + E)
            tr(bank(4)[:, 0:P], ident, ident).then_inc(sem("all_added"), 1)


NAMES = ["x", "mem", "ln1", "w_in", "token_mu", "rwkv_w0", "rwkv_w2", "rwkv_a0", "rwkv_a2", "rwkv_g2", "rwkv_k_k",
         "rwkv_k_a", "rwkv_r_k", "rwkv_ln_w", "rwkv_ln_b", "dil_q_norm", "dil_k_norm", "ln_mem", "w_mem_kv",
         "mem_q_norm", "mem_k_norm", "p_rwkv", "p_dil", "p_mem", "w_out", "ln2", "w_router", "b_router", "w1",
         "b1", "w2", "b2"]


def kernel(**inputs):
    import concourse.bacc as bacc
    from concourse.bass_utils import run_bass_kernel_spmd

    nc = bacc.Bacc("TRN2", target_bir_lowering=False, num_devices=1)
    arrays = {n: np.ascontiguousarray(inputs[n]) for n in NAMES}
    a = {n: nc.dram_tensor(n, v.shape, F32, kind="ExternalInput").ap() for n, v in arrays.items()}
    out = nc.dram_tensor("out", (1, SEQ, D), F32, kind="ExternalOutput").ap()
    build(nc, a, out)
    return run_bass_kernel_spmd(nc, [arrays], core_ids=[0]).results[0]["out"]
```
